# Optimizing a Trainium2 kernel written in Bass

```python
import math
import jax
import jax.numpy as jnp
from jax import lax
import numpy as np

D_MODEL = 1024
BATCH = 1
SEQ = 2048
DEPTH = 1

EPS = 1e-6
N_BRANCHES = 3
D_SSM = 3 * D_MODEL // 4
SSM_GROUP = 16
SSM_GROUPS = D_SSM // SSM_GROUP
SSM_STATE = 64
DT_MIN = 0.001
DT_MAX = 0.1
ATTN_HEAD_DIM = 64
ATTN_HEADS_PER_GROUP = 4
ATTN_CONFIGS = ((128, 1), (512, 4), (2048, 16))
N_ATTN_HEADS = ATTN_HEADS_PER_GROUP * len(ATTN_CONFIGS)
D_ATTN = N_ATTN_HEADS * ATTN_HEAD_DIM
ATTN_BLOCK = 128
NUM_BUCKETS = 32
REL_MAX_DISTANCE = 2048
NEG_INF = -1e30
MEM_LEN = 256
MEM_HEADS = 4
MEM_HEAD_DIM = D_MODEL // 8
D_MEM = MEM_HEADS * MEM_HEAD_DIM
D_IN = 2 * D_SSM + 4 * D_ATTN + 2 * D_MEM + N_BRANCHES * D_MODEL

kernel_name = "hybrid_s5_dilated_attn_memxattn_gated"

def rms_norm(x, g):
    x32 = x.astype(jnp.float32)
    y = x32 * lax.rsqrt(jnp.mean(x32 * x32, axis=-1, keepdims=True) + EPS)
    return (y * g.astype(jnp.float32)).astype(x.dtype)

def rel_bucket(dist):
    n = jnp.maximum(dist, 0)
    max_exact = NUM_BUCKETS // 2
    n_f = jnp.maximum(n, 1).astype(jnp.float32)
    large = max_exact + (jnp.log(n_f / max_exact) / math.log(REL_MAX_DISTANCE / max_exact)
                         * (NUM_BUCKETS - max_exact)).astype(jnp.int32)
    large = jnp.minimum(large, NUM_BUCKETS - 1)
    return jnp.where(n < max_exact, n, large)

def s5_ssm(u, lam_re, lam_im, log_dt, b_re, b_im, c_re, c_im, d):
    B, L, _ = u.shape
    f32 = jnp.float32
    u32 = u.astype(f32).reshape(B, L, SSM_GROUPS, SSM_GROUP)
    lre, lim = lam_re.astype(f32), lam_im.astype(f32)
    dt = jnp.exp(log_dt.astype(f32))[:, None]
    mag = jnp.exp(lre * dt)
    abar_re, abar_im = mag * jnp.cos(lim * dt), mag * jnp.sin(lim * dt)
    den = lre * lre + lim * lim
    nr, ni = abar_re - 1.0, abar_im
    f_re = (nr * lre + ni * lim) / den
    f_im = (ni * lre - nr * lim) / den
    br, bi = b_re.astype(f32), b_im.astype(f32)
    bbar_re = f_re[..., None] * br - f_im[..., None] * bi
    bbar_im = f_re[..., None] * bi + f_im[..., None] * br
    bu_re = jnp.einsum('blgh,gph->blgp', u32, bbar_re)
    bu_im = jnp.einsum('blgh,gph->blgp', u32, bbar_im)
    a_re = jnp.broadcast_to(abar_re, (L, SSM_GROUPS, SSM_STATE))
    a_im = jnp.broadcast_to(abar_im, (L, SSM_GROUPS, SSM_STATE))

    def combine(e1, e2):
        a1r, a1i, b1r, b1i = e1
        a2r, a2i, b2r, b2i = e2
        return (a1r * a2r - a1i * a2i,
                a1r * a2i + a1i * a2r,
                a2r * b1r - a2i * b1i + b2r,
                a2r * b1i + a2i * b1r + b2i)

    def scan_one(br_seq, bi_seq):
        _, _, xr, xi = lax.associative_scan(combine, (a_re, a_im, br_seq, bi_seq), axis=0)
        return xr, xi

    xr, xi = jax.vmap(scan_one)(bu_re, bu_im)
    y = (jnp.einsum('blgp,ghp->blgh', xr, c_re.astype(f32))
         - jnp.einsum('blgp,ghp->blgh', xi, c_im.astype(f32))
         + d.astype(f32).reshape(SSM_GROUPS, SSM_GROUP) * u32)
    return y.reshape(B, L, D_SSM).astype(u.dtype)

def dilated_window_attention(q, k, v, bias_tab, window, dilation):
    B, L, H, hd = q.shape
    r = dilation
    span = window // dilation
    unit = r * ATTN_BLOCK
    Lp = -(-L // unit) * unit
    M = Lp // r
    nb = M // ATTN_BLOCK
    pad = ((0, 0), (0, Lp - L), (0, 0), (0, 0))

    def to_blocks(a):
        a = jnp.pad(a, pad).reshape(B, M, r, H, hd).transpose(0, 2, 1, 3, 4)
        return a.reshape(B, r, nb, ATTN_BLOCK, H, hd)

    def with_prev(a):
        prev = jnp.pad(a[:, :, :-1], ((0, 0), (0, 0), (1, 0), (0, 0), (0, 0), (0, 0)))
        return jnp.concatenate([prev, a], axis=3)

    qb = to_blocks(q)
    kw = with_prev(to_blocks(k))
    vw = with_prev(to_blocks(v))
    s = jnp.einsum('brnqhd,brnkhd->brnhqk', qb, kw).astype(jnp.float32) * (hd ** -0.5)
    qi = jnp.arange(ATTN_BLOCK)[:, None]
    kj = jnp.arange(2 * ATTN_BLOCK)[None, :]
    delta = ATTN_BLOCK + qi - kj
    band = (delta >= 0) & (delta <= span)
    has_prev = (jnp.arange(nb) > 0)[:, None, None] | (kj >= ATTN_BLOCK)[None]
    valid = band[None] & has_prev
    bias = bias_tab[rel_bucket(jnp.maximum(delta, 0) * r)]
    s = s + bias.transpose(2, 0, 1).astype(jnp.float32)
    s = jnp.where(valid[:, None], s, NEG_INF)
    m = jnp.max(s, axis=-1, keepdims=True)
    p = jnp.exp(s - m)
    l = jnp.sum(p, axis=-1, keepdims=True)
    o = jnp.einsum('brnhqk,brnkhd->brnqhd', (p / l).astype(v.dtype), vw)
    lse = (m + jnp.log(l))[..., 0]
    o = o.reshape(B, r, M, H, hd).transpose(0, 2, 1, 3, 4).reshape(B, Lp, H, hd)[:, :L]
    lse = lse.transpose(0, 1, 2, 4, 3).reshape(B, r, M, H).transpose(0, 2, 1, 3).reshape(B, Lp, H)[:, :L]
    return o, lse

def setup_inputs(seed: int = 0) -> dict:
    key = jax.random.key(seed)
    ks = jax.random.split(key, 32)
    f32 = jnp.float32

    def nrm(k, shape, scale):
        return jax.random.normal(k, shape, f32) * scale

    G, P, Hg = SSM_GROUPS, SSM_STATE, SSM_GROUP
    return {
        "x": nrm(ks[0], (BATCH, SEQ, D_MODEL), 1.0),
        "mem": nrm(ks[1], (BATCH, MEM_LEN, D_MODEL), 1.0),
        "norm_g": 1.0 + nrm(ks[2], (DEPTH, D_MODEL), 0.1),
        "mem_norm_g": 1.0 + nrm(ks[3], (DEPTH, D_MODEL), 0.1),
        "w_in": nrm(ks[4], (DEPTH, D_MODEL, D_IN), D_MODEL ** -0.5),
        "b_gate": nrm(ks[5], (DEPTH, N_BRANCHES * D_MODEL), 0.1),
        "ssm_lambda_re": -0.5 + nrm(ks[6], (DEPTH, G, P), 0.01),
        "ssm_lambda_im": math.pi * jnp.arange(P, dtype=f32) + nrm(ks[7], (DEPTH, G, P), 0.01),
        "ssm_log_dt": jax.random.uniform(ks[8], (DEPTH, G), f32, math.log(DT_MIN), math.log(DT_MAX)),
        "ssm_b_re": nrm(ks[9], (DEPTH, G, P, Hg), (0.5 / Hg) ** 0.5),
        "ssm_b_im": nrm(ks[10], (DEPTH, G, P, Hg), (0.5 / Hg) ** 0.5),
        "ssm_c_re": nrm(ks[11], (DEPTH, G, Hg, P), (0.5 / P) ** 0.5),
        "ssm_c_im": nrm(ks[12], (DEPTH, G, Hg, P), (0.5 / P) ** 0.5),
        "ssm_d": nrm(ks[13], (DEPTH, D_SSM), 0.5),
        "w_glu": nrm(ks[14], (DEPTH, D_SSM, D_SSM), D_SSM ** -0.5),
        "b_glu": nrm(ks[15], (DEPTH, D_SSM), 0.1),
        "w_mem_kv": nrm(ks[16], (DEPTH, D_MODEL, 2 * D_MEM), D_MODEL ** -0.5),
        "w_br_ssm": nrm(ks[17], (DEPTH, D_SSM, D_MODEL), D_SSM ** -0.5),
        "w_br_attn": nrm(ks[18], (DEPTH, D_ATTN, D_MODEL), D_ATTN ** -0.5),
        "w_br_mem": nrm(ks[19], (DEPTH, D_MEM, D_MODEL), D_MEM ** -0.5),
        "w_out": nrm(ks[20], (DEPTH, D_MODEL, D_MODEL), D_MODEL ** -0.5),
        "rel_bias": nrm(ks[21], (NUM_BUCKETS, N_ATTN_HEADS), 0.5),
        "final_norm_g": 1.0 + nrm(ks[22], (D_MODEL,), 0.1),
    }

def reference(x, mem, norm_g, mem_norm_g, w_in, b_gate, ssm_lambda_re, ssm_lambda_im, ssm_log_dt,
              ssm_b_re, ssm_b_im, ssm_c_re, ssm_c_im, ssm_d, w_glu, b_glu, w_mem_kv, w_br_ssm,
              w_br_attn, w_br_mem, w_out, rel_bias, final_norm_g):
    B, L, _ = x.shape
    sizes = (D_SSM, D_SSM, D_ATTN, D_ATTN, D_ATTN, D_ATTN, D_MEM, D_MEM, N_BRANCHES * D_MODEL)
    split_at = np.cumsum(sizes)[:-1].tolist()
    for layer in range(DEPTH):
        h = rms_norm(x, norm_g[layer])
        proj = h @ w_in[layer]
        u_ssm, z_ssm, q, k, v, z_attn, q_mem, z_mem, gate_logits = jnp.split(proj, split_at, axis=-1)

        y = s5_ssm(u_ssm, ssm_lambda_re[layer], ssm_lambda_im[layer], ssm_log_dt[layer],
                   ssm_b_re[layer], ssm_b_im[layer], ssm_c_re[layer], ssm_c_im[layer], ssm_d[layer])
        y = jax.nn.gelu(y)
        y = y * jax.nn.sigmoid(y @ w_glu[layer] + b_glu[layer])
        o_ssm = y * jax.nn.silu(z_ssm)

        qh = q.reshape(B, L, N_ATTN_HEADS, ATTN_HEAD_DIM)
        kh = k.reshape(B, L, N_ATTN_HEADS, ATTN_HEAD_DIM)
        vh = v.reshape(B, L, N_ATTN_HEADS, ATTN_HEAD_DIM)
        outs, lses = [], []
        for g, (window, dilation) in enumerate(ATTN_CONFIGS):
            sl = slice(g * ATTN_HEADS_PER_GROUP, (g + 1) * ATTN_HEADS_PER_GROUP)
            o_g, lse_g = dilated_window_attention(qh[:, :, sl], kh[:, :, sl], vh[:, :, sl],
                                                  rel_bias[:, sl], window, dilation)
            outs.append(o_g)
            lses.append(lse_g)
        alpha = jax.nn.softmax(jnp.stack(lses, axis=0), axis=0)
        o_attn = jnp.concatenate([o_g * alpha[g][..., None].astype(o_g.dtype) for g, o_g in enumerate(outs)],
                                 axis=2).reshape(B, L, D_ATTN)
        o_attn = o_attn * jax.nn.silu(z_attn)

        kv_mem = rms_norm(mem, mem_norm_g[layer]) @ w_mem_kv[layer]
        k_mem, v_mem = jnp.split(kv_mem, 2, axis=-1)
        k_mem = k_mem.reshape(B, MEM_LEN, MEM_HEADS, MEM_HEAD_DIM)
        v_mem = v_mem.reshape(B, MEM_LEN, MEM_HEADS, MEM_HEAD_DIM)
        qm = q_mem.reshape(B, L, MEM_HEADS, MEM_HEAD_DIM)
        s_mem = jnp.einsum('blhd,bmhd->bhlm', qm, k_mem).astype(jnp.float32) * (MEM_HEAD_DIM ** -0.5)
        p_mem = jax.nn.softmax(s_mem, axis=-1).astype(v_mem.dtype)
        o_mem = jnp.einsum('bhlm,bmhd->blhd', p_mem, v_mem).reshape(B, L, D_MEM)
        o_mem = o_mem * jax.nn.silu(z_mem)

        gates = jax.nn.sigmoid((gate_logits + b_gate[layer]).astype(jnp.float32))
        gates = gates.reshape(B, L, N_BRANCHES, D_MODEL).astype(x.dtype)
        merged = (gates[:, :, 0] * (o_ssm @ w_br_ssm[layer])
                  + gates[:, :, 1] * (o_attn @ w_br_attn[layer])
                  + gates[:, :, 2] * (o_mem @ w_br_mem[layer]))
        x = x + merged @ w_out[layer]
    return rms_norm(x, final_norm_g)


_drawn_inputs = setup_inputs


def setup_inputs(seed=0):
    import zlib

    import numpy as np

    out = dict(_drawn_inputs(seed))
    spreads = {}
    factors = {'norm_g': 5.285,
     'mem_norm_g': 8.0,
     'b_gate': 8.0,
     'ssm_lambda_re': 64.0,
     'ssm_lambda_im': 64.0,
     'ssm_log_dt': 64.0,
     'ssm_b_re': 64.0,
     'ssm_b_im': 64.0,
     'ssm_c_re': 64.0,
     'ssm_c_im': 64.0,
     'w_glu': 6.651,
     'b_glu': 35.72,
     'rel_bias': 5.809}
    for name, (base, spread) in spreads.items():
        noise = np.random.default_rng([zlib.crc32(name.encode()), seed]).standard_normal(out[name].shape)
        drawn = base * np.exp(spread * noise) if base else spread * noise
        out[name] = jnp.asarray(drawn.astype(out[name].dtype))
    for name, factor in factors.items():
        out[name] = (out[name] * factor).astype(out[name].dtype)
    return out
```

```python
import math
from contextlib import ExitStack

import numpy as np
import concourse.bass as bass
from concourse import mybir

F32 = mybir.dt.float32
F32R = mybir.dt.float32r
ACT = mybir.ActivationFunctionType
ALU = mybir.AluOpType
AX = mybir.AxisListType

P = 128
D = 1024
L = 2048
KD = D // P
CW = 512
NQ = L // CW
EPS = 1e-6
D_SSM, HG, NS = 768, 16, 64
G = D_SSM // HG
GB = P // HG
NB = G // GB
UG = 4
NU = G // UG
CH = P // HG
NC = L // CH
HD, HPG = 64, 4
DIL = (1, 4, 16)
NH = HPG * len(DIL)
NBLK = L // P
KS = D_SSM // P
MH, MD, ML = 4, 128, 256
NBUCKET, MAXD = 32, 2048
BIG = 1e30
T_U, T_ZS, T_Q, T_K, T_V, T_ZA, T_QM, T_ZM, T_G = 0, 6, 12, 18, 24, 30, 36, 40, 44
NT = 68
TWO_PI_HI = 6.28125
TWO_PI_LO = 2 * math.pi - TWO_PI_HI
MAGIC = 1.5 * 2 ** 23
PI_SAFE = 3.1415925


def build_program(nc, x_t, mem_t, norm_g, mem_norm_g, final_g, w_in, w_kv, b_gate, ssm_par, ssm_d, w_glu, b_glu,
                  w_br, w_out, rel_bias, buckets, ident_c, anti_c, sign_c, steps_c, powers_c, y_out):
    ctx = ExitStack()
    with ctx:
        def sb(stack, name, shape, dt=F32):
            return stack.enter_context(nc.sbuf_tensor(name, shape, dt))

        def sem(name):
            return ctx.enter_context(nc.semaphore(name))

        def dram(name, shape):
            return nc.dram_tensor(name, shape, F32).ap()

        proj_d = dram("proj_d", [NT, P, L])
        v_d = dram("v_d", [3, P, 2 * L])
        ys_d = dram("ys_d", [KS, P, L])
        o_d = dram("o_d", [16, P, L])
        mats_d = dram("mats_d", [NU, P, UG, 5, P])
        cs_d = dram("cs_d", [NU, P, UG, 2, NC])
        m8_d = dram("m8_d", [NU, P, UG])
        bias_d = dram("bias_d", [3, NH, 384])
        st_d = dram("st_d", [2, NH * NBLK, P])
        f_d = dram("f_d", [3, HPG, NBLK, P])

        psum = [ctx.enter_context(nc.psum_tensor(f"bank{i}", [P, 512], F32)) for i in range(8)]

        w_raw = sb(ctx, "w_raw", [P, 2, KD, P])
        w_hi = sb(ctx, "w_hi", [P, 2, KD, P], F32R)
        w_lo = sb(ctx, "w_lo", [P, 2, KD, P], F32R)
        k_mem = sb(ctx, "k_mem", [P, MH, ML])
        v_mem = sb(ctx, "v_mem", [P, 2, MH * MD])
        ones = sb(ctx, "ones", [P, P])
        g_in = sb(ctx, "g_in", [P, 3, KD])
        bg = sb(ctx, "bg", [P, 24])
        bglu = sb(ctx, "bglu", [P, KS])
        eps = sb(ctx, "eps", [P, 1])
        ident = sb(ctx, "ident", [P, P])
        sign = sb(ctx, "sign", [P, 1])

        w_loaded = [sem(f"w_loaded{s}") for s in range(2)]
        w_split = [sem(f"w_split{s}") for s in range(2)]
        w_hi_done = sem("w_hi_done")
        consts = sem("consts")
        const_loaded = sem("const_loaded")
        block_ends = sem("block_ends")

        def load_pair(sp, n, src0, src1, kt=KD):
            for s, src in enumerate((src0, src1)):
                if not (isinstance(n, int) and n == 0):
                    sp.wait_ge(w_split[s], n)
                sp.dma_start(w_raw[:, s, 0:kt, :], src).then_inc(w_loaded[s], 16)

        def split_pair(dve, n, used, kt=KD, slots=(0, 1)):
            for s in slots:
                dve.wait_ge(w_loaded[s], 16 * (n + 1))
                if used is not None:
                    dve.wait_ge(*used(s))
                nc.vector.tensor_copy(w_hi[:, s, 0:kt, :], w_raw[:, s, 0:kt, :]).then_inc(w_hi_done, 1)
                dve.wait_ge(w_hi_done, 2 * n + s + 1)
                nc.vector.tensor_tensor(w_lo[:, s, 0:kt, :], w_raw[:, s, 0:kt, :],
                                        w_hi[:, s, 0:kt, :].bitcast(F32), ALU.subtract).then_inc(w_split[s], 1)

        def three_pass(out, pairs):
            last = None
            for n, ((ah, al), (bh, bl)) in enumerate(pairs):
                nc.tensor.matmul(out, ah, bh, start=(n == 0), stop=False)
                nc.tensor.matmul(out, ah, bl, start=False, stop=False)
                last = nc.tensor.matmul(out, al, bh, start=False, stop=(n == len(pairs) - 1))
            return last

        def wt(s, k, cols=slice(0, P)):
            return w_hi[:, s, k, cols], w_lo[:, s, k, cols]

        NKV = 4
        x_loaded = [sem(f"x_loaded{i}") for i in range(2)]
        sq_ready, sq_used, root_done, rstd_done = (sem(s) for s in (
            "sq_ready", "sq_used", "root_done", "rstd_done"))
        scaled, hi_done, h_ready = sem("scaled"), sem("hi_done"), sem("h_ready")
        kv_mm, kv_out = sem("kv_mm"), sem("kv_out")
        mm_done, bank_free = sem("mm_done"), sem("bank_free")
        stored = [sem(f"stored{s}") for s in range(2)]

        segments, m = [], 0
        for kind, n, tiles, r in (
            [("copy", 3, lambda i, s: T_U + 2 * i + s, CH), ("silu", 3, lambda i, s: T_ZS + 2 * i + s, 1)]
            + [("copy", 1, (lambda i, s, t=t + 2 * g: t + s), DIL[g]) for g in range(3) for t in (T_Q, T_K)]
            + [("value", 1, (lambda i, s, t=T_V + 2 * g: t + s), DIL[g]) for g in range(3)]
            + [("silu", 3, lambda i, s: T_ZA + 2 * i + s, 1), ("copy", 2, lambda i, s: T_QM + 2 * i + s, 1),
               ("silu", 2, lambda i, s: T_ZM + 2 * i + s, 1), ("gate", 12, lambda i, s: T_G + 2 * i + s, 1)]
        ):
            segments.append((kind, m, n, tiles, r))
            m += n
        N_MAIN = m
        kind_of = [kind for kind, _, n, _, _ in segments for _ in range(n)]

        with ExitStack() as ph:
            h_hi = sb(ph, "h_hi", [P, KD, L], F32R)
            h_lo = sb(ph, "h_lo", [P, KD, L], F32R)
            xa = sb(ph, "xa", [P, KD, CW])
            ev = sb(ph, "ev", [P, 2, L])
            sq = sb(ph, "sq", [P, 4, CW])
            rstd = sb(ph, "rstd", [P, 2, CW])
            xb = ev[:, :, :].rearrange("p s (k c) -> p (s k) c", c=CW)
            xbuf = (xa, xb)
            jobs = [(ML, mem_t, slice(0, ML), L - CW, 1)] + [
                (CW, x_t, slice(CW * q, CW * (q + 1)), CW * q, 0) for q in range(NQ)]

            with nc.Block() as block:
                @block.sync
                def _(sp):
                    sp.dma_start(g_in[:, 0, :], norm_g).then_inc(const_loaded, 16)
                    sp.dma_start(g_in[:, 1, :], mem_norm_g).then_inc(const_loaded, 16)
                    sp.dma_start(g_in[:, 2, :], final_g).then_inc(const_loaded, 16)
                    sp.dma_start(bg[:, :], b_gate).then_inc(const_loaded, 16)
                    sp.dma_start(bglu[:, :], b_glu).then_inc(const_loaded, 16)
                    sp.dma_start(ident[:, :], ident_c).then_inc(const_loaded, 16)
                    sp.dma_start(sign[:, :], sign_c).then_inc(const_loaded, 16)
                    for j, (w, src, cols, _, _) in enumerate(jobs):
                        if j >= 2:
                            sp.wait_ge(h_ready, 2 * (j - 1))
                        sp.dma_start(xbuf[j % 2][:, :, 0:w], src[:, :, cols]).then_inc(x_loaded[j % 2], 16)
                        if j < NKV:
                            load_pair(sp, j, w_kv[2 * j], w_kv[2 * j + 1])
                    for kind, m0, n, tiles, r in segments:
                        for i in range(n):
                            load_pair(sp, NKV + m0 + i, w_in[tiles(i, 0)], w_in[tiles(i, 1)])

                @block.gpsimd
                def _(pool):
                    for kind, m0, n, tiles, r in segments:
                        for i in range(n):
                            for s in range(2):
                                m = m0 + i
                                pool.wait_ge(bank_free, 8 * m + 4 * s + 4)
                                if kind == "value":
                                    dst = v_d[m - segments[8][1], :, L * s:L * (s + 1)]
                                else:
                                    dst = proj_d[tiles(i, s)]
                                pool.dma_start(dst, ev[:, s, :]).then_inc(stored[s], 16)
                    for s in range(2):
                        pool.wait_ge(stored[s], 16 * N_MAIN)

                @block.scalar
                def _(act):
                    act.wait_ge(consts, 2)
                    for j, (w, _, _, at, _) in enumerate(jobs):
                        act.wait_ge(x_loaded[j % 2], 16 * (j // 2 + 1))
                        for k in range(KD):
                            if 8 * j + k >= 4:
                                act.wait_ge(sq_used, 8 * j + k - 3)
                            nc.scalar.activation(sq[:, k % 4, 0:w], xbuf[j % 2][:, k, 0:w],
                                                 ACT.Square).then_inc(sq_ready, 1)
                        act.wait_ge(sq_used, 8 * (j + 1))
                        if j >= 2:
                            act.wait_ge(scaled, 8 * (j - 1))
                        nc.scalar.activation(rstd[:, j % 2, 0:w], psum[2 + j % 2][:, 0:w], ACT.Sqrt,
                                             bias=eps[:, 0:1], scale=1.0 / D).then_inc(root_done, 1)
                        for half in range(2):
                            ks = slice(4 * half, 4 * half + 4)
                            act.wait_ge(scaled, 8 * j + 4 * half + 4)
                            if j == NQ:
                                act.wait_ge(kv_mm, 2 * NKV)
                            nc.scalar.activation(h_hi[:, ks, at:at + w], xbuf[j % 2][:, ks, 0:w],
                                                 ACT.Copy).then_inc(hi_done, 1)
                    for n in range(NKV):
                        for s in range(2):
                            act.wait_ge(kv_mm, 2 * n + s + 1)
                            src = psum[4 + n][:, ML * s:ML * (s + 1)]
                            dst = k_mem[:, 2 * n + s, :] if n < 2 else v_mem[:, s, 256 * (n - 2):256 * (n - 1)]
                            nc.scalar.activation(dst, src, ACT.Copy).then_inc(kv_out, 1)
                    for kind, m0, n, tiles, r in segments:
                        for i in range(n):
                            m = m0 + i
                            for s in range(2):
                                if m == 0:
                                    act.wait_ge(h_ready, 2 * len(jobs))
                                else:
                                    act.wait_ge(stored[s], 16 * m)
                                for c in range(NQ):
                                    act.wait_ge(mm_done, 8 * m + 4 * s + c + 1)
                                    src = psum[4 * s + c][:, :]
                                    dst = ev[:, s, CW * c:CW * (c + 1)]
                                    if r > 1 and kind != "value":
                                        src = src.rearrange("p (m r) -> p r m", r=r)
                                        dst = ev[:, s, :].rearrange("p (r m) -> p r m", r=r)[
                                            :, :, CW // r * c:CW // r * (c + 1)]
                                    if kind == "silu":
                                        ins = nc.scalar.activation(dst, src, ACT.Silu)
                                    elif kind == "gate":
                                        t = tiles(i, s) - T_G
                                        ins = nc.scalar.activation(dst, src, ACT.Sigmoid, bias=bg[:, t:t + 1])
                                    else:
                                        ins = nc.scalar.activation(dst, src, ACT.Copy)
                                    ins.then_inc(bank_free, 1)

                @block.vector
                def _(dve):
                    nc.vector.memset(ones[:, :], 1.0).then_inc(consts, 1)
                    nc.vector.memset(eps[:, :], EPS).then_inc(consts, 1)
                    dve.wait_ge(const_loaded, 112)
                    for j, (w, _, _, at, gi) in enumerate(jobs):
                        dve.wait_ge(root_done, j + 1)
                        r = rstd[:, j % 2, 0:w]
                        nc.vector.reciprocal(r, r).then_inc(rstd_done, 1)
                        dve.wait_ge(rstd_done, j + 1)
                        x = xbuf[j % 2]
                        for k in range(KD):
                            nc.vector.scalar_tensor_tensor(x[:, k, 0:w], x[:, k, 0:w], g_in[:, gi, k:k + 1], r,
                                                           ALU.mult, ALU.mult).then_inc(scaled, 1)
                        for half in range(2):
                            ks = slice(4 * half, 4 * half + 4)
                            dve.wait_ge(hi_done, 2 * j + half + 1)
                            nc.vector.tensor_tensor(h_lo[:, ks, at:at + w], x[:, ks, 0:w],
                                                    h_hi[:, ks, at:at + w].bitcast(F32),
                                                    ALU.subtract).then_inc(h_ready, 1)
                        if j < NKV:
                            split_pair(dve, j, None if j == 0 else
                                       lambda s: (kv_mm, 2 * j - 1 + s if j < 3 else 2 * j))
                    for kind, m0, n, tiles, r in segments:
                        for i in range(n):
                            m = m0 + i
                            after_value = kind == "value" and i > 0 or m0 > 0 and m == m0 and kind_of[m - 1] == "value"
                            split_pair(dve, NKV + m, lambda s: (
                                (kv_mm, 2 * NKV) if m == 0 else
                                (mm_done, 8 * m if after_value else 8 * (m - 1) + 4 * s + 4)))

                @block.tensor
                def _(pe):
                    pe.wait_ge(consts, 2)

                    def sum_squares(j):
                        w = jobs[j][0]
                        if j >= 2:
                            pe.wait_ge(root_done, j - 1)
                        for k in range(KD):
                            pe.wait_ge(sq_ready, 8 * j + k + 1)
                            mm = nc.tensor.matmul(psum[2 + j % 2][:, 0:w], ones[:, :], sq[:, k % 4, 0:w],
                                                  start=(k == 0), stop=(k == KD - 1)).then_inc(sq_used, 1)

                    def memory_kv(n):
                        for s in range(2):
                            pe.wait_ge(w_split[s], n + 1)
                        mcol = L - CW
                        for s in range(2):
                            if n < 2:
                                pairs = [(wt(s, k), (h_hi[:, k, mcol:mcol + ML], h_lo[:, k, mcol:mcol + ML]))
                                         for k in range(KD)]
                                out = psum[4 + n][:, ML * s:ML * (s + 1)]
                            else:
                                tok = slice(mcol + P * s, mcol + P * (s + 1))
                                pairs = [((h_hi[:, k, tok], h_lo[:, k, tok]), (w_hi[:, :, k, :], w_lo[:, :, k, :]))
                                         for k in range(KD)]
                                out = psum[4 + n][:, ML * s:ML * (s + 1)].rearrange("p (a b) -> p a b", a=2)
                            three_pass(out, pairs).then_inc(kv_mm, 1)

                    sum_squares(0)
                    sum_squares(1)
                    pe.wait_ge(h_ready, 2)
                    memory_kv(0)
                    sum_squares(2)
                    memory_kv(1)
                    sum_squares(3)
                    memory_kv(2)
                    memory_kv(3)
                    sum_squares(4)
                    for kind, m0, n, tiles, r in segments:
                        for i in range(n):
                            m = m0 + i
                            for s in range(2):
                                pe.wait_ge(w_split[s], NKV + m + 1)
                                if kind == "value":
                                    pe.wait_ge(w_split[1], NKV + m + 1)
                                for c in range(NQ):
                                    if m == 0:
                                        pe.wait_ge(h_ready, 2 * (c + 2))
                                        if s == 0 and c in (2, 3):
                                            pe.wait_ge(root_done, len(jobs))
                                        if s == 1:
                                            pe.wait_ge(kv_out, 2 * NKV)
                                    else:
                                        pe.wait_ge(bank_free, 8 * (m - 1) + 4 * s + c + 1)
                                    bank = psum[4 * s + c]
                                    if kind != "value":
                                        cols = slice(CW * c, CW * (c + 1))
                                        mm = three_pass(bank[:, :], [(wt(s, k), (h_hi[:, k, cols], h_lo[:, k, cols]))
                                                                     for k in range(KD)])
                                        mm.then_inc(mm_done, 1)
                                        continue
                                    for half in range(2):
                                        b = 2 * (4 * s + c) + half
                                        res, blk = divmod(b, NBLK // r)
                                        first = res + r * P * blk
                                        tok = slice(first, first + r * (P - 1) + 1, r)
                                        out = bank[:, 256 * half:256 * (half + 1)].rearrange(
                                            "p (a b) -> p a b", a=2)
                                        mm = three_pass(out, [((h_hi[:, k, tok], h_lo[:, k, tok]),
                                                               (w_hi[:, :, k, :], w_lo[:, :, k, :]))
                                                              for k in range(KD)])
                                    mm.then_inc(mm_done, 1)

        NP = 9 + CH
        par_loaded, tab_stored = sem("par_loaded"), sem("tab_stored")
        tab = sem("tab")
        dt_done, pow_ready, pow_done, ang_ready, cs_done = (sem(a) for a in (
            "dt_done", "pow_ready", "pow_done", "ang_ready", "cs_done"))
        ca_ready, ba_ready, k_mm, bt_mm, unit_done = (sem(a) for a in (
            "ca_ready", "ba_ready", "k_mm", "bt_mm", "unit_done"))
        TAB_STORES = 6 + CH

        with ExitStack() as ph:
            par = sb(ph, "par", [P, UG * (3 + 4 * HG)])
            dpar = sb(ph, "dpar", [HG, UG, HG])
            steps = sb(ph, "steps", [P, NC])
            powers = sb(ph, "powers", [P, NP])
            small = {n: sb(ph, f"sm_{n}", [P, UG]) for n in (
                "dt", "ldt", "th", "den", "t0", "t1", "nr", "fr", "sfi", "sph")}
            pw = {n: sb(ph, f"pw_{n}", [P, UG, NP]) for n in ("x", "t", "mag", "sin", "cos", "ar", "ai", "sar", "sai", "nai")}
            bb = sb(ph, "bb", [P, UG, HG])
            bbs = sb(ph, "bbs", [P, UG, HG])
            ca = sb(ph, "ca", [P, UG, CH + 1, HG])
            cas = sb(ph, "cas", [P, UG, CH + 1, HG])
            tmp = sb(ph, "tmp", [P, UG, CH + 1, HG])
            ba = sb(ph, "ba", [P, UG, CH, HG])
            bas = sb(ph, "bas", [P, UG, CH, HG])
            m3 = sb(ph, "m3", [P, 2, UG, P])
            kpad = sb(ph, "kpad", [HG, UG, (2 * CH - 1) * HG])
            tx = sb(ph, "tx", [P, 3, NC])
            m8 = sb(ph, "m8", [P, UG])
            cs = sb(ph, "cs", [P, UG, 2, NC])
            ldr, lim, ldt_in = (par[:, UG * i:UG * (i + 1)] for i in range(3))
            bc = [par[:, UG * 3 + UG * HG * i:UG * 3 + UG * HG * (i + 1)].rearrange("p (g h) -> p g h", g=UG)
                  for i in range(4)]

            with nc.Block() as block:
                @block.sync
                def _(sp):
                    sp.dma_start(steps[:, :], steps_c).then_inc(const_loaded, 16)
                    sp.dma_start(powers[:, :], powers_c).then_inc(const_loaded, 16)
                    for u in range(NU):
                        if u:
                            sp.wait_ge(tab_stored, 16 * TAB_STORES * u)
                        sp.dma_start(par[:, :], ssm_par[u]).then_inc(par_loaded, 16)
                        sp.dma_start(dpar[:, :, :], ssm_d[u]).then_inc(par_loaded, 16)
                        sp.wait_ge(unit_done, u + 1)
                        md = mats_d[u]
                        for half in range(2):
                            sp.dma_start(md[:, :, half, :], m3[:, half, :, :]).then_inc(tab_stored, 16)
                        for kind, c in ((2, ca), (3, cas)):
                            sp.dma_start(md[:, :, kind, :].rearrange("p g (j h) -> p g j h", j=CH),
                                         c[:, :, 1:, :]).then_inc(tab_stored, 16)
                        for t in range(CH):
                            at = HG * (CH - 1 - t)
                            sp.dma_start(md[HG * t:HG * (t + 1), :, 4, :],
                                         kpad[:, :, at:at + P]).then_inc(tab_stored, 16)
                        sp.dma_start(cs_d[u], cs[:, :, :, :]).then_inc(tab_stored, 16)
                        sp.dma_start(m8_d[u], m8[:, :]).then_inc(tab_stored, 16)
                    sp.wait_ge(tab_stored, 16 * TAB_STORES * NU)

                @block.scalar
                def _(act):
                    for u in range(NU):
                        act.wait_ge(par_loaded, 32 * (u + 1))
                        nc.scalar.activation(small["dt"][:, :], ldt_in, ACT.Exp).then_inc(dt_done, 1)
                        act.wait_ge(pow_ready, u + 1)
                        nc.scalar.activation(pw["mag"][:, :, :], pw["t"][:, :, :], ACT.Exp).then_inc(pow_done, 1)
                        nc.scalar.activation(pw["sin"][:, :, :], pw["x"][:, :, :], ACT.Sin).then_inc(pow_done, 1)
                        nc.scalar.activation(pw["cos"][:, :, :], pw["x"][:, :, :], ACT.Sin,
                                             scale=0.5).then_inc(pow_done, 1)
                        for g in range(UG):
                            act.wait_ge(ang_ready, UG * u + g + 1)
                            nc.scalar.activation(cs[:, g, 1, :], tx[:, g % 2, :], ACT.Sin).then_inc(cs_done, 1)
                            nc.scalar.activation(cs[:, g, 0, :], tx[:, g % 2, :], ACT.Sin,
                                                 scale=0.5).then_inc(cs_done, 1)

                @block.tensor
                def _(pe):
                    for u in range(NU):
                        pe.wait_ge(ca_ready, u + 1)
                        for g in range(UG):
                            mm = nc.tensor.matmul(psum[0][0:HG, P * g:P * (g + 1)], bb[:, g, :],
                                                  ca[:, g, 0:CH, :], start=True, stop=True)
                        mm.then_inc(k_mm, 1)
                        pe.wait_ge(ba_ready, u + 1)
                        for half, m in ((0, ba), (1, bas)):
                            for g in range(UG):
                                mm = nc.tensor.transpose(psum[1 + half][:, P * g:P * (g + 1)],
                                                         m[:, g, :, :].rearrange("p s h -> p (s h)"), ident[:, :])
                            mm.then_inc(bt_mm, 1)

                @block.vector
                def _(dve):
                    steps_done = [0]

                    def link(ins):
                        steps_done[0] += 1
                        ins.then_inc(tab, 1)
                        dve.wait_ge(tab, steps_done[0])

                    def tt(out, a, b, op):
                        link(nc.vector.tensor_tensor(out, a, b, op))

                    def ts(out, a, s1, s2, op0, op1=None):
                        if op1 is None:
                            link(nc.vector.tensor_scalar(out, a, s1, None, op0))
                        else:
                            link(nc.vector.tensor_scalar(out, a, s1, s2, op0, op1))

                    def reduce_angle(x, t):
                        ts(t, x, 1 / (2 * math.pi), MAGIC, ALU.mult, ALU.add)
                        ts(t, t, MAGIC, None, ALU.subtract)
                        link(nc.vector.scalar_tensor_tensor(x, t, -TWO_PI_HI, x, ALU.mult, ALU.add))
                        link(nc.vector.scalar_tensor_tensor(x, t, -TWO_PI_LO, x, ALU.mult, ALU.add))

                    def clip(x):
                        return nc.vector.tensor_scalar(x, x, PI_SAFE, -PI_SAFE, ALU.min, ALU.max)

                    def combine(out, tm, p1, a1, p2, a2, op):
                        tt(out, p1, a1, ALU.mult)
                        tt(tm, p2, a2, ALU.mult)
                        return nc.vector.tensor_tensor(out, out, tm, op)

                    link(nc.vector.memset(kpad[:, :, :], 0.0))
                    dve.wait_ge(const_loaded, 16 * 9)
                    s = {n: a[:, :] for n, a in small.items()}
                    w = {n: a[:, :, :] for n, a in pw.items()}
                    for u in range(NU):
                        dve.wait_ge(par_loaded, 32 * (u + 1))
                        dve.wait_ge(dt_done, u + 1)
                        tt(s["ldt"], ldr, s["dt"], ALU.mult)
                        tt(s["th"], lim, s["dt"], ALU.mult)
                        reduce_angle(s["th"], s["t0"])
                        shape = (P, UG, NP)
                        pj = powers[:, :].unsqueeze(1).to_broadcast(shape)
                        tt(w["x"], s["th"].unsqueeze(2).to_broadcast(shape), pj, ALU.mult)
                        reduce_angle(w["x"], w["t"])
                        link(clip(w["x"]))
                        nc.vector.tensor_tensor(w["t"], s["ldt"].unsqueeze(2).to_broadcast(shape), pj,
                                                ALU.mult).then_inc(pow_ready, 1)
                        dve.wait_ge(pow_done, 3 * (u + 1))
                        tt(w["cos"], w["cos"], w["cos"], ALU.mult)
                        ts(w["cos"], w["cos"], -2.0, 1.0, ALU.mult, ALU.add)
                        tt(w["ar"], w["mag"], w["cos"], ALU.mult)
                        tt(w["ai"], w["mag"], w["sin"], ALU.mult)
                        ts(w["sar"], w["ar"], sign[:, 0:1], None, ALU.mult)
                        ts(w["sai"], w["ai"], sign[:, 0:1], None, ALU.mult)
                        ts(w["nai"], w["ai"], -1.0, None, ALU.mult)
                        link(nc.vector.tensor_copy(m8[:, :], pw["mag"][:, :, CH]))
                        ar1, ai1 = pw["ar"][:, :, 1], pw["ai"][:, :, 1]
                        tt(s["den"], ldr, ldr, ALU.mult)
                        tt(s["t0"], lim, lim, ALU.mult)
                        tt(s["den"], s["den"], s["t0"], ALU.add)
                        link(nc.vector.reciprocal(s["den"], s["den"]))
                        ts(s["nr"], ar1, -1.0, None, ALU.add)
                        tt(s["t0"], s["nr"], ldr, ALU.mult)
                        tt(s["t1"], ai1, lim, ALU.mult)
                        tt(s["t0"], s["t0"], s["t1"], ALU.add)
                        tt(s["fr"], s["t0"], s["den"], ALU.mult)
                        tt(s["t0"], ai1, ldr, ALU.mult)
                        tt(s["t1"], s["nr"], lim, ALU.mult)
                        tt(s["t0"], s["t0"], s["t1"], ALU.subtract)
                        tt(s["t0"], s["t0"], s["den"], ALU.mult)
                        ts(s["sfi"], s["t0"], sign[:, 0:1], None, ALU.mult)
                        ts(s["sph"], pw["x"][:, :, CH], sign[:, 0:1], None, ALU.mult)
                        sh = (P, UG, HG)
                        fr, sfi = (s[a].unsqueeze(2).to_broadcast(sh) for a in ("fr", "sfi"))
                        t3 = tmp[:, :, 0, :]
                        link(combine(bb[:, :, :], t3, fr, bc[2], sfi, bc[3], ALU.subtract))
                        link(combine(bbs[:, :, :], t3, fr, bc[3], sfi, bc[2], ALU.add))
                        sh = (P, UG, CH + 1, HG)
                        cv = [a.unsqueeze(2).to_broadcast(sh) for a in bc[0:2]]
                        pf = {a: pw[a][:, :, 0:CH + 1].unsqueeze(3).to_broadcast(sh) for a in ("sar", "nai")}
                        link(combine(cas[:, :, :, :], tmp[:, :, :, :], pf["nai"], cv[0], pf["sar"], cv[1],
                                     ALU.subtract))
                        combine(ca[:, :, :, :], tmp[:, :, :, :], pf["sar"], cv[0], pf["nai"], cv[1],
                                ALU.add).then_inc(ca_ready, 1)
                        dve.wait_ge(ca_ready, u + 1)
                        sh = (P, UG, CH, HG)
                        bv = [a[:, :, :].unsqueeze(2).to_broadcast(sh) for a in (bb, bbs)]
                        pf = {a: pw[a][:, :, CH + 1:NP].unsqueeze(3).to_broadcast(sh) for a in ("ar", "sai")}
                        tm = tmp[:, :, 0:CH, :]
                        link(combine(ba[:, :, :, :], tm, pf["ar"], bv[0], pf["sai"], bv[1], ALU.subtract))
                        combine(bas[:, :, :, :], tm, pf["ar"], bv[1], pf["sai"], bv[0],
                                ALU.add).then_inc(ba_ready, 1)
                        for g in range(UG):
                            x = tx[:, g % 2, :]
                            if g >= 2:
                                dve.wait_ge(cs_done, 2 * (UG * u + g - 1))
                            ts(x, steps[:, :], small["sph"][:, g:g + 1], None, ALU.mult)
                            reduce_angle(x, tx[:, 2, :])
                            clip(x).then_inc(ang_ready, 1)
                        dve.wait_ge(k_mm, u + 1)
                        kp = kpad[:, :, (CH - 1) * HG:]
                        idb = ident[0:HG, 0:HG].unsqueeze(1).to_broadcast((HG, UG, HG))
                        tt(dpar[:, :, :], dpar[:, :, :], idb, ALU.mult)
                        link(nc.vector.tensor_copy(kp, psum[0][0:HG, :].rearrange("p (g c) -> p g c", g=UG)))
                        tt(kp[:, :, 0:HG], kp[:, :, 0:HG], dpar[:, :, :], ALU.add)
                        for half in range(2):
                            dve.wait_ge(bt_mm, 2 * u + half + 1)
                            link(nc.vector.tensor_copy(m3[:, half, :, :].rearrange("p g c -> p (g c)"),
                                                       psum[1 + half][:, :]))
                        dve.wait_ge(cs_done, 2 * UG * (u + 1))
                        tt(cs[:, :, 0, :], cs[:, :, 0, :], cs[:, :, 0, :], ALU.mult)
                        nc.vector.tensor_scalar(cs[:, :, 0, :], cs[:, :, 0, :], -2.0, 1.0, ALU.mult,
                                                ALU.add).then_inc(unit_done, 1)
                        dve.wait_ge(unit_done, u + 1)

        mats_loaded = [sem(f"mats_loaded{i}") for i in range(2)]
        v_mm, turned, w_sum, scanned, state_done, y_mm, y_out_done = (sem(a) for a in (
            "v_mm", "turned", "w_sum", "scanned", "state_done", "y_mm", "y_out_done"))
        ys_stored = [sem(f"ys_stored{i}") for i in range(2)]
        BLOADS = 2 * 3 + CH
        with ExitStack() as ph:
            mats = sb(ph, "mats", [P, 2, GB, 5, P])
            csb = sb(ph, "csb", [P, 2, GB, 2, NC])
            m8b = sb(ph, "m8b", [P, 2, GB])
            ub = sb(ph, "ub", [P, 2, GB, NC])
            yb = sb(ph, "yb", [P, 2, GB, NC])
            tv = sb(ph, "tv", [P, 3, 2, NC])
            wv = sb(ph, "wv", [P, 3, NC])
            zv = sb(ph, "zv", [P, 3, NC])
            xz = sb(ph, "xz", [P, 3, 2, NC])
            R = 3

            with nc.Block() as block:
                @block.sync
                def _(sp):
                    for b in range(NB):
                        i = b % 2
                        if b >= 2:
                            sp.wait_ge(y_mm, GB * (b - 1))
                        for part in range(2):
                            gs = slice(UG * part, UG * (part + 1))
                            sp.dma_start(mats[:, i, gs, :, :], mats_d[2 * b + part]).then_inc(mats_loaded[i], 16)
                            sp.dma_start(csb[:, i, gs, :, :], cs_d[2 * b + part]).then_inc(mats_loaded[i], 16)
                            sp.dma_start(m8b[:, i, gs], m8_d[2 * b + part]).then_inc(mats_loaded[i], 16)
                        src = proj_d[T_U + b].rearrange("(g h) (s c) -> s h g c", g=GB, s=CH)
                        for t in range(CH):
                            sp.dma_start(ub[HG * t:HG * (t + 1), i, :, :], src[t]).then_inc(mats_loaded[i], 16)

                @block.gpsimd
                def _(pool):
                    for q in range(G + 1):
                        if q < G:
                            pool.wait_ge(turned, q + 1)
                            if q >= R:
                                pool.wait_ge(scanned, q - R + 1)
                            nc.gpsimd.tensor_tensor(wv[:, q % R, :], tv[:, q % R, 0, :], tv[:, q % R, 1, :],
                                                    ALU.add).then_inc(w_sum, 1)
                        if q >= 1:
                            g = q - 1
                            pool.wait_ge(scanned, g + 1)
                            if g >= R:
                                pool.wait_ge(y_mm, g - R + 1)
                            z = zv[:, g % R, :].unsqueeze(1).to_broadcast((P, 2, NC))
                            nc.gpsimd.tensor_tensor(xz[:, g % R, :, :], csb[:, g // GB % 2, g % GB, :, :], z,
                                                    ALU.mult).then_inc(state_done, 1)

                @block.vector
                def _(dve):
                    for q in range(G + 1):
                        if q < G:
                            if q % GB == 0:
                                b = q // GB
                                dve.wait_ge(mats_loaded[b % 2], 16 * BLOADS * (b // 2 + 1))
                            dve.wait_ge(v_mm, q + 1)
                            if q >= R:
                                dve.wait_ge(w_sum, q - R + 1)
                            nc.vector.tensor_tensor(tv[:, q % R, :, :],
                                                    psum[q % R][:, :].rearrange("p (a c) -> p a c", a=2),
                                                    csb[:, q // GB % 2, q % GB, :, :], ALU.mult).then_inc(turned, 1)
                        if q >= 1:
                            g = q - 1
                            dve.wait_ge(w_sum, g + 1)
                            if g >= R:
                                dve.wait_ge(state_done, g - R + 1)
                            m = m8b[:, g // GB % 2, g % GB:g % GB + 1].to_broadcast((P, NC))
                            nc.vector.tensor_tensor_scan(zv[:, g % R, :], m, wv[:, g % R, :], 0.0,
                                                         ALU.mult, ALU.add).then_inc(scanned, 1)

                @block.tensor
                def _(pe):
                    LAG = 2
                    for q in range(G + LAG):
                        if q < G:
                            b, g = divmod(q, GB)
                            if g == 0:
                                pe.wait_ge(mats_loaded[b % 2], 16 * BLOADS * (b // 2 + 1))
                            if q >= R:
                                pe.wait_ge(turned, q - R + 1)
                            for half in range(2):
                                mm = nc.tensor.matmul(psum[q % R][:, NC * half:NC * (half + 1)],
                                                      mats[:, b % 2, g, half, :], ub[:, b % 2, g, :],
                                                      start=True, stop=True)
                            mm.then_inc(v_mm, 1)
                        if q >= LAG:
                            q2 = q - LAG
                            b, g = divmod(q2, GB)
                            if q2 >= R:
                                pe.wait_ge(y_out_done, q2 - R + 1)
                            y = psum[3 + q2 % R]
                            nc.tensor.matmul(y[:, 0:NC], mats[:, b % 2, g, 4, :], ub[:, b % 2, g, :],
                                             start=True, stop=False)
                            pe.wait_ge(state_done, q2 + 1)
                            for part in range(2):
                                mm = nc.tensor.matmul(y[:, 1:NC], mats[:, b % 2, g, 2 + part, :],
                                                      xz[:, q2 % R, part, 0:NC - 1], start=False, stop=(part == 1))
                            mm.then_inc(y_mm, 1)

                @block.scalar
                def _(act):
                    for b in range(NB):
                        for g in range(GB):
                            q = GB * b + g
                            act.wait_ge(y_mm, q + 1)
                            if g == 0 and b >= 2:
                                act.wait_ge(ys_stored[b % 2], 16 * CH * (b // 2))
                            nc.scalar.activation(yb[:, b % 2, g, :], psum[3 + q % R][:, 0:NC],
                                                 ACT.Gelu_apprx_tanh).then_inc(y_out_done, 1)
                        act.wait_ge(y_out_done, GB * (b + 1))
                        dst = ys_d[b].rearrange("(g h) (s c) -> s h g c", g=GB, s=CH)
                        for t in range(CH):
                            act.dma_start(dst[t], yb[HG * t:HG * (t + 1), b % 2, :, :]).then_inc(ys_stored[b % 2], 16)
                    for i in range(2):
                        act.wait_ge(ys_stored[i], 16 * CH * (NB // 2))

        SCALE = HD ** -0.5
        batches = []
        for h in range(NH):
            g = h // HPG
            per = 4 if g == 2 else 2
            for b in range(0, NBLK, per):
                batches.append((h, g, list(range(b, b + per)), 512 // per))
        NT_B = len(batches)
        qk_loaded = [sem(f"qk_loaded{i}") for i in range(2)]
        vg_loaded = [sem(f"vg_loaded{i}") for i in range(2)]
        bias_in, bias_rows, bias_neg, bias_kept, bias_loaded = (sem(a) for a in (
            "bias_in", "bias_rows", "bias_neg", "bias_kept", "bias_loaded"))
        s_mm, s_biased, s_min, e_done, t_mm, t_out, o_mm, o_out = (sem(a) for a in (
            "s_mm", "s_biased", "s_min", "e_done", "t_mm", "t_out", "o_mm", "o_out"))
        st_mm, st_out, st_kept = sem("st_mm"), sem("st_out"), sem("st_kept")
        first_mask, bias_turned, bias_kept2 = sem("first_mask"), sem("bias_turned"), sem("bias_kept2")

        with ExitStack() as ph:
            oT = sb(ph, "oT", [P, NH // 2, L])
            qk = sb(ph, "qk", [P, 2, 2, L])
            with ExitStack() as pa:
                vg = sb(pa, "vg", [P, 2, NBLK, HPG * HD])
                bias = sb(pa, "bias", [P, NH, 2, 256])
                bk = sb(pa, "bk", [NBUCKET + 1, 3, 384])
                rel = sb(pa, "rel", [NBUCKET + 1, NH])
                brow = sb(pa, "brow", [NH, 3, 384])
                tsc = sb(pa, "tsc", [P, 3, 512])
                esc = sb(pa, "esc", [P, 3, 512])
                ptr = sb(pa, "ptr", [P, 3, 512])
                stat = sb(pa, "stat", [P, 2, NH * NBLK])
                strow = sb(pa, "strow", [P, 4, P])
                anti = sb(pa, "anti", [P, P])

                mirrored = vg[:, 1, 0:NH, :]

                def has_prev(g, b):
                    return b % (NBLK // DIL[g]) != 0

                with nc.Block() as block:
                    @block.sync
                    def _(sp):
                        sp.dma_start(bk[:, :, :], buckets).then_inc(bias_in, 16)
                        sp.dma_start(rel[0:NBUCKET, :], rel_bias).then_inc(bias_in, 16)
                        sp.dma_start(anti[:, :], anti_c).then_inc(bias_in, 16)
                        for pair in range(2):
                            for a, t in enumerate((T_Q, T_K)):
                                sp.dma_start(qk[:, pair, a, :], proj_d[t + pair]).then_inc(qk_loaded[pair], 16)
                        sp.dma_start(vg[:, 0, :, :].rearrange("p b c -> p (b c)"), v_d[0]).then_inc(vg_loaded[0], 16)
                        sp.wait_ge(bias_neg, 3)
                        for g in range(3):
                            sp.dma_start(bias_d[g], brow[:, g, :]).then_inc(bias_kept, 16)
                        sp.wait_ge(bias_kept, 48)
                        for h in range(NH):
                            row = bias_d[h // HPG, h]
                            src = bass.AP(row.tensor, row.offset, [[1, P], [1, 256]])
                            sp.dma_start(mirrored[:, h, :], src).then_inc(bias_loaded, 16)
                        sp.wait_ge(bias_turned, NH // 2)
                        sp.dma_start(vg[:, 1, :, :].rearrange("p b c -> p (b c)"), v_d[1]).then_inc(vg_loaded[1], 16)
                        for pair in range(2, NH // 2):
                            n = sum(1 for b in batches if b[0] < 2 * (pair - 1))
                            sp.wait_ge(s_mm, n)
                            for a, t in enumerate((T_Q, T_K)):
                                sp.dma_start(qk[:, pair % 2, a, :], proj_d[t + pair]).then_inc(
                                    qk_loaded[pair % 2], 16)
                            if pair == 4:
                                sp.wait_ge(o_mm, HPG * NBLK // 2)
                                sp.dma_start(vg[:, 0, :, :].rearrange("p b c -> p (b c)"), v_d[2]).then_inc(
                                    vg_loaded[0], 16)
                        sp.wait_ge(st_out, 1)
                        for w in range(2):
                            sp.dma_start(st_d[w, 0:P, :], strow[:, 2 * w, :]).then_inc(st_kept, 16)
                            sp.dma_start(st_d[w, P:NH * NBLK, :], strow[0:NH * NBLK - P, 2 * w + 1, :]).then_inc(
                                st_kept, 16)
                        sp.wait_ge(st_kept, 64)

                    @block.gpsimd
                    def _(pool):
                        nc.gpsimd.memset(rel[NBUCKET:NBUCKET + 1, :], 1.0).then_inc(first_mask, 1)
                        pool.wait_ge(first_mask, 1)
                        nc.gpsimd.memset(bias[:, :, 0, 0:128], BIG).then_inc(first_mask, 1)

                    @block.tensor
                    def _(pe):
                        pe.wait_ge(bias_in, 48)
                        pe.wait_ge(first_mask, 1)
                        for g in range(3):
                            nc.tensor.matmul(psum[g][0:NH, 0:384], rel[:, :], bk[:, g, :], start=True,
                                             stop=True).then_inc(bias_rows, 1)

                        pe.wait_ge(bias_loaded, 16 * NH)
                        for n in range(NH // 2):
                            nc.tensor.matmul(psum[2 + n][:, :].rearrange("p (a k) -> p a k", a=2), anti[:, :],
                                             mirrored[:, 2 * n:2 * n + 2, :], start=True, stop=True).then_inc(
                                                 bias_turned, 1)

                        def scores(t):
                            h, g, blocks, nk = batches[t]
                            pair, half = divmod(h, 2)
                            rows = slice(64 * half, 64 * half + 64)
                            pe.wait_ge(qk_loaded[pair % 2], 32 * (pair // 2 + 1))
                            if t < 2:
                                pe.wait_ge(bias_neg, 3)
                            else:
                                pe.wait_ge(s_biased, t - 1)
                            q, k = qk[rows, pair % 2, 0, :], qk[rows, pair % 2, 1, :]
                            for i, b in enumerate(blocks):
                                lhs = q[:, P * b:P * (b + 1)]
                                out = psum[t % 2][:, nk * i:nk * (i + 1)]
                                if nk == 128 or has_prev(g, b):
                                    mm = nc.tensor.matmul(out, lhs, k[:, P * (b + 1) - nk:P * (b + 1)],
                                                          start=True, stop=True)
                                else:
                                    for part in range(2):
                                        mm = nc.tensor.matmul(out[:, P * part:P * (part + 1)], lhs,
                                                              k[:, P * b:P * (b + 1)], start=True, stop=True)
                            mm.then_inc(s_mm, 1)

                        def turn(t):
                            pe.wait_ge(e_done, sum(len(b[2]) for b in batches[:t + 1]))
                            if t >= 2:
                                pe.wait_ge(t_out, t - 1)
                            else:
                                pe.wait_ge(bias_kept2, NH // 2)
                            for i in range(4):
                                mm = nc.tensor.transpose(psum[2 + t % 2][:, P * i:P * (i + 1)],
                                                         esc[:, t % 3, P * i:P * (i + 1)], ident[:, :])
                            mm.then_inc(t_mm, 1)

                        def output(t):
                            h, g, blocks, nk = batches[t]
                            rows = slice(64 * (h % 2), 64 * (h % 2) + 64)
                            pe.wait_ge(vg_loaded[g % 2], 16 * (g // 2 + 1))
                            pe.wait_ge(t_out, t + 1)
                            bank = (h * NBLK + blocks[0]) // 4
                            if blocks[0] % 4 == 0 and bank >= 4:
                                pe.wait_ge(o_out, bank - 3)
                            for i, b in enumerate(blocks):
                                out = psum[4 + bank % 4][rows, P * (b % 4):P * (b % 4 + 1)]
                                parts = [1] if nk == 256 else [0]
                                if nk == 256 and has_prev(g, b):
                                    parts = [0, 1]
                                for part in parts:
                                    kb = b - 1 + part if nk == 256 else b
                                    e = ptr[:, t % 3, nk * i + P * part:nk * i + P * (part + 1)]
                                    mm = nc.tensor.matmul(out, vg[:, g % 2, kb, HD * (h % HPG):HD * (h % HPG + 1)], e,
                                                          start=(part == parts[0]), stop=(part == parts[-1]))
                            mm.then_inc(o_mm, 1)

                        for t in range(NT_B + 4):
                            if t < NT_B:
                                scores(t)
                            if 0 <= t - 2 < NT_B:
                                turn(t - 2)
                            if 0 <= t - 3 < NT_B:
                                output(t - 3)
                        pe.wait_ge(o_out, NH * NBLK // 4)
                        for w in range(2):
                            nc.tensor.transpose(psum[0][:, 2 * w * P:(2 * w + 1) * P], stat[:, w, 0:P], ident[:, :])
                            mm = nc.tensor.transpose(psum[0][0:NH * NBLK - P, (2 * w + 1) * P:(2 * w + 2) * P],
                                                     stat[:, w, P:NH * NBLK], ident[:, :])
                        mm.then_inc(st_mm, 1)

                    @block.vector
                    def _(dve):
                        for g in range(3):
                            dve.wait_ge(bias_rows, g + 1)
                            nc.vector.tensor_scalar(brow[:, g, :], psum[g][0:NH, 0:384], -1.0, None,
                                                    ALU.mult).then_inc(bias_neg, 1)

                        def negate_and_min(t):
                            h, g, blocks, nk = batches[t]
                            n = len(blocks)
                            dve.wait_ge(s_mm, t + 1)
                            if t >= 3:
                                dve.wait_ge(e_done, sum(len(b[2]) for b in batches[:t - 2]))
                            out = tsc[:, t % 3, :].rearrange("p (n k) -> p n k", n=n)
                            sc = psum[t % 2][:, :].rearrange("p (n k) -> p n k", n=n)
                            if nk == 128:
                                bi = bias[:, h, 1, 128:256].unsqueeze(1).to_broadcast((P, n, nk))
                            elif has_prev(g, blocks[0]):
                                bi = bias[:, h, 1, :].unsqueeze(1).to_broadcast((P, n, nk))
                            else:
                                bi = bias[:, h, :, :]
                            nc.vector.scalar_tensor_tensor(out, sc, -SCALE, bi, ALU.mult,
                                                           ALU.add).then_inc(s_biased, 1)
                            dve.wait_ge(s_biased, t + 1)
                            at = h * NBLK + blocks[0]
                            nc.vector.tensor_reduce(stat[:, 0, at:at + n], out, AX.X, ALU.min).then_inc(s_min, 1)

                        def keep_turned(t):
                            dve.wait_ge(t_mm, t + 1)
                            if t >= 3:
                                dve.wait_ge(o_mm, t - 2)
                            nc.vector.tensor_copy(ptr[:, t % 3, :], psum[2 + t % 2][:, :]).then_inc(t_out, 1)

                        for n in range(NH // 2):
                            dve.wait_ge(bias_turned, n + 1)
                            src = psum[2 + n][:, :].rearrange("p (a k) -> p a k", a=2)
                            nc.vector.tensor_copy(bias[:, 2 * n:2 * n + 2, 1, :], src).then_inc(bias_kept2, 1)
                        dve.wait_ge(bias_kept2, NH // 2)
                        nc.vector.tensor_copy(bias[:, :, 0, P:2 * P], bias[:, :, 1, P:2 * P]).then_inc(bias_kept2, 1)
                        dve.wait_ge(bias_kept2, NH // 2 + 1)
                        dve.wait_ge(first_mask, 2)
                        for t in range(NT_B + 2):
                            if t < NT_B:
                                negate_and_min(t)
                            if t >= 2:
                                keep_turned(t - 2)
                        dve.wait_ge(st_mm, 1)
                        nc.vector.tensor_copy(strow[:, :, :].rearrange("p a b -> p (a b)"),
                                              psum[0][:, :]).then_inc(st_out, 1)

                    @block.scalar
                    def _(act):
                        def exponentials(t):
                            h, g, blocks, nk = batches[t]
                            act.wait_ge(s_min, t + 1)
                            if t >= 3:
                                act.wait_ge(t_mm, t - 2)
                            for i, b in enumerate(blocks):
                                at = h * NBLK + b
                                nc.scalar.activation(esc[:, t % 3, nk * i:nk * (i + 1)],
                                                     tsc[:, t % 3, nk * i:nk * (i + 1)], ACT.Exp,
                                                     bias=stat[:, 0, at:at + 1], scale=-1.0,
                                                     accum_out=stat[:, 1, at:at + 1]).then_inc(e_done, 1)

                        def keep_output(bank, batch):
                            h, b4 = divmod(bank, NBLK // 4)
                            g, r = h // HPG, DIL[h // HPG]
                            rows = slice(64 * (h % 2), 64 * (h % 2) + 64)
                            act.wait_ge(o_mm, batch + 1)
                            src = psum[4 + bank % 4][rows, :]
                            dst = oT[rows, h // 2, :]
                            if r == 1:
                                dst = dst[:, CW * b4:CW * (b4 + 1)]
                            elif r == 4:
                                dst = dst.rearrange("p (m r) -> p r m", r=r)[:, b4, :]
                            else:
                                dst = dst.rearrange("p (m r) -> p r m", r=r)[:, 4 * b4:4 * b4 + 4, :]
                                src = src.rearrange("p (r m) -> p r m", r=4)
                            nc.scalar.activation(dst, src, ACT.Copy).then_inc(o_out, 1)

                        kept = 0
                        for t in range(NT_B + 4):
                            if t < NT_B:
                                exponentials(t)
                            if t >= 4:
                                h, g, blocks, nk = batches[t - 4]
                                if blocks[-1] % 4 == 3:
                                    keep_output(kept, t - 4)
                                    kept += 1

            cmb_loaded, cmb, cmb_exp, f_kept = sem("cmb_loaded"), sem("cmb"), sem("cmb_exp"), sem("f_kept")
            fz_loaded = [sem(f"fz_loaded{i}") for i in range(2)]
            weighted, gated, oa_kept = sem("weighted"), sem("gated"), [sem(f"oa_kept{i}") for i in range(2)]
            with ExitStack() as pb:
                R64 = HPG * NBLK
                sraw = sb(pb, "sraw", [R64, 3, 2, P])
                sm = sb(pb, "sm", [R64, 3, 2, P])
                mn = sb(pb, "mn", [R64, P])
                fe = sb(pb, "fe", [R64, 3, P])
                el = sb(pb, "el", [R64, 3, P])
                fb = sb(pb, "fb", [P, 2, L])
                zb = sb(pb, "zb", [P, 2, L])
                with nc.Block() as block:
                    @block.sync
                    def _(sp):
                        st_rows = st_d.rearrange("w (h b) c -> w h (b c)", b=NBLK)
                        for pair in range(2):
                            sp.dma_start(zb[:, pair, :], proj_d[T_ZA + pair]).then_inc(fz_loaded[pair], 16)
                        for g, r in enumerate(DIL):
                            for w in range(2):
                                for j in range(HPG):
                                    src = st_rows[w, HPG * g + j].rearrange("(r a m) -> a r m", r=r, a=NBLK)
                                    dst = sraw[NBLK * j:NBLK * (j + 1), g, w, :].rearrange("p (r m) -> p r m", r=r)
                                    sp.dma_start(dst, src).then_inc(cmb_loaded, 16)
                        sp.wait_ge(cmb, 11)
                        for g in range(3):
                            sp.dma_start(f_d[g].rearrange("j a c -> (j a) c"), fe[:, g, :]).then_inc(f_kept, 16)
                        sp.wait_ge(f_kept, 48)
                        for pair in range(NH // 2):
                            i = pair % 2
                            if pair >= 2:
                                sp.wait_ge(oa_kept[i], 16 * (pair // 2))
                                sp.dma_start(zb[:, i, :], proj_d[T_ZA + pair]).then_inc(fz_loaded[i], 16)
                            for half in range(2):
                                g, j = divmod(2 * pair + half, HPG)
                                src = f_d[g, j].rearrange("a c -> (a c)").partition_broadcast(64)
                                sp.dma_start(fb[64 * half:64 * half + 64, i, :], src).then_inc(fz_loaded[i], 16)
                            sp.wait_ge(gated, pair + 1)
                            sp.dma_start(o_d[6 + pair], zb[:, i, :]).then_inc(oa_kept[i], 16)
                        for i in range(2):
                            sp.wait_ge(oa_kept[i], 16 * 3)

                    @block.vector
                    def _(dve):
                        n = [0]

                        def link(ins):
                            n[0] += 1
                            ins.then_inc(cmb, 1)
                            dve.wait_ge(cmb, n[0])

                        dve.wait_ge(cmb_loaded, 16 * 6 * HPG)
                        for g, r in enumerate(DIL):
                            link(nc.vector.tensor_copy(
                                sm[:, g, :, :].rearrange("p w (m r) -> p w r m", r=r),
                                sraw[:, g, :, :].rearrange("p w (r m) -> p w r m", r=r)))
                        link(nc.vector.tensor_tensor(mn[:, :], sm[:, 0, 0, :], sm[:, 1, 0, :], ALU.min))
                        link(nc.vector.tensor_tensor(mn[:, :], mn[:, :], sm[:, 2, 0, :], ALU.min))
                        link(nc.vector.tensor_tensor(fe[:, :, :], mn[:, :].unsqueeze(1).to_broadcast((R64, 3, P)),
                                                     sm[:, :, 0, :], ALU.subtract))
                        dve.wait_ge(cmb_exp, 1)
                        link(nc.vector.tensor_tensor(el[:, :, :], fe[:, :, :], sm[:, :, 1, :], ALU.mult))
                        link(nc.vector.tensor_tensor(mn[:, :], el[:, 0, :], el[:, 1, :], ALU.add))
                        link(nc.vector.tensor_tensor(mn[:, :], mn[:, :], el[:, 2, :], ALU.add))
                        link(nc.vector.reciprocal(mn[:, :], mn[:, :]))
                        link(nc.vector.tensor_tensor(fe[:, :, :], fe[:, :, :],
                                                     mn[:, :].unsqueeze(1).to_broadcast((R64, 3, P)), ALU.mult))
                        for pair in range(NH // 2):
                            i = pair % 2
                            dve.wait_ge(fz_loaded[i], 48 * (pair // 2 + 1))
                            nc.vector.tensor_tensor(oT[:, pair, :], oT[:, pair, :], fb[:, i, :],
                                                    ALU.mult).then_inc(weighted, 1)
                            dve.wait_ge(weighted, pair + 1)
                            nc.vector.tensor_tensor(zb[:, i, :], oT[:, pair, :], zb[:, i, :],
                                                    ALU.mult).then_inc(gated, 1)

                    @block.scalar
                    def _(act):
                        act.wait_ge(cmb, 6)
                        nc.scalar.activation(fe[:, :, :], fe[:, :, :], ACT.Exp).then_inc(cmb_exp, 1)

        MSCALE = MD ** -0.5
        MB = L // (2 * P)
        qm_loaded = [sem(f"qm_loaded{i}") for i in range(2)]
        om_kept = [sem(f"om_kept{i}") for i in range(2)]
        ms_mm, m_max, m_bias, m_exp, m_rec, m_norm, mt_mm, mt_out, mo_mm, mo_out = (sem(a) for a in (
            "ms_mm", "m_max", "m_bias", "m_exp", "m_rec", "m_norm", "mt_mm", "mt_out", "mo_mm", "mo_out"))
        with ExitStack() as ph:
            qm = sb(ph, "qm", [P, 2, L])
            zm = sb(ph, "zm", [P, 2, L])
            mx = sb(ph, "mx", [P, 4, 2])
            nb = sb(ph, "nb", [P, 4, 2])
            ls = sb(ph, "ls", [P, 4, 2])
            rl = sb(ph, "rl", [P, 4, 2])
            em = sb(ph, "em", [P, 4, 2, ML])
            pt = sb(ph, "pt", [P, 3, 2, 2 * P])
            NT_M = MH * MB
            with nc.Block() as block:
                @block.sync
                def _(sp):
                    for h in range(MH):
                        i = h % 2
                        if h >= 2:
                            sp.wait_ge(om_kept[i], 16 * (h // 2))
                        sp.dma_start(qm[:, i, :], proj_d[T_QM + h]).then_inc(qm_loaded[i], 16)
                        sp.dma_start(zm[:, i, :], proj_d[T_ZM + h]).then_inc(qm_loaded[i], 16)

                @block.gpsimd
                def _(pool):
                    for h in range(MH):
                        pool.wait_ge(mo_out, MB * (h + 1))
                        pool.dma_start(o_d[12 + h], zm[:, h % 2, :]).then_inc(om_kept[h % 2], 16)
                    for i in range(2):
                        pool.wait_ge(om_kept[i], 32)

                @block.tensor
                def _(pe):
                    def scores(t):
                        h, b = divmod(t, MB)
                        pe.wait_ge(qm_loaded[h % 2], 32 * (h // 2 + 1))
                        if t >= 2:
                            pe.wait_ge(m_exp, 2 * (t - 1))
                        for i in range(2):
                            q = qm[:, h % 2, P * (2 * b + i):P * (2 * b + i + 1)]
                            mm = nc.tensor.matmul(psum[t % 2][:, ML * i:ML * (i + 1)], q, k_mem[:, h, :],
                                                  start=True, stop=True)
                        mm.then_inc(ms_mm, 1)

                    def turn(t):
                        pe.wait_ge(m_norm, 2 * (t + 1))
                        if t >= 2:
                            pe.wait_ge(mt_out, t - 1)
                        for kb in range(2):
                            for i in range(2):
                                mm = nc.tensor.transpose(psum[2 + t % 2][:, P * (2 * kb + i):P * (2 * kb + i + 1)],
                                                         em[:, t % 4, i, P * kb:P * (kb + 1)], ident[:, :])
                        mm.then_inc(mt_mm, 1)

                    def output(t):
                        h = t // MB
                        pe.wait_ge(mt_out, t + 1)
                        if t >= 2:
                            pe.wait_ge(mo_out, t - 1)
                        for kb in range(2):
                            mm = nc.tensor.matmul(psum[4 + t % 2][:, 0:2 * P], v_mem[:, kb, MD * h:MD * (h + 1)],
                                                  pt[:, t % 3, kb, :], start=(kb == 0), stop=(kb == 1))
                        mm.then_inc(mo_mm, 1)

                    for t in range(NT_M + 3):
                        if t < NT_M:
                            scores(t)
                        if 0 <= t - 2 < NT_M:
                            turn(t - 2)
                        if 0 <= t - 3 < NT_M:
                            output(t - 3)

                @block.vector
                def _(dve):
                    def maximum(t):
                        dve.wait_ge(ms_mm, t + 1)
                        nc.vector.tensor_reduce(mx[:, t % 4, :], psum[t % 2][:, :].rearrange("p (n k) -> p n k", n=2),
                                                AX.X, ALU.max).then_inc(m_max, 1)
                        dve.wait_ge(m_max, t + 1)
                        if t >= 4:
                            dve.wait_ge(m_exp, 2 * (t - 3))
                        nc.vector.tensor_scalar(nb[:, t % 4, :], mx[:, t % 4, :], -MSCALE, None,
                                                ALU.mult).then_inc(m_bias, 1)

                    def normalise(t):
                        dve.wait_ge(m_exp, 2 * (t + 1))
                        nc.vector.reciprocal(rl[:, t % 4, :], ls[:, t % 4, :]).then_inc(m_rec, 1)
                        dve.wait_ge(m_rec, t + 1)
                        for i in range(2):
                            nc.vector.tensor_scalar(em[:, t % 4, i, :], em[:, t % 4, i, :], rl[:, t % 4, i:i + 1],
                                                    None, ALU.mult).then_inc(m_norm, 1)

                    def gate(t):
                        h, b = divmod(t, MB)
                        dve.wait_ge(mo_mm, t + 1)
                        dve.wait_ge(qm_loaded[h % 2], 32 * (h // 2 + 1))
                        z = zm[:, h % 2, 2 * P * b:2 * P * (b + 1)]
                        nc.vector.tensor_tensor(z, psum[4 + t % 2][:, 0:2 * P], z, ALU.mult).then_inc(mo_out, 1)

                    for t in range(NT_M + 4):
                        if t < NT_M:
                            maximum(t)
                        if 0 <= t - 1 < NT_M:
                            normalise(t - 1)
                        if 0 <= t - 4 < NT_M:
                            gate(t - 4)

                @block.scalar
                def _(act):
                    def exponentials(t):
                        act.wait_ge(m_bias, t + 1)
                        if t >= 4:
                            act.wait_ge(mt_mm, t - 3)
                        for i in range(2):
                            nc.scalar.activation(em[:, t % 4, i, :], psum[t % 2][:, ML * i:ML * (i + 1)], ACT.Exp,
                                                 bias=nb[:, t % 4, i:i + 1], scale=MSCALE,
                                                 accum_out=ls[:, t % 4, i:i + 1]).then_inc(m_exp, 1)

                    def keep_turned(t):
                        act.wait_ge(mt_mm, t + 1)
                        if t >= 3:
                            act.wait_ge(mo_mm, t - 2)
                        nc.scalar.activation(pt[:, t % 3, :, :].rearrange("p a b -> p (a b)"), psum[2 + t % 2][:, :],
                                             ACT.Copy).then_inc(mt_out, 1)

                    for t in range(NT_M + 2):
                        if t < NT_M:
                            exponentials(t)
                        if t >= 2:
                            keep_turned(t - 2)

        yr_loaded = [sem(f"yr_loaded{i}") for i in range(2)]
        ys_hi_done, ys_split = sem("ys_hi_done"), sem("ys_split")
        g_mm, g_sig, g_y, g_z = sem("g_mm"), sem("g_sig"), sem("g_y"), sem("g_z")
        zs_loaded = [sem(f"zs_loaded{i}") for i in range(2)]
        os_kept = [sem(f"os_kept{i}") for i in range(2)]
        N_GLU = NKV + N_MAIN
        with ExitStack() as ph:
            ys_hi = sb(ph, "ys_hi", [P, KS, L], F32R)
            ys_lo = sb(ph, "ys_lo", [P, KS, L], F32R)
            yr = sb(ph, "yr", [P, 2, L])
            sg = sb(ph, "sg", [P, 2, CW])
            zs = sb(ph, "zs", [P, 2, L])
            with nc.Block() as block:
                @block.sync
                def _(sp):
                    for i in range(2 * KS):
                        if i in (0, 1, KS + 2):
                            pair = min(i, 2)
                            load_pair(sp, N_GLU + pair, w_glu[2 * pair], w_glu[2 * pair + 1], KS)
                        if 2 <= i < 2 + KS:
                            sp.wait_ge(ys_split, i - 1)
                        elif i >= 2:
                            sp.wait_ge(g_z, NQ * (i - 1 - KS))
                        sp.dma_start(yr[:, i % 2, :], ys_d[i % KS]).then_inc(yr_loaded[i % 2], 16)

                @block.gpsimd
                def _(pool):
                    for n in range(2):
                        pool.dma_start(zs[:, n, :], proj_d[T_ZS + n]).then_inc(zs_loaded[n], 16)
                    for n in range(KS):
                        i = n % 2
                        pool.wait_ge(g_z, NQ * (n + 1))
                        pool.dma_start(o_d[n], zs[:, i, :]).then_inc(os_kept[i], 16)
                        if n + 2 < KS:
                            pool.wait_ge(os_kept[i], 16 * (n // 2 + 1))
                            pool.dma_start(zs[:, i, :], proj_d[T_ZS + n + 2]).then_inc(zs_loaded[i], 16)
                    for i in range(2):
                        pool.wait_ge(os_kept[i], 16 * KS // 2)

                @block.scalar
                def _(act):
                    for k in range(KS):
                        act.wait_ge(yr_loaded[k % 2], 16 * (k // 2 + 1))
                        nc.scalar.activation(ys_hi[:, k, :], yr[:, k % 2, :], ACT.Copy).then_inc(ys_hi_done, 1)
                    for n in range(KS):
                        for c in range(NQ):
                            u = NQ * n + c
                            act.wait_ge(g_mm, u + 1)
                            if u >= 2:
                                act.wait_ge(g_y, u - 1)
                            nc.scalar.activation(sg[:, u % 2, :], psum[4 * (n % 2) + c][:, :], ACT.Sigmoid,
                                                 bias=bglu[:, n:n + 1]).then_inc(g_sig, 1)

                @block.vector
                def _(dve):
                    split_pair(dve, N_GLU, lambda s: (mm_done, 8 * N_MAIN), KS)
                    for k in range(KS):
                        dve.wait_ge(ys_hi_done, k + 1)
                        nc.vector.tensor_tensor(ys_lo[:, k, :], yr[:, k % 2, :], ys_hi[:, k, :].bitcast(F32),
                                                ALU.subtract).then_inc(ys_split, 1)
                    for pair in range(3):
                        for n in (2 * pair, 2 * pair + 1):
                            dve.wait_ge(yr_loaded[n % 2], 16 * ((KS + n) // 2 + 1))
                            dve.wait_ge(zs_loaded[n % 2], 16 * (n // 2 + 1))
                            for c in range(NQ):
                                u = NQ * n + c
                                dve.wait_ge(g_sig, u + 1)
                                y = yr[:, n % 2, CW * c:CW * (c + 1)]
                                nc.vector.tensor_tensor(y, sg[:, u % 2, :], y, ALU.mult).then_inc(g_y, 1)
                                dve.wait_ge(g_y, u + 1)
                                z = zs[:, n % 2, :].rearrange("p (c s) -> p s c", s=CH)[
                                    :, CW // NC * c:CW // NC * (c + 1), :]
                                nc.vector.tensor_tensor(z, y.rearrange("p (s c) -> p s c", c=NC), z,
                                                        ALU.mult).then_inc(g_z, 1)
                            if pair < 2:
                                split_pair(dve, N_GLU + pair + 1, lambda s: (g_mm, 8 * pair + 4 * s + 4), KS,
                                           (n % 2,))

                @block.tensor
                def _(pe):
                    pe.wait_ge(ys_split, KS)
                    for n in range(KS):
                        s = n % 2
                        pe.wait_ge(w_split[s], N_GLU + n // 2 + 1)
                        for c in range(NQ):
                            if n >= 2:
                                pe.wait_ge(g_sig, NQ * (n - 2) + c + 1)
                            cols = slice(CW * c, CW * (c + 1))
                            three_pass(psum[4 * s + c][:, :], [
                                (wt(s, k), (ys_hi[:, k, cols], ys_lo[:, k, cols]))
                                for k in range(KS)]).then_inc(g_mm, 1)

        NBR, NOUT = D // P, D // (2 * P)
        N_MRG = N_GLU + 3
        o_loaded, o_hi_done, o_split = sem("o_loaded"), sem("o_hi_done"), sem("o_split")
        gt_loaded = [sem(f"gt_loaded{i}") for i in range(2)]
        xq_loaded, y_kept = sem("xq_loaded"), sem("y_kept")
        b_half = sem("b_half")
        b_mm, b_gated, b_sum, m_hi_done, m_split = (sem(a) for a in (
            "b_mm", "b_gated", "b_sum", "m_hi_done", "m_split"))
        p_mm, y_sum, y_sq, y_acc, f_mm, f_root, f_rstd, y_out_ready = (sem(a) for a in (
            "p_mm", "y_sum", "y_sq", "y_acc", "f_mm", "f_root", "f_rstd", "y_out_ready"))
        with ExitStack() as ph:
            KO = 16
            orw = sb(ph, "orw", [P, KO, CW])
            o_hi = sb(ph, "o_hi", [P, KO, CW], F32R)
            o_lo = sb(ph, "o_lo", [P, KO, CW], F32R)
            gt = sb(ph, "gt", [P, 2, 3, CW])
            m_hi = sb(ph, "m_hi", [P, KD, CW], F32R)
            m_lo = sb(ph, "m_lo", [P, KD, CW], F32R)
            xq = sb(ph, "xq", [P, KD, CW])
            tb = sb(ph, "tb", [P, CW])
            sqb = sb(ph, "sqb", [P, CW])
            acc = sb(ph, "acc", [P, CW])
            rs = sb(ph, "rs", [P, CW])
            BR = ((0, 6), (6, 12), (12, 16))

            def chunk_cols(q):
                return slice(CW * q, CW * (q + 1))

            with nc.Block() as block:
                @block.sync
                def _(sp):
                    for q in range(NQ):
                        if q == 0:
                            sp.dma_start(orw[:, :, :], o_d[:, :, chunk_cols(0)].rearrange(
                                "k p c -> p k c")).then_inc(o_loaded, 16)
                        for i in range(NBR):
                            load_pair(sp, N_MRG + 12 * q + i, w_br[i, 0], w_br[i, 1])
                            if i == 1:
                                if q:
                                    sp.wait_ge(y_kept, 16 * q)
                                sp.dma_start(xq[:, :, :], x_t[:, :, chunk_cols(q)]).then_inc(xq_loaded, 16)
                            if i == 4 and q + 1 < NQ:
                                sp.wait_ge(o_split, 4 * (q + 1))
                                sp.dma_start(orw[:, :, :], o_d[:, :, chunk_cols(q + 1)].rearrange(
                                    "k p c -> p k c")).then_inc(o_loaded, 16)
                        for i in range(NOUT):
                            load_pair(sp, N_MRG + 12 * q + NBR + i, w_out[2 * i], w_out[2 * i + 1])

                @block.gpsimd
                def _(pool):
                    for q in range(NQ):
                        for n in range(NBR):
                            u = NBR * q + n
                            if u >= 2:
                                pool.wait_ge(b_sum, u - 1)
                            src = proj_d[T_G:NT].rearrange("(b n) p c -> n p b c", b=3)
                            pool.dma_start(gt[:, u % 2, :, :], src[n][:, :, chunk_cols(q)]).then_inc(
                                gt_loaded[u % 2], 16)
                            if n == 2 and q:
                                pool.wait_ge(y_out_ready, KD * q)
                                pool.dma_start(y_out[:, :, chunk_cols(q - 1)], xq[:, :, :]).then_inc(y_kept, 16)
                    pool.wait_ge(y_out_ready, KD * NQ)
                    pool.dma_start(y_out[:, :, chunk_cols(NQ - 1)], xq[:, :, :]).then_inc(y_kept, 16)
                    pool.wait_ge(y_kept, 16 * NQ)

                @block.tensor
                def _(pe):
                    def total(q):
                        pe.wait_ge(y_acc, KD * (q + 1))
                        nc.tensor.matmul(psum[7][:, :], ones[:, :], acc[:, :], start=True, stop=True).then_inc(f_mm, 1)

                    for q in range(NQ):
                        for n in range(NBR):
                            u = NBR * q + n
                            for s in range(2):
                                pe.wait_ge(w_split[s], N_MRG + 12 * q + n + 1)
                            if n == 0:
                                pe.wait_ge(o_split, 4 * (q + 1))
                            for b, (k0, k1) in enumerate(BR):
                                if u >= 2:
                                    pe.wait_ge(b_gated, 3 * (u - 2) + b + 1)
                                three_pass(psum[3 * (n % 2) + b][:, :], [
                                    (wt(k // 8, k % 8), (o_hi[:, k, :], o_lo[:, k, :]))
                                    for k in range(k0, k1)]).then_inc(b_mm, 1)
                            if n == 0 and q:
                                total(q - 1)
                        for n in range(KD):
                            pe.wait_ge(w_split[n % 2], N_MRG + 12 * q + NBR + n // 2 + 1)
                            if n == 0:
                                pe.wait_ge(m_split, KD * (q + 1))
                            if n < 2 and q:
                                pe.wait_ge(y_sum, KD * q)
                                pe.wait_ge(f_root, q)
                            if n >= 2:
                                pe.wait_ge(y_sum, KD * q + n - 1)
                            three_pass(psum[6 + n % 2][:, :], [
                                (wt(n % 2, k), (m_hi[:, k, :], m_lo[:, k, :])) for k in range(KD)]).then_inc(p_mm, 1)
                    total(NQ - 1)

                @block.scalar
                def _(act):
                    def split_hi(q, piece):
                        act.wait_ge(o_loaded, 16 * (q + 1))
                        if q:
                            act.wait_ge(b_mm, 3 * NBR * q)
                        ks = slice(4 * piece, 4 * piece + 4)
                        nc.scalar.activation(o_hi[:, ks, :], orw[:, ks, :], ACT.Copy).then_inc(o_hi_done, 1)

                    def root(q):
                        act.wait_ge(f_mm, q + 1)
                        nc.scalar.activation(rs[:, :], psum[7][:, :], ACT.Sqrt, bias=eps[:, 0:1],
                                             scale=1.0 / D).then_inc(f_root, 1)

                    for piece in range(4):
                        split_hi(0, piece)
                    for q in range(NQ):
                        for n in range(NBR):
                            u = NBR * q + n
                            act.wait_ge(b_sum, u + 1)
                            if n == 0 and q:
                                act.wait_ge(p_mm, KD * q)
                            nc.scalar.activation(m_hi[:, n, :], tb[:, :], ACT.Copy).then_inc(m_hi_done, 1)
                            if n == 0 and q:
                                root(q - 1)
                        for n in range(KD):
                            u = KD * q + n
                            act.wait_ge(y_sum, u + 1)
                            if u >= 1:
                                act.wait_ge(y_acc, u)
                            nc.scalar.activation(sqb[:, :], xq[:, n, :], ACT.Square).then_inc(y_sq, 1)
                            if n % 2 and q + 1 < NQ:
                                split_hi(q + 1, n // 2)
                    root(NQ - 1)

                @block.vector
                def _(dve):
                    def split_lo(q, piece):
                        dve.wait_ge(o_hi_done, 4 * q + piece + 1)
                        ks = slice(4 * piece, 4 * piece + 4)
                        nc.vector.tensor_tensor(o_lo[:, ks, :], orw[:, ks, :], o_hi[:, ks, :].bitcast(F32),
                                                ALU.subtract).then_inc(o_split, 1)

                    def normalise(q):
                        dve.wait_ge(f_root, q + 1)
                        nc.vector.reciprocal(rs[:, :], rs[:, :]).then_inc(f_rstd, 1)
                        dve.wait_ge(f_rstd, q + 1)
                        for n in range(KD):
                            nc.vector.scalar_tensor_tensor(xq[:, n, :], xq[:, n, :], g_in[:, 2, n:n + 1], rs[:, :],
                                                           ALU.mult, ALU.mult).then_inc(y_out_ready, 1)

                    def used(q, i):
                        if q == 0 and i == 0:
                            return lambda s: (g_mm, 4 * KS)
                        if i == 0:
                            return lambda s: (p_mm, KD * q - 1 + s)
                        if i <= NBR:
                            return lambda s: (b_mm, 3 * (NBR * q + i - 1) + 2 + s)
                        return lambda s: (p_mm, KD * q + 2 * (i - NBR - 1) + 1 + s)

                    for piece in range(4):
                        if piece == 0:
                            split_pair(dve, N_MRG, used(0, 0))
                        split_lo(0, piece)
                    for q in range(NQ):
                        for n in range(NBR):
                            u = NBR * q + n
                            dve.wait_ge(gt_loaded[u % 2], 16 * (u // 2 + 1))
                            gates = gt[:, u % 2, :, :]
                            for b in range(3):
                                dve.wait_ge(b_mm, 3 * u + b + 1)
                                nc.vector.tensor_tensor(gates[:, b, :], psum[3 * (n % 2) + b][:, :], gates[:, b, :],
                                                        ALU.mult).then_inc(b_gated, 1)
                            split_pair(dve, N_MRG + 12 * q + n + 1, used(q, n + 1))
                            dve.wait_ge(b_gated, 3 * (u + 1))
                            nc.vector.tensor_tensor(gates[:, 0, :], gates[:, 0, :], gates[:, 1, :],
                                                    ALU.add).then_inc(b_half, 1)
                            dve.wait_ge(b_half, u + 1)
                            if u:
                                dve.wait_ge(m_split, u)
                            nc.vector.tensor_tensor(tb[:, :], gates[:, 0, :], gates[:, 2, :],
                                                    ALU.add).then_inc(b_sum, 1)
                            dve.wait_ge(m_hi_done, u + 1)
                            nc.vector.tensor_tensor(m_lo[:, n, :], tb[:, :], m_hi[:, n, :].bitcast(F32),
                                                    ALU.subtract).then_inc(m_split, 1)
                            if n == 0 and q:
                                normalise(q - 1)
                        dve.wait_ge(xq_loaded, 16 * (q + 1))
                        for n in range(KD):
                            u = KD * q + n
                            dve.wait_ge(p_mm, u + 1)
                            nc.vector.tensor_tensor(xq[:, n, :], psum[6 + n % 2][:, :], xq[:, n, :],
                                                    ALU.add).then_inc(y_sum, 1)
                            i = NBR + n // 2 + 1
                            if n % 2:
                                if i < 12:
                                    split_pair(dve, N_MRG + 12 * q + i, used(q, i))
                                elif q + 1 < NQ:
                                    split_pair(dve, N_MRG + 12 * (q + 1), used(q + 1, 0))
                            dve.wait_ge(y_sq, u + 1)
                            if n == 0:
                                if q:
                                    dve.wait_ge(f_mm, q)
                                nc.vector.tensor_copy(acc[:, :], sqb[:, :]).then_inc(y_acc, 1)
                            else:
                                dve.wait_ge(y_acc, u)
                                nc.vector.tensor_tensor(acc[:, :], acc[:, :], sqb[:, :], ALU.add).then_inc(y_acc, 1)
                            if n % 2 and q + 1 < NQ:
                                split_lo(q + 1, n // 2)
                    normalise(NQ - 1)


def _dram_inputs(nc, arrays):
    return {n: nc.dram_tensor(n, a.shape, mybir.dt.from_np(a.dtype), kind="ExternalInput").ap()
            for n, a in arrays.items()}


def rel_buckets():
    out = np.zeros((NBUCKET + 1, 3, 384), np.float32)
    for g, r in enumerate(DIL):
        for x in range(384):
            delta = 255 - x
            if not 0 <= delta <= P:
                out[NBUCKET, g, x] = -BIG
                continue
            n = delta * r
            if n < NBUCKET // 2:
                b = n
            else:
                b = NBUCKET // 2 + int(np.float32(
                    np.log(np.float32(n) / np.float32(NBUCKET // 2)) / np.float32(math.log(MAXD / (NBUCKET // 2)))
                    * np.float32(NBUCKET - NBUCKET // 2)))
                b = min(b, NBUCKET - 1)
            out[b, g, x] = 1.0
    return out


def layouts(i):
    def f(a):
        return np.ascontiguousarray(a, np.float32)

    def tiles(w):
        k, n = w.shape
        return f(w.reshape(k // P, P, n // P, P).transpose(2, 1, 0, 3))

    def by_channel(v):
        return f(v.reshape(-1, P).T)

    def transposed(x):
        return f(x.T.reshape(-1, P, x.shape[0]).transpose(1, 0, 2))

    def stack(re, im):
        return np.concatenate([re, im], 1)

    i = {k: np.asarray(v) for k, v in i.items()}
    lam = [i[n][0].T for n in ("ssm_lambda_re", "ssm_lambda_im")]
    dt = np.broadcast_to(i["ssm_log_dt"][0], (NS, G))
    b = [i[n][0].transpose(1, 0, 2) for n in ("ssm_b_re", "ssm_b_im")]
    c = [i[n][0].transpose(2, 0, 1) for n in ("ssm_c_re", "ssm_c_im")]

    def unit(parts, u):
        gs = slice(UG * u, UG * (u + 1))
        return np.concatenate([np.concatenate([p[:, gs].reshape(NS, -1) for p in half], 1) for half in parts], 0)

    halves = ([lam[0], lam[1], dt, c[0], c[1], b[0], b[1]], [lam[0], lam[1], dt, c[1], c[0], b[1], b[0]])
    ssm_par = np.stack([unit(halves, u) for u in range(NU)])
    d = i["ssm_d"][0].reshape(NU, 1, UG, HG)
    br = np.concatenate([i["w_br_ssm"][0], i["w_br_attn"][0], i["w_br_mem"][0]], 0)
    w_br = tiles(br).reshape(D // P, P, 2, 8, P).transpose(0, 2, 1, 3, 4)
    return {
        "x_t": transposed(i["x"][0]), "mem_t": transposed(i["mem"][0]),
        "norm_g": by_channel(i["norm_g"][0]), "mem_norm_g": by_channel(i["mem_norm_g"][0]),
        "final_g": by_channel(i["final_norm_g"]),
        "w_in": tiles(i["w_in"][0]), "w_kv": tiles(i["w_mem_kv"][0]), "b_gate": by_channel(i["b_gate"][0]),
        "ssm_par": f(ssm_par), "ssm_d": f(np.broadcast_to(d, (NU, HG, UG, HG))),
        "w_glu": tiles(i["w_glu"][0]), "b_glu": by_channel(i["b_glu"][0]),
        "w_br": f(w_br), "w_out": tiles(i["w_out"][0]), "rel_bias": f(i["rel_bias"]),
        "buckets": rel_buckets(), "ident_c": np.eye(P, dtype=np.float32),
        "anti_c": np.eye(P, dtype=np.float32)[::-1].copy(),
        "sign_c": np.repeat(np.array([1.0, -1.0], np.float32), NS)[:, None].copy(),
        "steps_c": np.tile(np.arange(1, NC + 1, dtype=np.float32), (P, 1)),
        "powers_c": np.tile(np.r_[np.arange(CH + 1), np.arange(CH)[::-1]].astype(np.float32), (P, 1)),
    }


def kernel(**inputs):
    import concourse.bacc as _bacc
    from concourse.bass_utils import run_bass_kernel_spmd as _run

    nc = _bacc.Bacc("TRN2", target_bir_lowering=False, num_devices=1)
    arrays = layouts(inputs)
    aps = _dram_inputs(nc, arrays)
    y_out = nc.dram_tensor("y_out", (P, KD, L), F32, kind="ExternalOutput").ap()
    build_program(nc, y_out=y_out, **aps)
    r = _run(nc, [arrays], core_ids=[0])
    y = r.results[0]["y_out"]
    return np.ascontiguousarray(y.transpose(2, 1, 0).reshape(1, L, D))
```

```python
import math
from contextlib import ExitStack

import numpy as np
import concourse.bass as bass
from concourse import mybir

F32 = mybir.dt.float32
F32R = mybir.dt.float32r
ACT = mybir.ActivationFunctionType
ALU = mybir.AluOpType
AX = mybir.AxisListType

P = 128
D = 1024
L = 2048
KD = D // P
CW = 512
NQ = L // CW
EPS = 1e-6
D_SSM, HG, NS = 768, 16, 64
G = D_SSM // HG
GB = P // HG
NB = G // GB
UG = 4
NU = G // UG
CH = P // HG
NC = L // CH
HD, HPG = 64, 4
DIL = (1, 4, 16)
NH = HPG * len(DIL)
NBLK = L // P
KS = D_SSM // P
MH, MD, ML = 4, 128, 256
NBUCKET, MAXD = 32, 2048
BIG = 1e30
T_U, T_ZS, T_Q, T_K, T_V, T_ZA, T_QM, T_ZM, T_G = 0, 6, 12, 18, 24, 30, 36, 40, 44
NT = 68
TWO_PI_HI = 6.28125
TWO_PI_LO = 2 * math.pi - TWO_PI_HI
MAGIC = 1.5 * 2 ** 23
PI_SAFE = 3.1415925


def build_program(nc, x_t, mem_t, norm_g, mem_norm_g, final_g, w_in, w_kv, b_gate, ssm_par, ssm_d, w_glu, b_glu,
                  w_br, w_out, rel_bias, buckets, ident_c, anti_c, sign_c, steps_c, powers_c, y_out):
    ctx = ExitStack()
    with ctx:
        def sb(stack, name, shape, dt=F32):
            return stack.enter_context(nc.sbuf_tensor(name, shape, dt))

        def sem(name):
            return ctx.enter_context(nc.semaphore(name))

        def dram(name, shape):
            return nc.dram_tensor(name, shape, F32).ap()

        proj_d = dram("proj_d", [NT, P, L])
        v_d = dram("v_d", [3, P, 2 * L])
        ys_d = dram("ys_d", [KS, P, L])
        o_d = dram("o_d", [16, P, L])
        mats_d = dram("mats_d", [NU, P, UG, 5, P])
        cs_d = dram("cs_d", [NU, P, UG, 2, NC])
        m8_d = dram("m8_d", [NU, P, UG])
        bias_d = dram("bias_d", [3, NH, 384])
        st_d = dram("st_d", [2, NH * NBLK, P])
        f_d = dram("f_d", [3, HPG, NBLK, P])

        psum = [ctx.enter_context(nc.psum_tensor(f"bank{i}", [P, 512], F32)) for i in range(8)]

        w_raw = sb(ctx, "w_raw", [P, 2, KD, P])
        w_hi = sb(ctx, "w_hi", [P, 2, KD, P], F32R)
        w_lo = sb(ctx, "w_lo", [P, 2, KD, P], F32R)
        k_mem = sb(ctx, "k_mem", [P, MH, ML])
        v_mem = sb(ctx, "v_mem", [P, 2, MH * MD])
        ones = sb(ctx, "ones", [P, P])
        g_in = sb(ctx, "g_in", [P, 3, KD])
        bg = sb(ctx, "bg", [P, 24])
        bglu = sb(ctx, "bglu", [P, KS])
        eps = sb(ctx, "eps", [P, 1])
        ident = sb(ctx, "ident", [P, P])
        sign = sb(ctx, "sign", [P, 1])

        w_loaded = [sem(f"w_loaded{s}") for s in range(2)]
        w_split = [sem(f"w_split{s}") for s in range(2)]
        w_hi_done = sem("w_hi_done")
        consts = sem("consts")
        const_loaded = sem("const_loaded")
        block_ends = sem("block_ends")

        def load_pair(sp, n, src0, src1, kt=KD):
            for s, src in enumerate((src0, src1)):
                if not (isinstance(n, int) and n == 0):
                    sp.wait_ge(w_split[s], n)
                sp.dma_start(w_raw[:, s, 0:kt, :], src).then_inc(w_loaded[s], 16)

        def split_pair(dve, n, used, kt=KD, slots=(0, 1), into=(w_hi, w_lo)):
            for s in slots:
                dve.wait_ge(w_loaded[s], 16 * (n + 1))
                if used is not None:
                    dve.wait_ge(*used(s))
                hi, lo = (t[:, s, 0:kt, :] for t in into)
                nc.vector.tensor_copy(hi, w_raw[:, s, 0:kt, :]).then_inc(w_hi_done, 1)
                dve.wait_ge(w_hi_done, 2 * n + s + 1)
                nc.vector.tensor_tensor(lo, w_raw[:, s, 0:kt, :], hi.bitcast(F32), ALU.subtract).then_inc(w_split[s], 1)

        def three_pass(out, pairs, start=True, stop=True):
            last = None
            for n, ((ah, al), (bh, bl)) in enumerate(pairs):
                nc.tensor.matmul(out, ah, bh, start=(start and n == 0), stop=False)
                nc.tensor.matmul(out, ah, bl, start=False, stop=False)
                last = nc.tensor.matmul(out, al, bh, start=False, stop=(stop and n == len(pairs) - 1))
            return last

        def wt(s, k, cols=slice(0, P)):
            return w_hi[:, s, k, cols], w_lo[:, s, k, cols]

        NKV = 4
        x_loaded = [sem(f"x_loaded{i}") for i in range(2)]
        sq_ready, sq_used, root_done, rstd_done = (sem(s) for s in (
            "sq_ready", "sq_used", "root_done", "rstd_done"))
        scaled, hi_done, h_ready = sem("scaled"), sem("hi_done"), sem("h_ready")
        kv_mm, kv_out = sem("kv_mm"), sem("kv_out")
        mm_done, bank_free = sem("mm_done"), sem("bank_free")
        stored = [sem(f"stored{s}") for s in range(2)]

        segments, m = [], 0
        for kind, n, tiles, r in (
            [("copy", 3, lambda i, s: T_U + 2 * i + s, CH)]
            + [("value", 1, (lambda i, s, t=T_V + 2 * g: t + s), DIL[g]) for g in range(3)]
            + [("silu", 3, lambda i, s: T_ZS + 2 * i + s, 1)]
            + [("copy", 1, (lambda i, s, t=t + 2 * g: t + s), DIL[g]) for g in range(3) for t in (T_Q, T_K)]
            + [("silu", 3, lambda i, s: T_ZA + 2 * i + s, 1), ("copy", 2, lambda i, s: T_QM + 2 * i + s, 1),
               ("silu", 2, lambda i, s: T_ZM + 2 * i + s, 1), ("gate", 12, lambda i, s: T_G + 2 * i + s, 1)]
        ):
            segments.append((kind, m, n, tiles, r))
            m += n
        N_MAIN = m
        kind_of = [kind for kind, _, n, _, _ in segments for _ in range(n)]

        NP = 9 + CH
        M_TAB = 6
        par_loaded, tab = sem("par_loaded"), sem("tab")
        dt_done, pow_ready, pow_done, ang_ready, cs_done, cs_ready = (sem(a) for a in (
            "dt_done", "pow_ready", "pow_done", "ang_ready", "cs_done", "cs_ready"))
        ca_ready, ba_ready, k_mm, k_ready, bt_mm, m3_half = (sem(a) for a in (
            "ca_ready", "ba_ready", "k_mm", "k_ready", "bt_mm", "m3_half"))
        ca_kept, k_kept, m3_kept, m8_kept = (sem(a) for a in ("ca_kept", "k_kept", "m3_kept", "m8_kept"))
        k_out = sem("k_out")
        cs_kept = [sem(f"cs_kept{i}") for i in range(2)]

        def unit_of(m, ahead=0):
            u, part = divmod(m - M_TAB + ahead, 2)
            return (u, part) if 0 <= u < NU else (None, part)

        with ExitStack() as ph:
            h_hi = sb(ph, "h_hi", [P, KD, L], F32R)
            h_lo = sb(ph, "h_lo", [P, KD, L], F32R)
            ev = sb(ph, "ev", [P, 2, L])
            with ExitStack() as pn:
                xa = sb(pn, "xa", [P, KD, CW])
                sq = sb(pn, "sq", [P, 4, CW])
                rstd = sb(pn, "rstd", [P, 2, CW])
            par = sb(ph, "par", [P, UG * (3 + 4 * HG)])
            dpar = sb(ph, "dpar", [HG, UG, HG])
            steps = sb(ph, "steps", [P, NC])
            powers = sb(ph, "powers", [P, NP])
            small = {n: sb(ph, f"sm_{n}", [P, UG]) for n in (
                "dt", "ldt", "th", "den", "t0", "t1", "nr", "fr", "sfi", "sph")}
            pw = {n: sb(ph, f"pw_{n}", [P, UG, NP]) for n in (
                "x", "t", "mag", "sin", "cos", "ar", "ai", "sar", "sai", "nai")}
            bb = sb(ph, "bb", [P, UG, HG])
            bbs = sb(ph, "bbs", [P, UG, HG])
            ca = sb(ph, "ca", [P, UG, CH + 1, HG])
            cas = sb(ph, "cas", [P, UG, CH + 1, HG])
            tmp = sb(ph, "tmp", [P, UG, CH + 1, HG])
            ba = sb(ph, "ba", [P, UG, CH, HG])
            bas = sb(ph, "bas", [P, UG, CH, HG])
            m3 = sb(ph, "m3", [P, 2, UG, P])
            kpad = sb(ph, "kpad", [HG, UG, (2 * CH - 1) * HG])
            tx = sb(ph, "tx", [P, 2, NC])
            cs = sb(ph, "cs", [P, 2, 2, NC])
            m8 = sb(ph, "m8", [P, UG])
            ldr, lim, ldt_in = (par[:, UG * i:UG * (i + 1)] for i in range(3))
            bc = [par[:, UG * 3 + UG * HG * i:UG * 3 + UG * HG * (i + 1)].rearrange("p (g h) -> p g h", g=UG)
                  for i in range(4)]
            xb = ev[:, :, :].rearrange("p s (k c) -> p (s k) c", c=CW)
            xbuf = (xa, xb)
            jobs = [(ML, mem_t, slice(0, ML), L - CW, 1)] + [
                (CW, x_t, slice(CW * q, CW * (q + 1)), CW * q, 0) for q in range(NQ)]

            with nc.Block() as block:
                @block.sync
                def _(sp):
                    sp.dma_start(g_in[:, 0, :], norm_g).then_inc(const_loaded, 16)
                    sp.dma_start(g_in[:, 1, :], mem_norm_g).then_inc(const_loaded, 16)
                    sp.dma_start(g_in[:, 2, :], final_g).then_inc(const_loaded, 16)
                    sp.dma_start(bg[:, :], b_gate).then_inc(const_loaded, 16)
                    sp.dma_start(bglu[:, :], b_glu).then_inc(const_loaded, 16)
                    sp.dma_start(ident[:, :], ident_c).then_inc(const_loaded, 16)
                    sp.dma_start(sign[:, :], sign_c).then_inc(const_loaded, 16)
                    for j, (w, src, cols, _, _) in enumerate(jobs):
                        if j >= 2:
                            sp.wait_ge(h_ready, 2 * (j - 1))
                        sp.dma_start(xbuf[j % 2][:, :, 0:w], src[:, :, cols]).then_inc(x_loaded[j % 2], 16)
                        if j < NKV:
                            load_pair(sp, j, w_kv[2 * j], w_kv[2 * j + 1])
                    pairs = [(tiles(i, 0), tiles(i, 1)) for _, _, n, tiles, _ in segments for i in range(n)]
                    for m in range(-2, N_MAIN):
                        if m + 2 < N_MAIN:
                            load_pair(sp, NKV + m + 2, w_in[pairs[m + 2][0]], w_in[pairs[m + 2][1]])
                        if m == M_TAB - 1:
                            sp.wait_ge(h_ready, 2 * len(jobs))
                            sp.dma_start(steps[:, :], steps_c).then_inc(const_loaded, 16)
                            sp.dma_start(powers[:, :], powers_c).then_inc(const_loaded, 16)
                        u, part = unit_of(m, 1)
                        if u is not None and part == 0:
                            if u:
                                sp.wait_ge(k_ready, u)
                            sp.dma_start(par[:, :], ssm_par[u]).then_inc(par_loaded, 16)
                            sp.dma_start(dpar[:, :, :], ssm_d[u]).then_inc(par_loaded, 16)
                        u, part = unit_of(m)
                        if u is not None and part == 1:
                            md = mats_d[u]
                            sp.wait_ge(ca_ready, u + 1)
                            for kind, c in ((2, ca), (3, cas)):
                                sp.dma_start(md[:, :, kind, :].rearrange("p g (j h) -> p g j h", j=CH),
                                             c[:, :, 1:, :]).then_inc(ca_kept, 16)
                            sp.dma_start(m8_d[u], m8[:, :]).then_inc(m8_kept, 16)
                            sp.wait_ge(k_ready, u + 1)
                            for t in range(CH):
                                at = HG * (CH - 1 - t)
                                sp.dma_start(md[HG * t:HG * (t + 1), :, 4, :],
                                             kpad[:, :, at:at + P]).then_inc(k_kept, 16)
                            sp.wait_ge(cs_ready, 2 * u + 1)
                            for g in range(2):
                                sp.dma_start(cs_d[u, :, g, :, :], cs[:, g, :, :]).then_inc(cs_kept[g], 16)
                        u, part = unit_of(m, -2)
                        if u is not None and part == 0:
                            sp.wait_ge(m3_half, 2 * u + 2)
                            sp.wait_ge(cs_ready, 2 * u + 2)
                            for half in range(2):
                                sp.dma_start(mats_d[u][:, :, half, :], m3[:, half, :, :]).then_inc(m3_kept, 16)
                            for g in range(2):
                                sp.dma_start(cs_d[u, :, 2 + g, :, :], cs[:, g, :, :]).then_inc(cs_kept[g], 16)
                    sp.wait_ge(ca_kept, 32 * NU)
                    sp.wait_ge(m8_kept, 16 * NU)
                    sp.wait_ge(k_kept, 16 * CH * NU)
                    sp.wait_ge(m3_kept, 32 * NU)
                    for g in range(2):
                        sp.wait_ge(cs_kept[g], 32 * NU)

                @block.gpsimd
                def _(pool):
                    for kind, m0, n, tiles, r in segments:
                        for i in range(n):
                            for s in range(2):
                                m = m0 + i
                                pool.wait_ge(bank_free, 8 * m + 4 * s + 4)
                                if kind == "value":
                                    dst = v_d[m - segments[1][1], :, L * s:L * (s + 1)]
                                else:
                                    dst = proj_d[tiles(i, s)]
                                pool.dma_start(dst, ev[:, s, :]).then_inc(stored[s], 16)
                    for s in range(2):
                        pool.wait_ge(stored[s], 16 * N_MAIN)

                @block.scalar
                def _(act):
                    act.wait_ge(consts, 2)
                    for j, (w, _, _, at, _) in enumerate(jobs):
                        act.wait_ge(x_loaded[j % 2], 16 * (j // 2 + 1))
                        for k in range(KD):
                            if 8 * j + k >= 4:
                                act.wait_ge(sq_used, 8 * j + k - 3)
                            nc.scalar.activation(sq[:, k % 4, 0:w], xbuf[j % 2][:, k, 0:w],
                                                 ACT.Square).then_inc(sq_ready, 1)
                        act.wait_ge(sq_used, 8 * (j + 1))
                        if j >= 2:
                            act.wait_ge(scaled, 8 * (j - 1))
                        nc.scalar.activation(rstd[:, j % 2, 0:w], psum[2 + j % 2][:, 0:w], ACT.Sqrt,
                                             bias=eps[:, 0:1], scale=1.0 / D).then_inc(root_done, 1)
                        for half in range(2):
                            ks = slice(4 * half, 4 * half + 4)
                            act.wait_ge(scaled, 8 * j + 4 * half + 4)
                            if j == NQ:
                                act.wait_ge(kv_mm, 2 * NKV)
                            nc.scalar.activation(h_hi[:, ks, at:at + w], xbuf[j % 2][:, ks, 0:w],
                                                 ACT.Copy).then_inc(hi_done, 1)
                    def table_window(m, s):
                        u, part = unit_of(m)
                        if u is not None and (part, s) == (0, 0):
                            act.wait_ge(pow_ready, u + 1)
                            nc.scalar.activation(pw["mag"][:, :, :], pw["t"][:, :, :], ACT.Exp).then_inc(pow_done, 1)
                            nc.scalar.activation(pw["sin"][:, :, :], pw["x"][:, :, :], ACT.Sin).then_inc(pow_done, 1)
                            nc.scalar.activation(pw["cos"][:, :, :], pw["x"][:, :, :], ACT.Sin,
                                                 scale=0.5).then_inc(pow_done, 1)
                        if u is not None and part == 1:
                            for g in (2 * s, 2 * s + 1):
                                act.wait_ge(ang_ready, UG * u + g + 1)
                                if 2 * u + s:
                                    act.wait_ge(cs_kept[g % 2], 16 * (2 * u + s))
                                nc.scalar.activation(cs[:, g % 2, 1, :], tx[:, g % 2, :], ACT.Sin).then_inc(cs_done, 1)
                                nc.scalar.activation(cs[:, g % 2, 0, :], tx[:, g % 2, :], ACT.Sin,
                                                     scale=0.5).then_inc(cs_done, 1)
                        u, part = unit_of(m, 1)
                        if u is not None and (part, s) == (0, 1):
                            act.wait_ge(par_loaded, 32 * (u + 1))
                            nc.scalar.activation(small["dt"][:, :], ldt_in, ACT.Exp).then_inc(dt_done, 1)

                    for n in range(NKV):
                        for s in range(2):
                            act.wait_ge(kv_mm, 2 * n + s + 1)
                            src = psum[4 + n][:, ML * s:ML * (s + 1)]
                            dst = k_mem[:, 2 * n + s, :] if n < 2 else v_mem[:, s, 256 * (n - 2):256 * (n - 1)]
                            nc.scalar.activation(dst, src, ACT.Copy).then_inc(kv_out, 1)
                    for kind, m0, n, tiles, r in segments:
                        for i in range(n):
                            m = m0 + i
                            for s in range(2):
                                if m == 0:
                                    act.wait_ge(h_ready, 2 * len(jobs))
                                else:
                                    act.wait_ge(stored[s], 16 * m)
                                for c in range(NQ):
                                    act.wait_ge(mm_done, 8 * m + 4 * s + c + 1)
                                    src = psum[4 * s + c][:, :]
                                    dst = ev[:, s, CW * c:CW * (c + 1)]
                                    if r > 1 and kind != "value":
                                        src = src.rearrange("p (m r) -> p r m", r=r)
                                        dst = ev[:, s, :].rearrange("p (r m) -> p r m", r=r)[
                                            :, :, CW // r * c:CW // r * (c + 1)]
                                    if kind == "silu":
                                        ins = nc.scalar.activation(dst, src, ACT.Silu)
                                    elif kind == "gate":
                                        t = tiles(i, s) - T_G
                                        ins = nc.scalar.activation(dst, src, ACT.Sigmoid, bias=bg[:, t:t + 1])
                                    else:
                                        ins = nc.scalar.activation(dst, src, ACT.Copy)
                                    ins.then_inc(bank_free, 1)
                                table_window(m, s)

                @block.vector
                def _(dve):
                    nc.vector.memset(ones[:, :], 1.0).then_inc(consts, 1)
                    nc.vector.memset(eps[:, :], EPS).then_inc(consts, 1)
                    dve.wait_ge(const_loaded, 112)
                    for j, (w, _, _, at, gi) in enumerate(jobs):
                        dve.wait_ge(root_done, j + 1)
                        r = rstd[:, j % 2, 0:w]
                        nc.vector.reciprocal(r, r).then_inc(rstd_done, 1)
                        dve.wait_ge(rstd_done, j + 1)
                        x = xbuf[j % 2]
                        for k in range(KD):
                            nc.vector.scalar_tensor_tensor(x[:, k, 0:w], x[:, k, 0:w], g_in[:, gi, k:k + 1], r,
                                                           ALU.mult, ALU.mult).then_inc(scaled, 1)
                        for half in range(2):
                            ks = slice(4 * half, 4 * half + 4)
                            dve.wait_ge(hi_done, 2 * j + half + 1)
                            nc.vector.tensor_tensor(h_lo[:, ks, at:at + w], x[:, ks, 0:w],
                                                    h_hi[:, ks, at:at + w].bitcast(F32),
                                                    ALU.subtract).then_inc(h_ready, 1)
                        if j < NKV:
                            split_pair(dve, j, None if j == 0 else
                                       lambda s: (kv_mm, 2 * j - 1 + s if j < 3 else 2 * j))
                    steps_done = [0]

                    def link(ins):
                        steps_done[0] += 1
                        ins.then_inc(tab, 1)
                        dve.wait_ge(tab, steps_done[0])

                    def tt(out, a, b, op):
                        link(nc.vector.tensor_tensor(out, a, b, op))

                    def ts(out, a, s1, s2, op0, op1=None):
                        if op1 is None:
                            link(nc.vector.tensor_scalar(out, a, s1, None, op0))
                        else:
                            link(nc.vector.tensor_scalar(out, a, s1, s2, op0, op1))

                    def reduce_angle(x, t):
                        ts(t, x, 1 / (2 * math.pi), MAGIC, ALU.mult, ALU.add)
                        ts(t, t, MAGIC, None, ALU.subtract)
                        link(nc.vector.scalar_tensor_tensor(x, t, -TWO_PI_HI, x, ALU.mult, ALU.add))
                        link(nc.vector.scalar_tensor_tensor(x, t, -TWO_PI_LO, x, ALU.mult, ALU.add))

                    def clip(x):
                        return nc.vector.tensor_scalar(x, x, PI_SAFE, -PI_SAFE, ALU.min, ALU.max)

                    def combine(out, tm, p1, a1, p2, a2, op):
                        tt(out, p1, a1, ALU.mult)
                        tt(tm, p2, a2, ALU.mult)
                        return nc.vector.tensor_tensor(out, out, tm, op)

                    s_ = {n: a[:, :] for n, a in small.items()}
                    w_ = {n: a[:, :, :] for n, a in pw.items()}

                    def powers_of(u):
                        s, w = s_, w_
                        dve.wait_ge(par_loaded, 32 * (u + 1))
                        dve.wait_ge(dt_done, u + 1)
                        tt(s["ldt"], ldr, s["dt"], ALU.mult)
                        tt(s["th"], lim, s["dt"], ALU.mult)
                        reduce_angle(s["th"], s["t0"])
                        shape = (P, UG, NP)
                        pj = powers[:, :].unsqueeze(1).to_broadcast(shape)
                        tt(w["x"], s["th"].unsqueeze(2).to_broadcast(shape), pj, ALU.mult)
                        reduce_angle(w["x"], w["t"])
                        link(clip(w["x"]))
                        nc.vector.tensor_tensor(w["t"], s["ldt"].unsqueeze(2).to_broadcast(shape), pj,
                                                ALU.mult).then_inc(pow_ready, 1)

                    def matrices(u):
                        s, w = s_, w_
                        dve.wait_ge(pow_done, 3 * (u + 1))
                        tt(w["cos"], w["cos"], w["cos"], ALU.mult)
                        ts(w["cos"], w["cos"], -2.0, 1.0, ALU.mult, ALU.add)
                        tt(w["ar"], w["mag"], w["cos"], ALU.mult)
                        tt(w["ai"], w["mag"], w["sin"], ALU.mult)
                        ts(w["sar"], w["ar"], sign[:, 0:1], None, ALU.mult)
                        ts(w["sai"], w["ai"], sign[:, 0:1], None, ALU.mult)
                        ts(w["nai"], w["ai"], -1.0, None, ALU.mult)
                        if u:
                            dve.wait_ge(m8_kept, 16 * u)
                        link(nc.vector.tensor_copy(m8[:, :], pw["mag"][:, :, CH]))
                        ar1, ai1 = pw["ar"][:, :, 1], pw["ai"][:, :, 1]
                        tt(s["den"], ldr, ldr, ALU.mult)
                        tt(s["t0"], lim, lim, ALU.mult)
                        tt(s["den"], s["den"], s["t0"], ALU.add)
                        link(nc.vector.reciprocal(s["den"], s["den"]))
                        ts(s["nr"], ar1, -1.0, None, ALU.add)
                        tt(s["t0"], s["nr"], ldr, ALU.mult)
                        tt(s["t1"], ai1, lim, ALU.mult)
                        tt(s["t0"], s["t0"], s["t1"], ALU.add)
                        tt(s["fr"], s["t0"], s["den"], ALU.mult)
                        tt(s["t0"], ai1, ldr, ALU.mult)
                        tt(s["t1"], s["nr"], lim, ALU.mult)
                        tt(s["t0"], s["t0"], s["t1"], ALU.subtract)
                        tt(s["t0"], s["t0"], s["den"], ALU.mult)
                        ts(s["sfi"], s["t0"], sign[:, 0:1], None, ALU.mult)
                        ts(s["sph"], pw["x"][:, :, CH], sign[:, 0:1], None, ALU.mult)
                        sh = (P, UG, HG)
                        fr, sfi = (s[a].unsqueeze(2).to_broadcast(sh) for a in ("fr", "sfi"))
                        t3 = tmp[:, :, 0, :]
                        link(combine(bb[:, :, :], t3, fr, bc[2], sfi, bc[3], ALU.subtract))
                        link(combine(bbs[:, :, :], t3, fr, bc[3], sfi, bc[2], ALU.add))
                        if u:
                            dve.wait_ge(ca_kept, 32 * u)
                        sh = (P, UG, CH + 1, HG)
                        cv = [a.unsqueeze(2).to_broadcast(sh) for a in bc[0:2]]
                        pf = {a: pw[a][:, :, 0:CH + 1].unsqueeze(3).to_broadcast(sh) for a in ("sar", "nai")}
                        link(combine(cas[:, :, :, :], tmp[:, :, :, :], pf["nai"], cv[0], pf["sar"], cv[1],
                                     ALU.subtract))
                        combine(ca[:, :, :, :], tmp[:, :, :, :], pf["sar"], cv[0], pf["nai"], cv[1],
                                ALU.add).then_inc(ca_ready, 1)

                    def transposable(u):
                        dve.wait_ge(ca_ready, u + 1)
                        if u:
                            dve.wait_ge(bt_mm, 2 * u)
                        sh = (P, UG, CH, HG)
                        bv = [a[:, :, :].unsqueeze(2).to_broadcast(sh) for a in (bb, bbs)]
                        pf = {a: pw[a][:, :, CH + 1:NP].unsqueeze(3).to_broadcast(sh) for a in ("ar", "sai")}
                        tm = tmp[:, :, 0:CH, :]
                        link(combine(ba[:, :, :, :], tm, pf["ar"], bv[0], pf["sai"], bv[1], ALU.subtract))
                        combine(bas[:, :, :, :], tm, pf["ar"], bv[1], pf["sai"], bv[0],
                                ALU.add).then_inc(ba_ready, 1)

                    def angles(u, half):
                        for g in (2 * half, 2 * half + 1):
                            x = tx[:, g % 2, :]
                            if u or half:
                                dve.wait_ge(cs_done, 2 * (UG * u + g - 1))
                            ts(x, steps[:, :], small["sph"][:, g:g + 1], None, ALU.mult)
                            reduce_angle(x, tmp[:, :, :, :].rearrange("p g j h -> p (g j h)")[:, 0:NC])
                            clip(x).then_inc(ang_ready, 1)

                    def cosines(u, half):
                        dve.wait_ge(cs_done, 2 * (UG * u + 2 * half + 2))
                        c = cs[:, :, 0, :]
                        tt(c, c, c, ALU.mult)
                        nc.vector.tensor_scalar(c, c, -2.0, 1.0, ALU.mult, ALU.add).then_inc(cs_ready, 1)

                    def response(u):
                        dve.wait_ge(k_mm, u + 1)
                        if u:
                            dve.wait_ge(k_kept, 16 * CH * u)
                        kp = kpad[:, :, (CH - 1) * HG:]
                        idb = ident[0:HG, 0:HG].unsqueeze(1).to_broadcast((HG, UG, HG))
                        tt(dpar[:, :, :], dpar[:, :, :], idb, ALU.mult)
                        nc.vector.tensor_copy(kp, psum[7][0:HG, :].rearrange("p (g c) -> p g c", g=UG)).then_inc(k_out, 1)
                        dve.wait_ge(k_out, u + 1)
                        nc.vector.tensor_tensor(kp[:, :, 0:HG], kp[:, :, 0:HG], dpar[:, :, :], ALU.add).then_inc(k_ready, 1)

                    def turned_inputs(u):
                        if u:
                            dve.wait_ge(m3_kept, 32 * u)
                        for half in range(2):
                            dve.wait_ge(bt_mm, 2 * u + half + 1)
                            nc.vector.tensor_copy(m3[:, half, :, :].rearrange("p g c -> p (g c)"),
                                                  psum[6 + half][:, :]).then_inc(m3_half, 1)
                        dve.wait_ge(m3_half, 2 * u + 2)

                    def table_window(m, slot):
                        u, part = unit_of(m, -2)
                        if u is not None and (part, slot) == (0, 0):
                            turned_inputs(u)
                            cosines(u, 1)
                        u, part = unit_of(m)
                        if u is None:
                            return
                        if (part, slot) == (0, 0):
                            powers_of(u)
                        elif (part, slot) == (0, 1):
                            matrices(u)
                        elif (part, slot) == (1, 0):
                            response(u)
                            transposable(u)
                            angles(u, 0)
                        else:
                            cosines(u, 0)
                            angles(u, 1)

                    for s in range(2):
                        split_pair(dve, NKV, lambda s: (kv_mm, 2 * NKV), slots=(s,))
                    for m in range(N_MAIN):
                        if m == M_TAB:
                            nc.vector.memset(kpad[:, :, :], 0.0).then_inc(tab, 1)
                            steps_done[0] += 1
                            dve.wait_ge(tab, steps_done[0])
                            dve.wait_ge(const_loaded, 16 * 9)
                        for s in range(2):
                            if m + 1 < N_MAIN:
                                done = 8 * m + 8 if kind_of[m] == "value" else 8 * m + 4 * s + 4
                                split_pair(dve, NKV + m + 1, lambda s: (mm_done, done), slots=(s,))
                            table_window(m, s)

                @block.tensor
                def _(pe):
                    pe.wait_ge(consts, 2)

                    def sum_squares(j):
                        w = jobs[j][0]
                        if j >= 2:
                            pe.wait_ge(root_done, j - 1)
                        for k in range(KD):
                            pe.wait_ge(sq_ready, 8 * j + k + 1)
                            mm = nc.tensor.matmul(psum[2 + j % 2][:, 0:w], ones[:, :], sq[:, k % 4, 0:w],
                                                  start=(k == 0), stop=(k == KD - 1)).then_inc(sq_used, 1)

                    def memory_kv(n):
                        for s in range(2):
                            pe.wait_ge(w_split[s], n + 1)
                        mcol = L - CW
                        for s in range(2):
                            if n < 2:
                                pairs = [(wt(s, k), (h_hi[:, k, mcol:mcol + ML], h_lo[:, k, mcol:mcol + ML]))
                                         for k in range(KD)]
                                out = psum[4 + n][:, ML * s:ML * (s + 1)]
                            else:
                                tok = slice(mcol + P * s, mcol + P * (s + 1))
                                pairs = [((h_hi[:, k, tok], h_lo[:, k, tok]), (w_hi[:, :, k, :], w_lo[:, :, k, :]))
                                         for k in range(KD)]
                                out = psum[4 + n][:, ML * s:ML * (s + 1)].rearrange("p (a b) -> p a b", a=2)
                            three_pass(out, pairs).then_inc(kv_mm, 1)

                    def table_window(m, s):
                        if s == 0:
                            return
                        u, part = unit_of(m)
                        if u is not None and part == 1:
                            pe.wait_ge(ca_ready, u + 1)
                            pe.wait_ge(bank_free, 8 * m)
                            for g in range(UG):
                                mm = nc.tensor.matmul(psum[7][0:HG, P * g:P * (g + 1)], bb[:, g, :],
                                                      ca[:, g, 0:CH, :], start=True, stop=True)
                            mm.then_inc(k_mm, 1)
                        u, part = unit_of(m, -2)
                        if u is not None and part == 0:
                            pe.wait_ge(ba_ready, u + 1)
                            pe.wait_ge(bank_free, 8 * m)
                            for half, b in ((0, ba), (1, bas)):
                                for g in range(UG):
                                    mm = nc.tensor.transpose(psum[6 + half][:, P * g:P * (g + 1)],
                                                             b[:, g, :, :].rearrange("p s h -> p (s h)"), ident[:, :])
                                mm.then_inc(bt_mm, 1)

                    def table_banks_free(m):
                        u, part = unit_of(m)
                        if u is not None and part == 1:
                            pe.wait_ge(k_out, u + 1)
                        u, part = unit_of(m, -2)
                        if u is not None and part == 0:
                            pe.wait_ge(m3_half, 2 * u + 2)

                    sum_squares(0)
                    sum_squares(1)
                    pe.wait_ge(h_ready, 2)
                    memory_kv(0)
                    sum_squares(2)
                    memory_kv(1)
                    sum_squares(3)
                    memory_kv(2)
                    memory_kv(3)
                    sum_squares(4)
                    for kind, m0, n, tiles, r in segments:
                        for i in range(n):
                            m = m0 + i
                            for s in range(2):
                                table_window(m, s)
                                pe.wait_ge(w_split[s], NKV + m + 1)
                                if kind == "value":
                                    pe.wait_ge(w_split[1], NKV + m + 1)
                                for c in range(NQ):
                                    if m == 0:
                                        pe.wait_ge(h_ready, 2 * (c + 2))
                                        if s == 0 and c in (2, 3):
                                            pe.wait_ge(root_done, len(jobs))
                                        if s == 1:
                                            pe.wait_ge(kv_out, 2 * NKV)
                                    else:
                                        pe.wait_ge(bank_free, 8 * (m - 1) + 4 * s + c + 1)
                                        if s == 1 and c == 2:
                                            table_banks_free(m)
                                    bank = psum[4 * s + c]
                                    if kind != "value":
                                        cols = slice(CW * c, CW * (c + 1))
                                        mm = three_pass(bank[:, :], [(wt(s, k), (h_hi[:, k, cols], h_lo[:, k, cols]))
                                                                     for k in range(KD)])
                                        mm.then_inc(mm_done, 1)
                                        continue
                                    for half in range(2):
                                        b = 2 * (4 * s + c) + half
                                        res, blk = divmod(b, NBLK // r)
                                        first = res + r * P * blk
                                        tok = slice(first, first + r * (P - 1) + 1, r)
                                        out = bank[:, 256 * half:256 * (half + 1)].rearrange(
                                            "p (a b) -> p a b", a=2)
                                        mm = three_pass(out, [((h_hi[:, k, tok], h_lo[:, k, tok]),
                                                               (w_hi[:, :, k, :], w_lo[:, :, k, :]))
                                                              for k in range(KD)])
                                    mm.then_inc(mm_done, 1)

        mats_loaded = [sem(f"mats_loaded{i}") for i in range(2)]
        v_mm, turned, w_sum, scanned, state_done, y_mm, y_out_done = (sem(a) for a in (
            "v_mm", "turned", "w_sum", "scanned", "state_done", "y_mm", "y_out_done"))
        ys_stored = [sem(f"ys_stored{i}") for i in range(2)]
        BLOADS = 2 * 3 + CH
        with ExitStack() as ph:
            mats = sb(ph, "mats", [P, 2, GB, 5, P])
            csb = sb(ph, "csb", [P, 2, GB, 2, NC])
            m8b = sb(ph, "m8b", [P, 2, GB])
            ub = sb(ph, "ub", [P, 2, GB, NC])
            yb = sb(ph, "yb", [P, 2, GB, NC])
            tv = sb(ph, "tv", [P, 4, 2, NC])
            wv = sb(ph, "wv", [P, 4, NC])
            zv = sb(ph, "zv", [P, 4, NC])
            xz = sb(ph, "xz", [P, 4, 2, NC])
            R = 4

            with nc.Block() as block:
                @block.sync
                def _(sp):
                    for b in range(NB):
                        i = b % 2
                        if b >= 2:
                            sp.wait_ge(y_mm, GB * (b - 1))
                        for part in range(2):
                            gs = slice(UG * part, UG * (part + 1))
                            sp.dma_start(mats[:, i, gs, :, :], mats_d[2 * b + part]).then_inc(mats_loaded[i], 16)
                            sp.dma_start(csb[:, i, gs, :, :], cs_d[2 * b + part]).then_inc(mats_loaded[i], 16)
                            sp.dma_start(m8b[:, i, gs], m8_d[2 * b + part]).then_inc(mats_loaded[i], 16)
                        src = proj_d[T_U + b].rearrange("(g h) (s c) -> s h g c", g=GB, s=CH)
                        for t in range(CH):
                            sp.dma_start(ub[HG * t:HG * (t + 1), i, :, :], src[t]).then_inc(mats_loaded[i], 16)

                @block.gpsimd
                def _(pool):
                    for q in range(G):
                        pool.wait_ge(turned, q + 1)
                        if q >= R:
                            pool.wait_ge(scanned, q - R + 1)
                        nc.gpsimd.tensor_tensor(wv[:, q % R, :], tv[:, q % R, 0, :], tv[:, q % R, 1, :],
                                                ALU.add).then_inc(w_sum, 1)

                @block.vector
                def _(dve):
                    for q in range(G + 2):
                        if q < G:
                            if q % GB == 0:
                                b = q // GB
                                dve.wait_ge(mats_loaded[b % 2], 16 * BLOADS * (b // 2 + 1))
                            dve.wait_ge(v_mm, q + 1)
                            if q >= R:
                                dve.wait_ge(w_sum, q - R + 1)
                            nc.vector.tensor_tensor(tv[:, q % R, :, :],
                                                    psum[q % 4][:, :].rearrange("p (a c) -> p a c", a=2),
                                                    csb[:, q // GB % 2, q % GB, :, :], ALU.mult).then_inc(turned, 1)
                        if q >= 2:
                            g = q - 2
                            dve.wait_ge(w_sum, g + 1)
                            if g >= R:
                                dve.wait_ge(state_done, g - R + 1)
                            m = m8b[:, g // GB % 2, g % GB:g % GB + 1].to_broadcast((P, NC))
                            nc.vector.tensor_tensor_scan(zv[:, g % R, :], m, wv[:, g % R, :], 0.0,
                                                         ALU.mult, ALU.add).then_inc(scanned, 1)
                            dve.wait_ge(scanned, g + 1)
                            if g >= R:
                                dve.wait_ge(y_mm, g - R + 1)
                            z = zv[:, g % R, :].unsqueeze(1).to_broadcast((P, 2, NC))
                            nc.vector.tensor_tensor(xz[:, g % R, :, :], csb[:, g // GB % 2, g % GB, :, :], z,
                                                    ALU.mult).then_inc(state_done, 1)

                @block.tensor
                def _(pe):
                    LAG = 3
                    for q in range(G + LAG):
                        if q < G:
                            b, g = divmod(q, GB)
                            if g == 0:
                                pe.wait_ge(mats_loaded[b % 2], 16 * BLOADS * (b // 2 + 1))
                            if q >= R:
                                pe.wait_ge(turned, q - R + 1)
                            for half in range(2):
                                mm = nc.tensor.matmul(psum[q % 4][:, NC * half:NC * (half + 1)],
                                                      mats[:, b % 2, g, half, :], ub[:, b % 2, g, :],
                                                      start=True, stop=True)
                            mm.then_inc(v_mm, 1)
                        if q >= LAG:
                            q2 = q - LAG
                            b, g = divmod(q2, GB)
                            if q2 >= R:
                                pe.wait_ge(y_out_done, q2 - R + 1)
                            y = psum[4 + q2 % 4]
                            nc.tensor.matmul(y[:, 0:NC], mats[:, b % 2, g, 4, :], ub[:, b % 2, g, :],
                                             start=True, stop=False)
                            pe.wait_ge(state_done, q2 + 1)
                            for part in range(2):
                                mm = nc.tensor.matmul(y[:, 1:NC], mats[:, b % 2, g, 2 + part, :],
                                                      xz[:, q2 % R, part, 0:NC - 1], start=False, stop=(part == 1))
                            mm.then_inc(y_mm, 1)

                @block.scalar
                def _(act):
                    for b in range(NB):
                        for g in range(GB):
                            q = GB * b + g
                            act.wait_ge(y_mm, q + 1)
                            if g == 0 and b >= 2:
                                act.wait_ge(ys_stored[b % 2], 16 * CH * (b // 2))
                            nc.scalar.activation(yb[:, b % 2, g, :], psum[4 + q % 4][:, 0:NC],
                                                 ACT.Gelu_apprx_tanh).then_inc(y_out_done, 1)
                        act.wait_ge(y_out_done, GB * (b + 1))
                        dst = ys_d[b].rearrange("(g h) (s c) -> s h g c", g=GB, s=CH)
                        for t in range(CH):
                            act.dma_start(dst[t], yb[HG * t:HG * (t + 1), b % 2, :, :]).then_inc(ys_stored[b % 2], 16)
                    for i in range(2):
                        act.wait_ge(ys_stored[i], 16 * CH * (NB // 2))

        SCALE = HD ** -0.5
        batches = []
        for h in range(NH):
            g = h // HPG
            per = 4 if g == 2 else 2
            for b in range(0, NBLK, per):
                batches.append((h, g, list(range(b, b + per)), 512 // per))
        NT_B = len(batches)
        qk_loaded = [sem(f"qk_loaded{i}") for i in range(2)]
        vg_loaded = [sem(f"vg_loaded{i}") for i in range(2)]
        bias_in, bias_rows, bias_neg, bias_kept, bias_loaded = (sem(a) for a in (
            "bias_in", "bias_rows", "bias_neg", "bias_kept", "bias_loaded"))
        s_mm, s_biased, s_min, e_done, t_mm, t_out, o_mm, o_out = (sem(a) for a in (
            "s_mm", "s_biased", "s_min", "e_done", "t_mm", "t_out", "o_mm", "o_out"))
        st_mm, st_out, st_kept = sem("st_mm"), sem("st_out"), sem("st_kept")
        first_mask, bias_turned, bias_kept2 = sem("first_mask"), sem("bias_turned"), sem("bias_kept2")

        with ExitStack() as ph:
            oT = sb(ph, "oT", [P, NH // 2, L])
            qk = sb(ph, "qk", [P, 2, 2, L])
            with ExitStack() as pa:
                vg = sb(pa, "vg", [P, 2, NBLK, HPG * HD])
                bias = sb(pa, "bias", [P, NH, 2, 256])
                bk = sb(pa, "bk", [NBUCKET + 1, 3, 384])
                rel = sb(pa, "rel", [NBUCKET + 1, NH])
                brow = sb(pa, "brow", [NH, 3, 384])
                tsc = sb(pa, "tsc", [P, 3, 512])
                esc = sb(pa, "esc", [P, 3, 512])
                ptr = sb(pa, "ptr", [P, 3, 512])
                stat = sb(pa, "stat", [P, 2, NH * NBLK])
                strow = sb(pa, "strow", [P, 4, P])
                anti = sb(pa, "anti", [P, P])

                mirrored = vg[:, 1, 0:NH, :]

                def has_prev(g, b):
                    return b % (NBLK // DIL[g]) != 0

                with nc.Block() as block:
                    @block.sync
                    def _(sp):
                        sp.dma_start(bk[:, :, :], buckets).then_inc(bias_in, 16)
                        sp.dma_start(rel[0:NBUCKET, :], rel_bias).then_inc(bias_in, 16)
                        sp.dma_start(anti[:, :], anti_c).then_inc(bias_in, 16)
                        for pair in range(2):
                            for a, t in enumerate((T_Q, T_K)):
                                sp.dma_start(qk[:, pair, a, :], proj_d[t + pair]).then_inc(qk_loaded[pair], 16)
                        sp.dma_start(vg[:, 0, :, :].rearrange("p b c -> p (b c)"), v_d[0]).then_inc(vg_loaded[0], 16)
                        sp.wait_ge(bias_neg, 3)
                        for g in range(3):
                            sp.dma_start(bias_d[g], brow[:, g, :]).then_inc(bias_kept, 16)
                        sp.wait_ge(bias_kept, 48)
                        for h in range(NH):
                            row = bias_d[h // HPG, h]
                            src = bass.AP(row.tensor, row.offset, [[1, P], [1, 256]])
                            sp.dma_start(mirrored[:, h, :], src).then_inc(bias_loaded, 16)
                        sp.wait_ge(bias_turned, NH // 2)
                        sp.dma_start(vg[:, 1, :, :].rearrange("p b c -> p (b c)"), v_d[1]).then_inc(vg_loaded[1], 16)
                        for pair in range(2, NH // 2):
                            n = sum(1 for b in batches if b[0] < 2 * (pair - 1))
                            sp.wait_ge(s_mm, n)
                            for a, t in enumerate((T_Q, T_K)):
                                sp.dma_start(qk[:, pair % 2, a, :], proj_d[t + pair]).then_inc(
                                    qk_loaded[pair % 2], 16)
                            if pair == 4:
                                sp.wait_ge(o_mm, HPG * NBLK // 2)
                                sp.dma_start(vg[:, 0, :, :].rearrange("p b c -> p (b c)"), v_d[2]).then_inc(
                                    vg_loaded[0], 16)
                        sp.wait_ge(st_out, 1)
                        for w in range(2):
                            sp.dma_start(st_d[w, 0:P, :], strow[:, 2 * w, :]).then_inc(st_kept, 16)
                            sp.dma_start(st_d[w, P:NH * NBLK, :], strow[0:NH * NBLK - P, 2 * w + 1, :]).then_inc(
                                st_kept, 16)
                        sp.wait_ge(st_kept, 64)

                    @block.gpsimd
                    def _(pool):
                        nc.gpsimd.memset(rel[NBUCKET:NBUCKET + 1, :], 1.0).then_inc(first_mask, 1)
                        pool.wait_ge(first_mask, 1)
                        nc.gpsimd.memset(bias[:, :, 0, 0:128], BIG).then_inc(first_mask, 1)

                    @block.tensor
                    def _(pe):
                        pe.wait_ge(bias_in, 48)
                        pe.wait_ge(first_mask, 1)
                        for g in range(3):
                            nc.tensor.matmul(psum[g][0:NH, 0:384], rel[:, :], bk[:, g, :], start=True,
                                             stop=True).then_inc(bias_rows, 1)

                        pe.wait_ge(bias_loaded, 16 * NH)
                        for n in range(NH // 2):
                            nc.tensor.matmul(psum[2 + n][:, :].rearrange("p (a k) -> p a k", a=2), anti[:, :],
                                             mirrored[:, 2 * n:2 * n + 2, :], start=True, stop=True).then_inc(
                                                 bias_turned, 1)

                        def scores(t):
                            h, g, blocks, nk = batches[t]
                            pair, half = divmod(h, 2)
                            rows = slice(64 * half, 64 * half + 64)
                            pe.wait_ge(qk_loaded[pair % 2], 32 * (pair // 2 + 1))
                            if t < 2:
                                pe.wait_ge(bias_neg, 3)
                            else:
                                pe.wait_ge(s_biased, t - 1)
                            q, k = qk[rows, pair % 2, 0, :], qk[rows, pair % 2, 1, :]
                            for i, b in enumerate(blocks):
                                lhs = q[:, P * b:P * (b + 1)]
                                out = psum[t % 2][:, nk * i:nk * (i + 1)]
                                if nk == 128 or has_prev(g, b):
                                    mm = nc.tensor.matmul(out, lhs, k[:, P * (b + 1) - nk:P * (b + 1)],
                                                          start=True, stop=True)
                                else:
                                    for part in range(2):
                                        mm = nc.tensor.matmul(out[:, P * part:P * (part + 1)], lhs,
                                                              k[:, P * b:P * (b + 1)], start=True, stop=True)
                            mm.then_inc(s_mm, 1)

                        def turn(t):
                            pe.wait_ge(e_done, sum(len(b[2]) for b in batches[:t + 1]))
                            if t >= 2:
                                pe.wait_ge(t_out, t - 1)
                            else:
                                pe.wait_ge(bias_kept2, NH // 2)
                            for i in range(4):
                                mm = nc.tensor.transpose(psum[2 + t % 2][:, P * i:P * (i + 1)],
                                                         esc[:, t % 3, P * i:P * (i + 1)], ident[:, :])
                            mm.then_inc(t_mm, 1)

                        def output(t):
                            h, g, blocks, nk = batches[t]
                            rows = slice(64 * (h % 2), 64 * (h % 2) + 64)
                            pe.wait_ge(vg_loaded[g % 2], 16 * (g // 2 + 1))
                            pe.wait_ge(t_out, t + 1)
                            bank = (h * NBLK + blocks[0]) // 4
                            if blocks[0] % 4 == 0 and bank >= 4:
                                pe.wait_ge(o_out, bank - 3)
                            for i, b in enumerate(blocks):
                                out = psum[4 + bank % 4][rows, P * (b % 4):P * (b % 4 + 1)]
                                parts = [1] if nk == 256 else [0]
                                if nk == 256 and has_prev(g, b):
                                    parts = [0, 1]
                                for part in parts:
                                    kb = b - 1 + part if nk == 256 else b
                                    e = ptr[:, t % 3, nk * i + P * part:nk * i + P * (part + 1)]
                                    mm = nc.tensor.matmul(out, vg[:, g % 2, kb, HD * (h % HPG):HD * (h % HPG + 1)], e,
                                                          start=(part == parts[0]), stop=(part == parts[-1]))
                            mm.then_inc(o_mm, 1)

                        for t in range(NT_B + 4):
                            if t < NT_B:
                                scores(t)
                            if 0 <= t - 2 < NT_B:
                                turn(t - 2)
                            if 0 <= t - 3 < NT_B:
                                output(t - 3)
                        pe.wait_ge(o_out, NH * NBLK // 4)
                        for w in range(2):
                            nc.tensor.transpose(psum[0][:, 2 * w * P:(2 * w + 1) * P], stat[:, w, 0:P], ident[:, :])
                            mm = nc.tensor.transpose(psum[0][0:NH * NBLK - P, (2 * w + 1) * P:(2 * w + 2) * P],
                                                     stat[:, w, P:NH * NBLK], ident[:, :])
                        mm.then_inc(st_mm, 1)

                    @block.vector
                    def _(dve):
                        for g in range(3):
                            dve.wait_ge(bias_rows, g + 1)
                            nc.vector.tensor_scalar(brow[:, g, :], psum[g][0:NH, 0:384], -1.0, None,
                                                    ALU.mult).then_inc(bias_neg, 1)

                        def negate_and_min(t):
                            h, g, blocks, nk = batches[t]
                            n = len(blocks)
                            dve.wait_ge(s_mm, t + 1)
                            if t >= 3:
                                dve.wait_ge(e_done, sum(len(b[2]) for b in batches[:t - 2]))
                            out = tsc[:, t % 3, :].rearrange("p (n k) -> p n k", n=n)
                            sc = psum[t % 2][:, :].rearrange("p (n k) -> p n k", n=n)
                            if nk == 128:
                                bi = bias[:, h, 1, 128:256].unsqueeze(1).to_broadcast((P, n, nk))
                            elif has_prev(g, blocks[0]):
                                bi = bias[:, h, 1, :].unsqueeze(1).to_broadcast((P, n, nk))
                            else:
                                bi = bias[:, h, :, :]
                            nc.vector.scalar_tensor_tensor(out, sc, -SCALE, bi, ALU.mult,
                                                           ALU.add).then_inc(s_biased, 1)
                            dve.wait_ge(s_biased, t + 1)
                            at = h * NBLK + blocks[0]
                            nc.vector.tensor_reduce(stat[:, 0, at:at + n], out, AX.X, ALU.min).then_inc(s_min, 1)

                        def keep_turned(t):
                            dve.wait_ge(t_mm, t + 1)
                            if t >= 3:
                                dve.wait_ge(o_mm, t - 2)
                            nc.vector.tensor_copy(ptr[:, t % 3, :], psum[2 + t % 2][:, :]).then_inc(t_out, 1)

                        for n in range(NH // 2):
                            dve.wait_ge(bias_turned, n + 1)
                            src = psum[2 + n][:, :].rearrange("p (a k) -> p a k", a=2)
                            nc.vector.tensor_copy(bias[:, 2 * n:2 * n + 2, 1, :], src).then_inc(bias_kept2, 1)
                        dve.wait_ge(bias_kept2, NH // 2)
                        nc.vector.tensor_copy(bias[:, :, 0, P:2 * P], bias[:, :, 1, P:2 * P]).then_inc(bias_kept2, 1)
                        dve.wait_ge(bias_kept2, NH // 2 + 1)
                        dve.wait_ge(first_mask, 2)
                        for t in range(NT_B + 2):
                            if t < NT_B:
                                negate_and_min(t)
                            if t >= 2:
                                keep_turned(t - 2)
                        dve.wait_ge(st_mm, 1)
                        nc.vector.tensor_copy(strow[:, :, :].rearrange("p a b -> p (a b)"),
                                              psum[0][:, :]).then_inc(st_out, 1)

                    @block.scalar
                    def _(act):
                        def exponentials(t):
                            h, g, blocks, nk = batches[t]
                            act.wait_ge(s_min, t + 1)
                            if t >= 3:
                                act.wait_ge(t_mm, t - 2)
                            for i, b in enumerate(blocks):
                                at = h * NBLK + b
                                nc.scalar.activation(esc[:, t % 3, nk * i:nk * (i + 1)],
                                                     tsc[:, t % 3, nk * i:nk * (i + 1)], ACT.Exp,
                                                     bias=stat[:, 0, at:at + 1], scale=-1.0,
                                                     accum_out=stat[:, 1, at:at + 1]).then_inc(e_done, 1)

                        def keep_output(bank, batch):
                            h, b4 = divmod(bank, NBLK // 4)
                            g, r = h // HPG, DIL[h // HPG]
                            rows = slice(64 * (h % 2), 64 * (h % 2) + 64)
                            act.wait_ge(o_mm, batch + 1)
                            src = psum[4 + bank % 4][rows, :]
                            dst = oT[rows, h // 2, :]
                            if r == 1:
                                dst = dst[:, CW * b4:CW * (b4 + 1)]
                            elif r == 4:
                                dst = dst.rearrange("p (m r) -> p r m", r=r)[:, b4, :]
                            else:
                                dst = dst.rearrange("p (m r) -> p r m", r=r)[:, 4 * b4:4 * b4 + 4, :]
                                src = src.rearrange("p (r m) -> p r m", r=4)
                            nc.scalar.activation(dst, src, ACT.Copy).then_inc(o_out, 1)

                        kept = 0
                        for t in range(NT_B + 4):
                            if t < NT_B:
                                exponentials(t)
                            if t >= 4:
                                h, g, blocks, nk = batches[t - 4]
                                if blocks[-1] % 4 == 3:
                                    keep_output(kept, t - 4)
                                    kept += 1

            cmb_loaded, cmb, cmb_exp, f_kept = sem("cmb_loaded"), sem("cmb"), sem("cmb_exp"), sem("f_kept")
            fz_loaded = [sem(f"fz_loaded{i}") for i in range(2)]
            weighted, gated, oa_kept = sem("weighted"), sem("gated"), [sem(f"oa_kept{i}") for i in range(2)]
            with ExitStack() as pb:
                R64 = HPG * NBLK
                sraw = sb(pb, "sraw", [R64, 3, 2, P])
                sm = sb(pb, "sm", [R64, 3, 2, P])
                mn = sb(pb, "mn", [R64, P])
                fe = sb(pb, "fe", [R64, 3, P])
                el = sb(pb, "el", [R64, 3, P])
                fb = sb(pb, "fb", [P, 2, L])
                zb = sb(pb, "zb", [P, 2, L])
                with nc.Block() as block:
                    @block.sync
                    def _(sp):
                        st_rows = st_d.rearrange("w (h b) c -> w h (b c)", b=NBLK)
                        for pair in range(2):
                            sp.dma_start(zb[:, pair, :], proj_d[T_ZA + pair]).then_inc(fz_loaded[pair], 16)
                        for g, r in enumerate(DIL):
                            for w in range(2):
                                for j in range(HPG):
                                    src = st_rows[w, HPG * g + j].rearrange("(r a m) -> a r m", r=r, a=NBLK)
                                    dst = sraw[NBLK * j:NBLK * (j + 1), g, w, :].rearrange("p (r m) -> p r m", r=r)
                                    sp.dma_start(dst, src).then_inc(cmb_loaded, 16)
                        sp.wait_ge(cmb, 11)
                        for g in range(3):
                            sp.dma_start(f_d[g].rearrange("j a c -> (j a) c"), fe[:, g, :]).then_inc(f_kept, 16)
                        sp.wait_ge(f_kept, 48)
                        for pair in range(NH // 2):
                            i = pair % 2
                            if pair >= 2:
                                sp.wait_ge(oa_kept[i], 16 * (pair // 2))
                                sp.dma_start(zb[:, i, :], proj_d[T_ZA + pair]).then_inc(fz_loaded[i], 16)
                            for half in range(2):
                                g, j = divmod(2 * pair + half, HPG)
                                src = f_d[g, j].rearrange("a c -> (a c)").partition_broadcast(64)
                                sp.dma_start(fb[64 * half:64 * half + 64, i, :], src).then_inc(fz_loaded[i], 16)
                            sp.wait_ge(gated, pair + 1)
                            sp.dma_start(o_d[6 + pair], zb[:, i, :]).then_inc(oa_kept[i], 16)
                        for i in range(2):
                            sp.wait_ge(oa_kept[i], 16 * 3)

                    @block.vector
                    def _(dve):
                        n = [0]

                        def link(ins):
                            n[0] += 1
                            ins.then_inc(cmb, 1)
                            dve.wait_ge(cmb, n[0])

                        dve.wait_ge(cmb_loaded, 16 * 6 * HPG)
                        for g, r in enumerate(DIL):
                            link(nc.vector.tensor_copy(
                                sm[:, g, :, :].rearrange("p w (m r) -> p w r m", r=r),
                                sraw[:, g, :, :].rearrange("p w (r m) -> p w r m", r=r)))
                        link(nc.vector.tensor_tensor(mn[:, :], sm[:, 0, 0, :], sm[:, 1, 0, :], ALU.min))
                        link(nc.vector.tensor_tensor(mn[:, :], mn[:, :], sm[:, 2, 0, :], ALU.min))
                        link(nc.vector.tensor_tensor(fe[:, :, :], mn[:, :].unsqueeze(1).to_broadcast((R64, 3, P)),
                                                     sm[:, :, 0, :], ALU.subtract))
                        dve.wait_ge(cmb_exp, 1)
                        link(nc.vector.tensor_tensor(el[:, :, :], fe[:, :, :], sm[:, :, 1, :], ALU.mult))
                        link(nc.vector.tensor_tensor(mn[:, :], el[:, 0, :], el[:, 1, :], ALU.add))
                        link(nc.vector.tensor_tensor(mn[:, :], mn[:, :], el[:, 2, :], ALU.add))
                        link(nc.vector.reciprocal(mn[:, :], mn[:, :]))
                        link(nc.vector.tensor_tensor(fe[:, :, :], fe[:, :, :],
                                                     mn[:, :].unsqueeze(1).to_broadcast((R64, 3, P)), ALU.mult))
                        for pair in range(NH // 2):
                            i = pair % 2
                            dve.wait_ge(fz_loaded[i], 48 * (pair // 2 + 1))
                            nc.vector.tensor_tensor(oT[:, pair, :], oT[:, pair, :], fb[:, i, :],
                                                    ALU.mult).then_inc(weighted, 1)
                            dve.wait_ge(weighted, pair + 1)
                            nc.vector.tensor_tensor(zb[:, i, :], oT[:, pair, :], zb[:, i, :],
                                                    ALU.mult).then_inc(gated, 1)

                    @block.scalar
                    def _(act):
                        act.wait_ge(cmb, 6)
                        nc.scalar.activation(fe[:, :, :], fe[:, :, :], ACT.Exp).then_inc(cmb_exp, 1)

        MSCALE = MD ** -0.5
        MB = L // (2 * P)
        qm_loaded = [sem(f"qm_loaded{i}") for i in range(2)]
        om_kept = [sem(f"om_kept{i}") for i in range(2)]
        ms_mm, m_max, m_bias, m_exp, m_rec, m_norm, mt_mm, mt_out, mo_mm, mo_out = (sem(a) for a in (
            "ms_mm", "m_max", "m_bias", "m_exp", "m_rec", "m_norm", "mt_mm", "mt_out", "mo_mm", "mo_out"))
        with ExitStack() as ph:
            qm = sb(ph, "qm", [P, 2, L])
            zm = sb(ph, "zm", [P, 2, L])
            mx = sb(ph, "mx", [P, 4, 2])
            nb = sb(ph, "nb", [P, 4, 2])
            ls = sb(ph, "ls", [P, 4, 2])
            rl = sb(ph, "rl", [P, 4, 2])
            em = sb(ph, "em", [P, 4, 2, ML])
            pt = sb(ph, "pt", [P, 3, 2, 2 * P])
            NT_M = MH * MB
            with nc.Block() as block:
                @block.sync
                def _(sp):
                    for h in range(MH):
                        i = h % 2
                        if h >= 2:
                            sp.wait_ge(om_kept[i], 16 * (h // 2))
                        sp.dma_start(qm[:, i, :], proj_d[T_QM + h]).then_inc(qm_loaded[i], 16)
                        sp.dma_start(zm[:, i, :], proj_d[T_ZM + h]).then_inc(qm_loaded[i], 16)

                @block.gpsimd
                def _(pool):
                    for h in range(MH):
                        pool.wait_ge(mo_out, MB * (h + 1))
                        pool.dma_start(o_d[12 + h], zm[:, h % 2, :]).then_inc(om_kept[h % 2], 16)
                    for i in range(2):
                        pool.wait_ge(om_kept[i], 32)

                @block.tensor
                def _(pe):
                    def scores(t):
                        h, b = divmod(t, MB)
                        pe.wait_ge(qm_loaded[h % 2], 32 * (h // 2 + 1))
                        if t >= 2:
                            pe.wait_ge(m_exp, 2 * (t - 1))
                        for i in range(2):
                            q = qm[:, h % 2, P * (2 * b + i):P * (2 * b + i + 1)]
                            mm = nc.tensor.matmul(psum[t % 2][:, ML * i:ML * (i + 1)], q, k_mem[:, h, :],
                                                  start=True, stop=True)
                        mm.then_inc(ms_mm, 1)

                    def turn(t):
                        pe.wait_ge(m_norm, 2 * (t + 1))
                        if t >= 2:
                            pe.wait_ge(mt_out, t - 1)
                        for kb in range(2):
                            for i in range(2):
                                mm = nc.tensor.transpose(psum[2 + t % 2][:, P * (2 * kb + i):P * (2 * kb + i + 1)],
                                                         em[:, t % 4, i, P * kb:P * (kb + 1)], ident[:, :])
                        mm.then_inc(mt_mm, 1)

                    def output(t):
                        h = t // MB
                        pe.wait_ge(mt_out, t + 1)
                        if t >= 2:
                            pe.wait_ge(mo_out, t - 1)
                        for kb in range(2):
                            mm = nc.tensor.matmul(psum[4 + t % 2][:, 0:2 * P], v_mem[:, kb, MD * h:MD * (h + 1)],
                                                  pt[:, t % 3, kb, :], start=(kb == 0), stop=(kb == 1))
                        mm.then_inc(mo_mm, 1)

                    for t in range(NT_M + 3):
                        if t < NT_M:
                            scores(t)
                        if 0 <= t - 2 < NT_M:
                            turn(t - 2)
                        if 0 <= t - 3 < NT_M:
                            output(t - 3)

                @block.vector
                def _(dve):
                    def maximum(t):
                        dve.wait_ge(ms_mm, t + 1)
                        nc.vector.tensor_reduce(mx[:, t % 4, :], psum[t % 2][:, :].rearrange("p (n k) -> p n k", n=2),
                                                AX.X, ALU.max).then_inc(m_max, 1)
                        dve.wait_ge(m_max, t + 1)
                        if t >= 4:
                            dve.wait_ge(m_exp, 2 * (t - 3))
                        nc.vector.tensor_scalar(nb[:, t % 4, :], mx[:, t % 4, :], -MSCALE, None,
                                                ALU.mult).then_inc(m_bias, 1)

                    def normalise(t):
                        dve.wait_ge(m_exp, 2 * (t + 1))
                        nc.vector.reciprocal(rl[:, t % 4, :], ls[:, t % 4, :]).then_inc(m_rec, 1)
                        dve.wait_ge(m_rec, t + 1)
                        for i in range(2):
                            nc.vector.tensor_scalar(em[:, t % 4, i, :], em[:, t % 4, i, :], rl[:, t % 4, i:i + 1],
                                                    None, ALU.mult).then_inc(m_norm, 1)

                    def gate(t):
                        h, b = divmod(t, MB)
                        dve.wait_ge(mo_mm, t + 1)
                        dve.wait_ge(qm_loaded[h % 2], 32 * (h // 2 + 1))
                        z = zm[:, h % 2, 2 * P * b:2 * P * (b + 1)]
                        nc.vector.tensor_tensor(z, psum[4 + t % 2][:, 0:2 * P], z, ALU.mult).then_inc(mo_out, 1)

                    for t in range(NT_M + 4):
                        if t < NT_M:
                            maximum(t)
                        if 0 <= t - 1 < NT_M:
                            normalise(t - 1)
                        if 0 <= t - 4 < NT_M:
                            gate(t - 4)

                @block.scalar
                def _(act):
                    def exponentials(t):
                        act.wait_ge(m_bias, t + 1)
                        if t >= 4:
                            act.wait_ge(mt_mm, t - 3)
                        for i in range(2):
                            nc.scalar.activation(em[:, t % 4, i, :], psum[t % 2][:, ML * i:ML * (i + 1)], ACT.Exp,
                                                 bias=nb[:, t % 4, i:i + 1], scale=MSCALE,
                                                 accum_out=ls[:, t % 4, i:i + 1]).then_inc(m_exp, 1)

                    def keep_turned(t):
                        act.wait_ge(mt_mm, t + 1)
                        if t >= 3:
                            act.wait_ge(mo_mm, t - 2)
                        nc.scalar.activation(pt[:, t % 3, :, :].rearrange("p a b -> p (a b)"), psum[2 + t % 2][:, :],
                                             ACT.Copy).then_inc(mt_out, 1)

                    for t in range(NT_M + 2):
                        if t < NT_M:
                            exponentials(t)
                        if t >= 2:
                            keep_turned(t - 2)

        yr_loaded = [sem(f"yr_loaded{c}") for c in range(NQ)]
        ys_hi_done, ys_split = sem("ys_hi_done"), sem("ys_split")
        g_mm, g_sig, g_y, g_z = sem("g_mm"), sem("g_sig"), sem("g_y"), sem("g_z")
        zs_loaded = [sem(f"zs_loaded{i}") for i in range(2)]
        os_kept = [sem(f"os_kept{i}") for i in range(2)]
        N_GLU = NKV + N_MAIN
        with ExitStack() as ph:
            ys_hi = sb(ph, "ys_hi", [P, KS, L], F32R)
            ys_lo = sb(ph, "ys_lo", [P, KS, L], F32R)
            yr = sb(ph, "yr", [P, KS, L])
            sg = sb(ph, "sg", [P, 2, CW])
            zs = sb(ph, "zs", [P, 2, L])
            with nc.Block() as block:
                @block.sync
                def _(sp):
                    for c in range(NQ):
                        cols = slice(CW * c, CW * (c + 1))
                        sp.dma_start(yr[:, :, cols], ys_d[:, :, cols].rearrange("k p c -> p k c")).then_inc(
                            yr_loaded[c], 16)
                        if c == 0:
                            load_pair(sp, N_GLU, w_glu[0], w_glu[1], KS)
                    for pair in (1, 2):
                        load_pair(sp, N_GLU + pair, w_glu[2 * pair], w_glu[2 * pair + 1], KS)

                @block.gpsimd
                def _(pool):
                    for n in range(2):
                        pool.dma_start(zs[:, n, :], proj_d[T_ZS + n]).then_inc(zs_loaded[n], 16)
                    for n in range(KS):
                        i = n % 2
                        pool.wait_ge(g_z, NQ * (n + 1))
                        pool.dma_start(o_d[n], zs[:, i, :]).then_inc(os_kept[i], 16)
                        if n + 2 < KS:
                            pool.wait_ge(os_kept[i], 16 * (n // 2 + 1))
                            pool.dma_start(zs[:, i, :], proj_d[T_ZS + n + 2]).then_inc(zs_loaded[i], 16)
                    for i in range(2):
                        pool.wait_ge(os_kept[i], 16 * KS // 2)

                @block.scalar
                def _(act):
                    for c in range(NQ):
                        act.wait_ge(yr_loaded[c], 16)
                        cols = slice(CW * c, CW * (c + 1))
                        nc.scalar.activation(ys_hi[:, :, cols], yr[:, :, cols], ACT.Copy).then_inc(ys_hi_done, 1)
                    for n in range(KS):
                        for c in range(NQ):
                            u = NQ * n + c
                            act.wait_ge(g_mm, u + 1)
                            if u >= 2:
                                act.wait_ge(g_y, u - 1)
                            nc.scalar.activation(sg[:, u % 2, :], psum[4 * (n % 2) + c][:, :], ACT.Sigmoid,
                                                 bias=bglu[:, n:n + 1]).then_inc(g_sig, 1)

                @block.vector
                def _(dve):
                    split_pair(dve, N_GLU, lambda s: (mm_done, 8 * N_MAIN), KS)
                    for c in range(NQ):
                        dve.wait_ge(ys_hi_done, c + 1)
                        cols = slice(CW * c, CW * (c + 1))
                        nc.vector.tensor_tensor(ys_lo[:, :, cols], yr[:, :, cols], ys_hi[:, :, cols].bitcast(F32),
                                                ALU.subtract).then_inc(ys_split, 1)
                    for pair in range(3):
                        for n in (2 * pair, 2 * pair + 1):
                            dve.wait_ge(zs_loaded[n % 2], 16 * (n // 2 + 1))
                            for c in range(NQ):
                                u = NQ * n + c
                                dve.wait_ge(g_sig, u + 1)
                                y = yr[:, n, CW * c:CW * (c + 1)]
                                nc.vector.tensor_tensor(y, sg[:, u % 2, :], y, ALU.mult).then_inc(g_y, 1)
                                dve.wait_ge(g_y, u + 1)
                                z = zs[:, n % 2, :].rearrange("p (c s) -> p s c", s=CH)[
                                    :, CW // NC * c:CW // NC * (c + 1), :]
                                nc.vector.tensor_tensor(z, y.rearrange("p (s c) -> p s c", c=NC), z,
                                                        ALU.mult).then_inc(g_z, 1)
                            if pair < 2:
                                split_pair(dve, N_GLU + pair + 1, lambda s: (g_mm, 8 * pair + 4 * s + 4), KS,
                                           (n % 2,))

                @block.tensor
                def _(pe):
                    for n in range(KS):
                        s = n % 2
                        pe.wait_ge(w_split[s], N_GLU + n // 2 + 1)
                        for c in range(NQ):
                            if n >= 2:
                                pe.wait_ge(g_sig, NQ * (n - 2) + c + 1)
                            if n == 0:
                                pe.wait_ge(ys_split, c + 1)
                            cols = slice(CW * c, CW * (c + 1))
                            three_pass(psum[4 * s + c][:, :], [
                                (wt(s, k), (ys_hi[:, k, cols], ys_lo[:, k, cols]))
                                for k in range(KS)]).then_inc(g_mm, 1)

        NBR, NOUT = D // P, D // (2 * P)
        N_MRG = N_GLU + 3
        o_loaded, o_hi_done, o_split = sem("o_loaded"), sem("o_hi_done"), sem("o_split")
        gt_loaded = [sem(f"gt_loaded{i}") for i in range(2)]
        xq_loaded, y_kept = sem("xq_loaded"), sem("y_kept")
        b_half = sem("b_half")
        b_mm, b_gated, b_sum, m_hi_done, m_split = (sem(a) for a in (
            "b_mm", "b_gated", "b_sum", "m_hi_done", "m_split"))
        p_mm, y_sum, y_sq, y_acc, f_mm, f_root, f_rstd, y_out_ready = (sem(a) for a in (
            "p_mm", "y_sum", "y_sq", "y_acc", "f_mm", "f_root", "f_rstd", "y_out_ready"))
        with ExitStack() as ph:
            KO = 16
            orw = sb(ph, "orw", [P, KO // 2, CW])
            wx_hi = sb(ph, "wx_hi", [P, 2, KD, P], F32R)
            wx_lo = sb(ph, "wx_lo", [P, 2, KD, P], F32R)
            o_hi = sb(ph, "o_hi", [P, KO, CW], F32R)
            o_lo = sb(ph, "o_lo", [P, KO, CW], F32R)
            gt = sb(ph, "gt", [P, 2, 3, CW])
            m_hi = sb(ph, "m_hi", [P, KD, CW], F32R)
            m_lo = sb(ph, "m_lo", [P, KD, CW], F32R)
            xq = sb(ph, "xq", [P, KD, CW])
            tb = sb(ph, "tb", [P, CW])
            sqb = sb(ph, "sqb", [P, CW])
            acc = sb(ph, "acc", [P, CW])
            rs = sb(ph, "rs", [P, CW])
            BR = ((0, 6), (6, 12), (12, 16))

            def wq(i, s, k):
                hi, lo = (w_hi, w_lo) if i % 2 == 0 else (wx_hi, wx_lo)
                return hi[:, s, k, :], lo[:, s, k, :]

            def chunk_cols(q):
                return slice(CW * q, CW * (q + 1))

            with nc.Block() as block:
                @block.sync
                def _(sp):
                    def load_o(q, half):
                        if q or half:
                            sp.wait_ge(o_split, 4 * q + 2 * half)
                        src = o_d[KO // 2 * half:KO // 2 * (half + 1), :, chunk_cols(q)]
                        sp.dma_start(orw[:, :, :], src.rearrange("k p c -> p k c")).then_inc(o_loaded, 16)

                    for q in range(NQ):
                        if q == 0:
                            load_o(0, 0)
                        for i in range(NBR):
                            load_pair(sp, N_MRG + 12 * q + i, w_br[i, 0], w_br[i, 1])
                            if i == 0:
                                load_o(q, 1)
                            if i == 5:
                                if q:
                                    sp.wait_ge(y_kept, 16 * q)
                                sp.dma_start(xq[:, :, :], x_t[:, :, chunk_cols(q)]).then_inc(xq_loaded, 16)
                            if i == 4 and q + 1 < NQ:
                                load_o(q + 1, 0)
                        for i in range(NOUT):
                            load_pair(sp, N_MRG + 12 * q + NBR + i, w_out[2 * i], w_out[2 * i + 1])

                @block.gpsimd
                def _(pool):
                    for q in range(NQ):
                        for n in range(NBR):
                            u = NBR * q + n
                            if u >= 2:
                                pool.wait_ge(b_sum, u - 1)
                            src = proj_d[T_G:NT].rearrange("(b n) p c -> n p b c", b=3)
                            pool.dma_start(gt[:, u % 2, :, :], src[n][:, :, chunk_cols(q)]).then_inc(
                                gt_loaded[u % 2], 16)
                            if n == 2 and q:
                                pool.wait_ge(y_out_ready, KD * q)
                                pool.dma_start(y_out[:, :, chunk_cols(q - 1)], xq[:, :, :]).then_inc(y_kept, 16)
                    pool.wait_ge(y_out_ready, KD * NQ)
                    pool.dma_start(y_out[:, :, chunk_cols(NQ - 1)], xq[:, :, :]).then_inc(y_kept, 16)
                    pool.wait_ge(y_kept, 16 * NQ)

                @block.tensor
                def _(pe):
                    def total(q):
                        pe.wait_ge(y_acc, KD * (q + 1))
                        nc.tensor.matmul(psum[7][:, :], ones[:, :], acc[:, :], start=True, stop=True).then_inc(f_mm, 1)

                    for q in range(NQ):
                        for n in range(NBR):
                            u = NBR * q + n
                            for s in range(2):
                                pe.wait_ge(w_split[s], N_MRG + 12 * q + n + 1)
                            if n == 0:
                                pe.wait_ge(o_split, 4 * (q + 1))
                            for b, (k0, k1) in enumerate(BR):
                                if u >= 2:
                                    pe.wait_ge(b_gated, 3 * (u - 2) + b + 1)
                                three_pass(psum[3 * (n % 2) + b][:, :], [
                                    (wq(n, k // 8, k % 8), (o_hi[:, k, :], o_lo[:, k, :]))
                                    for k in range(k0, k1)]).then_inc(b_mm, 1)
                            if n == 0 and q:
                                total(q - 1)
                        for n in range(KD):
                            pe.wait_ge(w_split[n % 2], N_MRG + 12 * q + NBR + n // 2 + 1)
                            if n == 0:
                                pe.wait_ge(m_split, KD * (q + 1) - 1)
                            if n < 2 and q:
                                pe.wait_ge(y_sum, KD * q)
                                pe.wait_ge(f_root, q)
                            if n >= 2:
                                pe.wait_ge(y_sum, KD * q + n - 1)
                            out = psum[6 + n % 2][:, :]
                            parts = [(wq(NBR + n // 2, n % 2, k), (m_hi[:, k, :], m_lo[:, k, :])) for k in range(KD)]
                            three_pass(out, parts[:-1], stop=False)
                            if n == 0:
                                pe.wait_ge(m_split, KD * (q + 1))
                            three_pass(out, parts[-1:], start=False).then_inc(p_mm, 1)
                    total(NQ - 1)

                @block.scalar
                def _(act):
                    def split_hi(q, piece):
                        act.wait_ge(o_loaded, 16 * (2 * q + piece // 2 + 1))
                        if q:
                            act.wait_ge(b_mm, 3 * NBR * q)
                        ks = slice(4 * piece, 4 * piece + 4)
                        rows = slice(4 * (piece % 2), 4 * (piece % 2) + 4)
                        nc.scalar.activation(o_hi[:, ks, :], orw[:, rows, :], ACT.Copy).then_inc(o_hi_done, 1)

                    def root(q):
                        act.wait_ge(f_mm, q + 1)
                        nc.scalar.activation(rs[:, :], psum[7][:, :], ACT.Sqrt, bias=eps[:, 0:1],
                                             scale=1.0 / D).then_inc(f_root, 1)

                    for piece in range(4):
                        split_hi(0, piece)
                    for q in range(NQ):
                        for n in range(NBR):
                            u = NBR * q + n
                            act.wait_ge(b_sum, u + 1)
                            if n == 0 and q:
                                act.wait_ge(p_mm, KD * q)
                            nc.scalar.activation(m_hi[:, n, :], tb[:, :], ACT.Copy).then_inc(m_hi_done, 1)
                            if n == 0 and q:
                                root(q - 1)
                        for n in range(KD):
                            u = KD * q + n
                            act.wait_ge(y_sum, u + 1)
                            if u >= 1:
                                act.wait_ge(y_acc, u)
                            nc.scalar.activation(sqb[:, :], xq[:, n, :], ACT.Square).then_inc(y_sq, 1)
                            if n % 2 and q + 1 < NQ:
                                split_hi(q + 1, n // 2)
                    root(NQ - 1)

                @block.vector
                def _(dve):
                    def split_lo(q, piece):
                        dve.wait_ge(o_hi_done, 4 * q + piece + 1)
                        ks = slice(4 * piece, 4 * piece + 4)
                        rows = slice(4 * (piece % 2), 4 * (piece % 2) + 4)
                        nc.vector.tensor_tensor(o_lo[:, ks, :], orw[:, rows, :], o_hi[:, ks, :].bitcast(F32),
                                                ALU.subtract).then_inc(o_split, 1)

                    def normalise(q):
                        dve.wait_ge(f_root, q + 1)
                        nc.vector.reciprocal(rs[:, :], rs[:, :]).then_inc(f_rstd, 1)
                        dve.wait_ge(f_rstd, q + 1)
                        for n in range(KD):
                            nc.vector.scalar_tensor_tensor(xq[:, n, :], xq[:, n, :], g_in[:, 2, n:n + 1], rs[:, :],
                                                           ALU.mult, ALU.mult).then_inc(y_out_ready, 1)

                    def split_next(i):
                        if i >= 12 * NQ:
                            return
                        q, n = divmod(i - 2, 12)
                        if i < 2:
                            used = (lambda s: (g_mm, 4 * KS)) if i == 0 else None
                        elif n < NBR:
                            used = lambda s: (b_mm, 3 * (NBR * q + n) + 2 + s)
                        else:
                            used = lambda s: (p_mm, KD * q + 2 * (n - NBR) + 1 + s)
                        split_pair(dve, N_MRG + i, used, into=(w_hi, w_lo) if i % 2 == 0 else (wx_hi, wx_lo))

                    split_next(0)
                    for piece in range(4):
                        split_lo(0, piece)
                        if piece == 1:
                            split_next(1)
                    for q in range(NQ):
                        for n in range(NBR):
                            u = NBR * q + n
                            dve.wait_ge(gt_loaded[u % 2], 16 * (u // 2 + 1))
                            gates = gt[:, u % 2, :, :]
                            for b in range(3):
                                dve.wait_ge(b_mm, 3 * u + b + 1)
                                nc.vector.tensor_tensor(gates[:, b, :], psum[3 * (n % 2) + b][:, :], gates[:, b, :],
                                                        ALU.mult).then_inc(b_gated, 1)
                            split_next(12 * q + n + 2)
                            dve.wait_ge(b_gated, 3 * (u + 1))
                            nc.vector.tensor_tensor(gates[:, 0, :], gates[:, 0, :], gates[:, 1, :],
                                                    ALU.add).then_inc(b_half, 1)
                            dve.wait_ge(b_half, u + 1)
                            if u:
                                dve.wait_ge(m_split, u)
                            nc.vector.tensor_tensor(tb[:, :], gates[:, 0, :], gates[:, 2, :],
                                                    ALU.add).then_inc(b_sum, 1)
                            dve.wait_ge(m_hi_done, u + 1)
                            nc.vector.tensor_tensor(m_lo[:, n, :], tb[:, :], m_hi[:, n, :].bitcast(F32),
                                                    ALU.subtract).then_inc(m_split, 1)
                            if n == 0 and q:
                                normalise(q - 1)
                        dve.wait_ge(xq_loaded, 16 * (q + 1))
                        for n in range(KD):
                            u = KD * q + n
                            dve.wait_ge(p_mm, u + 1)
                            nc.vector.tensor_tensor(xq[:, n, :], psum[6 + n % 2][:, :], xq[:, n, :],
                                                    ALU.add).then_inc(y_sum, 1)
                            if n % 2:
                                split_next(12 * q + NBR + n // 2 + 2)
                            dve.wait_ge(y_sq, u + 1)
                            if n == 0:
                                if q:
                                    dve.wait_ge(f_mm, q)
                                nc.vector.tensor_copy(acc[:, :], sqb[:, :]).then_inc(y_acc, 1)
                            else:
                                dve.wait_ge(y_acc, u)
                                nc.vector.tensor_tensor(acc[:, :], acc[:, :], sqb[:, :], ALU.add).then_inc(y_acc, 1)
                            if n % 2 and q + 1 < NQ:
                                split_lo(q + 1, n // 2)
                    normalise(NQ - 1)


def _dram_inputs(nc, arrays):
    return {n: nc.dram_tensor(n, a.shape, mybir.dt.from_np(a.dtype), kind="ExternalInput").ap()
            for n, a in arrays.items()}


def rel_buckets():
    out = np.zeros((NBUCKET + 1, 3, 384), np.float32)
    for g, r in enumerate(DIL):
        for x in range(384):
            delta = 255 - x
            if not 0 <= delta <= P:
                out[NBUCKET, g, x] = -BIG
                continue
            n = delta * r
            if n < NBUCKET // 2:
                b = n
            else:
                b = NBUCKET // 2 + int(np.float32(
                    np.log(np.float32(n) / np.float32(NBUCKET // 2)) / np.float32(math.log(MAXD / (NBUCKET // 2)))
                    * np.float32(NBUCKET - NBUCKET // 2)))
                b = min(b, NBUCKET - 1)
            out[b, g, x] = 1.0
    return out


def layouts(i):
    def f(a):
        return np.ascontiguousarray(a, np.float32)

    def tiles(w):
        k, n = w.shape
        return f(w.reshape(k // P, P, n // P, P).transpose(2, 1, 0, 3))

    def by_channel(v):
        return f(v.reshape(-1, P).T)

    def transposed(x):
        return f(x.T.reshape(-1, P, x.shape[0]).transpose(1, 0, 2))

    def stack(re, im):
        return np.concatenate([re, im], 1)

    i = {k: np.asarray(v) for k, v in i.items()}
    lam = [i[n][0].T for n in ("ssm_lambda_re", "ssm_lambda_im")]
    dt = np.broadcast_to(i["ssm_log_dt"][0], (NS, G))
    b = [i[n][0].transpose(1, 0, 2) for n in ("ssm_b_re", "ssm_b_im")]
    c = [i[n][0].transpose(2, 0, 1) for n in ("ssm_c_re", "ssm_c_im")]

    def unit(parts, u):
        gs = slice(UG * u, UG * (u + 1))
        return np.concatenate([np.concatenate([p[:, gs].reshape(NS, -1) for p in half], 1) for half in parts], 0)

    halves = ([lam[0], lam[1], dt, c[0], c[1], b[0], b[1]], [lam[0], lam[1], dt, c[1], c[0], b[1], b[0]])
    ssm_par = np.stack([unit(halves, u) for u in range(NU)])
    d = i["ssm_d"][0].reshape(NU, 1, UG, HG)
    br = np.concatenate([i["w_br_ssm"][0], i["w_br_attn"][0], i["w_br_mem"][0]], 0)
    w_br = tiles(br).reshape(D // P, P, 2, 8, P).transpose(0, 2, 1, 3, 4)
    return {
        "x_t": transposed(i["x"][0]), "mem_t": transposed(i["mem"][0]),
        "norm_g": by_channel(i["norm_g"][0]), "mem_norm_g": by_channel(i["mem_norm_g"][0]),
        "final_g": by_channel(i["final_norm_g"]),
        "w_in": tiles(i["w_in"][0]), "w_kv": tiles(i["w_mem_kv"][0]), "b_gate": by_channel(i["b_gate"][0]),
        "ssm_par": f(ssm_par), "ssm_d": f(np.broadcast_to(d, (NU, HG, UG, HG))),
        "w_glu": tiles(i["w_glu"][0]), "b_glu": by_channel(i["b_glu"][0]),
        "w_br": f(w_br), "w_out": tiles(i["w_out"][0]), "rel_bias": f(i["rel_bias"]),
        "buckets": rel_buckets(), "ident_c": np.eye(P, dtype=np.float32),
        "anti_c": np.eye(P, dtype=np.float32)[::-1].copy(),
        "sign_c": np.repeat(np.array([1.0, -1.0], np.float32), NS)[:, None].copy(),
        "steps_c": np.tile(np.arange(1, NC + 1, dtype=np.float32), (P, 1)),
        "powers_c": np.tile(np.r_[np.arange(CH + 1), np.arange(CH)[::-1]].astype(np.float32), (P, 1)),
    }


def kernel(**inputs):
    import concourse.bacc as _bacc
    from concourse.bass_utils import run_bass_kernel_spmd as _run

    nc = _bacc.Bacc("TRN2", target_bir_lowering=False, num_devices=1)
    arrays = layouts(inputs)
    aps = _dram_inputs(nc, arrays)
    y_out = nc.dram_tensor("y_out", (P, KD, L), F32, kind="ExternalOutput").ap()
    build_program(nc, y_out=y_out, **aps)
    r = _run(nc, [arrays], core_ids=[0])
    y = r.results[0]["y_out"]
    return np.ascontiguousarray(y.transpose(2, 1, 0).reshape(1, L, D))
```

```python
import math
from contextlib import ExitStack

import numpy as np
import concourse.bass as bass
from concourse import mybir

F32 = mybir.dt.float32
F32R = mybir.dt.float32r
ACT = mybir.ActivationFunctionType
ALU = mybir.AluOpType
AX = mybir.AxisListType

P = 128
D = 1024
L = 2048
KD = D // P
CW = 512
NQ = L // CW
EPS = 1e-6
D_SSM, HG, NS = 768, 16, 64
G = D_SSM // HG
GB = P // HG
NB = G // GB
UG = 4
NU = G // UG
CH = P // HG
NC = L // CH
HD, HPG = 64, 4
DIL = (1, 4, 16)
NH = HPG * len(DIL)
NBLK = L // P
KS = D_SSM // P
MH, MD, ML = 4, 128, 256
NBUCKET, MAXD = 32, 2048
BIG = 1e30
T_U, T_ZS, T_Q, T_K, T_V, T_ZA, T_QM, T_ZM, T_G = 0, 6, 12, 18, 24, 30, 36, 40, 44
NT = 68
TWO_PI_HI = 6.28125
TWO_PI_LO = 2 * math.pi - TWO_PI_HI
MAGIC = 1.5 * 2 ** 23
PI_SAFE = 3.1415925


def build_program(nc, x_t, mem_t, norm_g, mem_norm_g, final_g, w_in, w_kv, b_gate, ssm_par, ssm_d, w_glu, b_glu,
                  w_br, w_out, rel_bias, buckets, ident_c, anti_c, sign_c, steps_c, powers_c, y_out):
    ctx = ExitStack()
    with ctx:
        def sb(stack, name, shape, dt=F32):
            return stack.enter_context(nc.sbuf_tensor(name, shape, dt))

        def sem(name):
            return ctx.enter_context(nc.semaphore(name))

        def dram(name, shape):
            return nc.dram_tensor(name, shape, F32).ap()

        proj_d = dram("proj_d", [NT, P, L])
        v_d = dram("v_d", [3, P, 2 * L])
        ys_d = dram("ys_d", [KS, P, L])
        o_d = dram("o_d", [16, P, L])
        mats_d = dram("mats_d", [NU, P, UG, 5, P])
        cs_d = dram("cs_d", [NU, P, UG, 2, NC])
        m8_d = dram("m8_d", [NU, P, UG])
        bias_d = dram("bias_d", [3, NH, 384])
        st_d = dram("st_d", [2, NH * NBLK, P])
        f_d = dram("f_d", [3, HPG, NBLK, P])

        psum = [ctx.enter_context(nc.psum_tensor(f"bank{i}", [P, 512], F32)) for i in range(8)]

        w_raw = sb(ctx, "w_raw", [P, 2, KD, P])
        w_hi = sb(ctx, "w_hi", [P, 2, KD, P], F32R)
        w_lo = sb(ctx, "w_lo", [P, 2, KD, P], F32R)
        k_mem = sb(ctx, "k_mem", [P, MH, ML])
        v_mem = sb(ctx, "v_mem", [P, 2, MH * MD])
        ones = sb(ctx, "ones", [P, P])
        g_in = sb(ctx, "g_in", [P, 3, KD])
        bg = sb(ctx, "bg", [P, 24])
        bglu = sb(ctx, "bglu", [P, KS])
        eps = sb(ctx, "eps", [P, 1])
        ident = sb(ctx, "ident", [P, P])
        sign = sb(ctx, "sign", [P, 1])

        w_loaded = [sem(f"w_loaded{s}") for s in range(2)]
        w_split = [sem(f"w_split{s}") for s in range(2)]
        w_hi_done = sem("w_hi_done")
        consts = sem("consts")
        const_loaded = sem("const_loaded")

        def load_pair(sp, n, src0, src1, kt=KD):
            for s, src in enumerate((src0, src1)):
                if not (isinstance(n, int) and n == 0):
                    sp.wait_ge(w_split[s], n)
                sp.dma_start(w_raw[:, s, 0:kt, :], src).then_inc(w_loaded[s], 16)

        def split_pair(dve, n, used, kt=KD, slots=(0, 1), into=(w_hi, w_lo), raw=w_raw, loaded=w_loaded, loads=None):
            for s in slots:
                dve.wait_ge(loaded[s], 16 * (n + 1 if loads is None else loads))
                if used is not None:
                    dve.wait_ge(*used(s))
                hi, lo = (t[:, s, 0:kt, :] for t in into)
                nc.vector.tensor_copy(hi, raw[:, s, 0:kt, :]).then_inc(w_hi_done, 1)
                dve.wait_ge(w_hi_done, 2 * n + s + 1)
                nc.vector.tensor_tensor(lo, raw[:, s, 0:kt, :], hi.bitcast(F32), ALU.subtract).then_inc(w_split[s], 1)

        def three_pass(out, pairs, start=True, stop=True):
            last = None
            for n, ((ah, al), (bh, bl)) in enumerate(pairs):
                nc.tensor.matmul(out, ah, bh, start=(start and n == 0), stop=False)
                nc.tensor.matmul(out, ah, bl, start=False, stop=False)
                last = nc.tensor.matmul(out, al, bh, start=False, stop=(stop and n == len(pairs) - 1))
            return last

        def wt(s, k, cols=slice(0, P)):
            return w_hi[:, s, k, cols], w_lo[:, s, k, cols]

        NKV = 4
        x_loaded = [sem(f"x_loaded{i}") for i in range(2)]
        sq_ready, sq_used, root_done, rstd_done = (sem(s) for s in (
            "sq_ready", "sq_used", "root_done", "rstd_done"))
        scaled, hi_done, h_ready = sem("scaled"), sem("hi_done"), sem("h_ready")
        kv_mm, kv_out = sem("kv_mm"), sem("kv_out")
        mm_done, bank_free = sem("mm_done"), sem("bank_free")
        stored = [sem(f"stored{s}") for s in range(2)]

        segments, m = [], 0
        for kind, n, tiles, r in (
            [("copy", 3, lambda i, s: T_U + 2 * i + s, CH)]
            + [("value", 1, (lambda i, s, t=T_V + 2 * g: t + s), DIL[g]) for g in range(3)]
            + [("silu", 3, lambda i, s: T_ZS + 2 * i + s, 1)]
            + [("copy", 1, (lambda i, s, t=t + 2 * g: t + s), DIL[g]) for g in range(3) for t in (T_Q, T_K)]
            + [("silu", 3, lambda i, s: T_ZA + 2 * i + s, 1), ("copy", 2, lambda i, s: T_QM + 2 * i + s, 1),
               ("silu", 2, lambda i, s: T_ZM + 2 * i + s, 1), ("gate", 12, lambda i, s: T_G + 2 * i + s, 1)]
        ):
            segments.append((kind, m, n, tiles, r))
            m += n
        N_MAIN = m

        def products(m, s, c):
            return 2 * c + s + 1 if m == 0 else 8 * m + 4 * s + c + 1

        kind_of = [kind for kind, _, n, _, _ in segments for _ in range(n)]

        NP = 9 + CH
        M_TAB = 6
        par_loaded, tab = sem("par_loaded"), sem("tab")
        dt_done, pow_ready, pow_done, ang_ready, cs_done, cs_ready = (sem(a) for a in (
            "dt_done", "pow_ready", "pow_done", "ang_ready", "cs_done", "cs_ready"))
        ca_ready, ba_ready, k_mm, k_ready, bt_mm, m3_half = (sem(a) for a in (
            "ca_ready", "ba_ready", "k_mm", "k_ready", "bt_mm", "m3_half"))
        ca_kept, k_kept, m3_kept, m8_kept = (sem(a) for a in ("ca_kept", "k_kept", "m3_kept", "m8_kept"))
        k_out = sem("k_out")
        cs_kept = [sem(f"cs_kept{i}") for i in range(2)]

        def unit_of(m, ahead=0):
            u, part = divmod(m - M_TAB + ahead, 2)
            return (u, part) if 0 <= u < NU else (None, part)

        with ExitStack() as ph:
            h_hi = sb(ph, "h_hi", [P, KD, L], F32R)
            h_lo = sb(ph, "h_lo", [P, KD, L], F32R)
            ev = sb(ph, "ev", [P, 2, L])
            with ExitStack() as pn:
                xa = sb(pn, "xa", [P, KD, CW])
                sq = sb(pn, "sq", [P, 4, CW])
                rstd = sb(pn, "rstd", [P, 2, CW])
            par = sb(ph, "par", [P, UG * (3 + 4 * HG)])
            dpar = sb(ph, "dpar", [HG, UG, HG])
            steps = sb(ph, "steps", [P, NC])
            powers = sb(ph, "powers", [P, NP])
            small = {n: sb(ph, f"sm_{n}", [P, UG]) for n in (
                "dt", "ldt", "th", "den", "t0", "t1", "nr", "fr", "sfi", "sph")}
            pw = {n: sb(ph, f"pw_{n}", [P, UG, NP]) for n in (
                "x", "t", "mag", "sin", "cos", "ar", "ai", "sar", "sai", "nai")}
            bb = sb(ph, "bb", [P, UG, HG])
            bbs = sb(ph, "bbs", [P, UG, HG])
            ca = sb(ph, "ca", [P, UG, CH + 1, HG])
            cas = sb(ph, "cas", [P, UG, CH + 1, HG])
            tmp = sb(ph, "tmp", [P, UG, CH + 1, HG])
            ba = sb(ph, "ba", [P, UG, CH, HG])
            bas = sb(ph, "bas", [P, UG, CH, HG])
            m3 = sb(ph, "m3", [P, 2, UG, P])
            kpad = sb(ph, "kpad", [HG, UG, (2 * CH - 1) * HG])
            tx = sb(ph, "tx", [P, 2, NC])
            cs = sb(ph, "cs", [P, 2, 2, NC])
            m8 = sb(ph, "m8", [P, UG])
            ldr, lim, ldt_in = (par[:, UG * i:UG * (i + 1)] for i in range(3))
            bc = [par[:, UG * 3 + UG * HG * i:UG * 3 + UG * HG * (i + 1)].rearrange("p (g h) -> p g h", g=UG)
                  for i in range(4)]
            xb = ev[:, :, :].rearrange("p s (k c) -> p (s k) c", c=CW)
            xbuf = (xa, xb)
            jobs = [(ML, mem_t, slice(0, ML), L - CW, 1)] + [
                (CW, x_t, slice(CW * q, CW * (q + 1)), CW * q, 0) for q in range(NQ)]

            with nc.Block() as block:
                @block.sync
                def _(sp):
                    pairs = [(tiles(i, 0), tiles(i, 1)) for _, _, n, tiles, _ in segments for i in range(n)]
                    for j, (w, src, cols, _, _) in enumerate(jobs):
                        if j == NKV:
                            load_pair(sp, NKV, w_in[pairs[0][0]], w_in[pairs[0][1]])
                        if j >= 2:
                            sp.wait_ge(h_ready, 2 * (j - 1))
                        sp.dma_start(xbuf[j % 2][:, :, 0:w], src[:, :, cols]).then_inc(x_loaded[j % 2], 16)
                        if j == 0:
                            sp.dma_start(g_in[:, 0, :], norm_g).then_inc(const_loaded, 16)
                            sp.dma_start(g_in[:, 1, :], mem_norm_g).then_inc(const_loaded, 16)
                            sp.dma_start(g_in[:, 2, :], final_g).then_inc(const_loaded, 16)
                            sp.dma_start(bg[:, :], b_gate).then_inc(const_loaded, 16)
                            sp.dma_start(bglu[:, :], b_glu).then_inc(const_loaded, 16)
                            sp.dma_start(ident[:, :], ident_c).then_inc(const_loaded, 16)
                            sp.dma_start(sign[:, :], sign_c).then_inc(const_loaded, 16)
                        if j < NKV:
                            load_pair(sp, j, w_kv[2 * j], w_kv[2 * j + 1])
                    for m in range(-1, N_MAIN):
                        if m + 2 < N_MAIN:
                            load_pair(sp, NKV + m + 2, w_in[pairs[m + 2][0]], w_in[pairs[m + 2][1]])
                        if m == M_TAB - 1:
                            sp.wait_ge(h_ready, 2 * len(jobs))
                            sp.dma_start(steps[:, :], steps_c).then_inc(const_loaded, 16)
                            sp.dma_start(powers[:, :], powers_c).then_inc(const_loaded, 16)
                        u, part = unit_of(m, 1)
                        if u is not None and part == 0:
                            if u:
                                sp.wait_ge(k_ready, u)
                            sp.dma_start(par[:, :], ssm_par[u]).then_inc(par_loaded, 16)
                            sp.dma_start(dpar[:, :, :], ssm_d[u]).then_inc(par_loaded, 16)
                        u, part = unit_of(m)
                        if u is not None and part == 1:
                            md = mats_d[u]
                            sp.wait_ge(ca_ready, u + 1)
                            for kind, c in ((2, ca), (3, cas)):
                                sp.dma_start(md[:, :, kind, :].rearrange("p g (j h) -> p g j h", j=CH),
                                             c[:, :, 1:, :]).then_inc(ca_kept, 16)
                            sp.dma_start(m8_d[u], m8[:, :]).then_inc(m8_kept, 16)
                            sp.wait_ge(k_ready, u + 1)
                            for t in range(CH):
                                at = HG * (CH - 1 - t)
                                sp.dma_start(md[HG * t:HG * (t + 1), :, 4, :],
                                             kpad[:, :, at:at + P]).then_inc(k_kept, 16)
                            sp.wait_ge(cs_ready, 2 * u + 1)
                            for g in range(2):
                                sp.dma_start(cs_d[u, :, g, :, :], cs[:, g, :, :]).then_inc(cs_kept[g], 16)
                        u, part = unit_of(m, -2)
                        if u is not None and part == 0:
                            sp.wait_ge(m3_half, 2 * u + 2)
                            sp.wait_ge(cs_ready, 2 * u + 2)
                            for half in range(2):
                                sp.dma_start(mats_d[u][:, :, half, :], m3[:, half, :, :]).then_inc(m3_kept, 16)
                            for g in range(2):
                                sp.dma_start(cs_d[u, :, 2 + g, :, :], cs[:, g, :, :]).then_inc(cs_kept[g], 16)
                    sp.wait_ge(ca_kept, 32 * NU)
                    sp.wait_ge(m8_kept, 16 * NU)
                    sp.wait_ge(k_kept, 16 * CH * NU)
                    sp.wait_ge(m3_kept, 32 * NU)
                    for g in range(2):
                        sp.wait_ge(cs_kept[g], 32 * NU)

                @block.gpsimd
                def _(pool):
                    for kind, m0, n, tiles, r in segments:
                        for i in range(n):
                            for s in range(2):
                                m = m0 + i
                                pool.wait_ge(bank_free, 8 * m + 4 * s + 4)
                                if kind == "value":
                                    dst = v_d[m - segments[1][1], :, L * s:L * (s + 1)]
                                else:
                                    dst = proj_d[tiles(i, s)]
                                pool.dma_start(dst, ev[:, s, :]).then_inc(stored[s], 16)
                    for s in range(2):
                        pool.wait_ge(stored[s], 16 * N_MAIN)

                @block.scalar
                def _(act):
                    act.wait_ge(consts, 2)
                    def squares(j):
                        w = jobs[j][0]
                        act.wait_ge(x_loaded[j % 2], 16 * (j // 2 + 1))
                        for k in range(KD):
                            if 8 * j + k >= 4:
                                act.wait_ge(sq_used, 8 * j + k - 3)
                            nc.scalar.activation(sq[:, k % 4, 0:w], xbuf[j % 2][:, k, 0:w],
                                                 ACT.Square).then_inc(sq_ready, 1)

                    def root(j):
                        w = jobs[j][0]
                        act.wait_ge(sq_used, 8 * (j + 1))
                        if j >= 2:
                            act.wait_ge(scaled, 8 * (j - 1))
                        nc.scalar.activation(rstd[:, j % 2, 0:w], psum[2 + j % 2][:, 0:w], ACT.Sqrt,
                                             bias=eps[:, 0:1], scale=1.0 / D).then_inc(root_done, 1)

                    def hi_parts(j):
                        w, at = jobs[j][0], jobs[j][3]
                        for half in range(2):
                            ks = slice(4 * half, 4 * half + 4)
                            act.wait_ge(scaled, 8 * j + 4 * half + 4)
                            if j == NQ:
                                act.wait_ge(kv_mm, 2 * NKV)
                            nc.scalar.activation(h_hi[:, ks, at:at + w], xbuf[j % 2][:, ks, 0:w],
                                                 ACT.Copy).then_inc(hi_done, 1)

                    def keep_kv(n):
                        for s in range(2):
                            act.wait_ge(kv_mm, 2 * n + s + 1)
                            src = psum[4 + n][:, ML * s:ML * (s + 1)]
                            dst = k_mem[:, 2 * n + s, :] if n < 2 else v_mem[:, s, 256 * (n - 2):256 * (n - 1)]
                            nc.scalar.activation(dst, src, ACT.Copy).then_inc(kv_out, 1)

                    def table_window(m, s):
                        u, part = unit_of(m)
                        if u is not None and (part, s) == (0, 0):
                            act.wait_ge(pow_ready, u + 1)
                            nc.scalar.activation(pw["mag"][:, :, :], pw["t"][:, :, :], ACT.Exp).then_inc(pow_done, 1)
                            nc.scalar.activation(pw["sin"][:, :, :], pw["x"][:, :, :], ACT.Sin).then_inc(pow_done, 1)
                            nc.scalar.activation(pw["cos"][:, :, :], pw["x"][:, :, :], ACT.Sin,
                                                 scale=0.5).then_inc(pow_done, 1)
                        if u is not None and part == 1:
                            for g in (2 * s, 2 * s + 1):
                                act.wait_ge(ang_ready, UG * u + g + 1)
                                if 2 * u + s:
                                    act.wait_ge(cs_kept[g % 2], 16 * (2 * u + s))
                                nc.scalar.activation(cs[:, g % 2, 1, :], tx[:, g % 2, :], ACT.Sin).then_inc(cs_done, 1)
                                nc.scalar.activation(cs[:, g % 2, 0, :], tx[:, g % 2, :], ACT.Sin,
                                                     scale=0.5).then_inc(cs_done, 1)
                        u, part = unit_of(m, 1)
                        if u is not None and (part, s) == (0, 1):
                            act.wait_ge(par_loaded, 32 * (u + 1))
                            nc.scalar.activation(small["dt"][:, :], ldt_in, ACT.Exp).then_inc(dt_done, 1)

                    squares(0)
                    root(0)
                    squares(1)
                    hi_parts(0)
                    root(1)
                    hi_parts(1)
                    for j in range(2, len(jobs)):
                        squares(j)
                        root(j)
                        if j < 4:
                            keep_kv(2 * j - 4)
                            keep_kv(2 * j - 3)
                        hi_parts(j)
                    for kind, m0, n, tiles, r in segments:
                        for i in range(n):
                            m = m0 + i
                            for s in range(2):
                                if m == 0:
                                    act.wait_ge(h_ready, 2 * len(jobs))
                                else:
                                    act.wait_ge(stored[s], 16 * m)
                                for c in range(NQ):
                                    act.wait_ge(mm_done, products(m, s, c))
                                    src = psum[4 * s + c][:, :]
                                    dst = ev[:, s, CW * c:CW * (c + 1)]
                                    if r > 1 and kind != "value":
                                        src = src.rearrange("p (m r) -> p r m", r=r)
                                        dst = ev[:, s, :].rearrange("p (r m) -> p r m", r=r)[
                                            :, :, CW // r * c:CW // r * (c + 1)]
                                    if kind == "silu":
                                        ins = nc.scalar.activation(dst, src, ACT.Silu)
                                    elif kind == "gate":
                                        t = tiles(i, s) - T_G
                                        ins = nc.scalar.activation(dst, src, ACT.Sigmoid, bias=bg[:, t:t + 1])
                                    else:
                                        ins = nc.scalar.activation(dst, src, ACT.Copy)
                                    ins.then_inc(bank_free, 1)
                                table_window(m, s)

                @block.vector
                def _(dve):
                    nc.vector.memset(ones[:, :], 1.0).then_inc(consts, 1)
                    nc.vector.memset(eps[:, :], EPS).then_inc(consts, 1)
                    dve.wait_ge(const_loaded, 112)
                    for j, (w, _, _, at, gi) in enumerate(jobs):
                        dve.wait_ge(root_done, j + 1)
                        r = rstd[:, j % 2, 0:w]
                        nc.vector.reciprocal(r, r).then_inc(rstd_done, 1)
                        dve.wait_ge(rstd_done, j + 1)
                        x = xbuf[j % 2]
                        for k in range(KD):
                            nc.vector.scalar_tensor_tensor(x[:, k, 0:w], x[:, k, 0:w], g_in[:, gi, k:k + 1], r,
                                                           ALU.mult, ALU.mult).then_inc(scaled, 1)
                        if j < 3:
                            n = (0, 1, 3)[j]
                            split_pair(dve, n, (None, lambda s: (kv_mm, s + 1), None, lambda s: (kv_mm, 6))[n])
                        if j == 3:
                            split_pair(dve, NKV, lambda s: (kv_mm, 2 * NKV))
                        for half in range(2):
                            ks = slice(4 * half, 4 * half + 4)
                            dve.wait_ge(hi_done, 2 * j + half + 1)
                            nc.vector.tensor_tensor(h_lo[:, ks, at:at + w], x[:, ks, 0:w],
                                                    h_hi[:, ks, at:at + w].bitcast(F32),
                                                    ALU.subtract).then_inc(h_ready, 1)
                        if j == 1:
                            split_pair(dve, 2, lambda s: (kv_mm, s + 3))
                    steps_done = [0]

                    def link(ins):
                        steps_done[0] += 1
                        ins.then_inc(tab, 1)
                        dve.wait_ge(tab, steps_done[0])

                    def tt(out, a, b, op):
                        link(nc.vector.tensor_tensor(out, a, b, op))

                    def ts(out, a, s1, s2, op0, op1=None):
                        if op1 is None:
                            link(nc.vector.tensor_scalar(out, a, s1, None, op0))
                        else:
                            link(nc.vector.tensor_scalar(out, a, s1, s2, op0, op1))

                    def reduce_angle(x, t):
                        ts(t, x, 1 / (2 * math.pi), MAGIC, ALU.mult, ALU.add)
                        ts(t, t, MAGIC, None, ALU.subtract)
                        link(nc.vector.scalar_tensor_tensor(x, t, -TWO_PI_HI, x, ALU.mult, ALU.add))
                        link(nc.vector.scalar_tensor_tensor(x, t, -TWO_PI_LO, x, ALU.mult, ALU.add))

                    def clip(x):
                        return nc.vector.tensor_scalar(x, x, PI_SAFE, -PI_SAFE, ALU.min, ALU.max)

                    def combine(out, tm, p1, a1, p2, a2, op):
                        tt(out, p1, a1, ALU.mult)
                        tt(tm, p2, a2, ALU.mult)
                        return nc.vector.tensor_tensor(out, out, tm, op)

                    s_ = {n: a[:, :] for n, a in small.items()}
                    w_ = {n: a[:, :, :] for n, a in pw.items()}

                    def powers_of(u):
                        s, w = s_, w_
                        dve.wait_ge(par_loaded, 32 * (u + 1))
                        dve.wait_ge(dt_done, u + 1)
                        tt(s["ldt"], ldr, s["dt"], ALU.mult)
                        tt(s["th"], lim, s["dt"], ALU.mult)
                        reduce_angle(s["th"], s["t0"])
                        shape = (P, UG, NP)
                        pj = powers[:, :].unsqueeze(1).to_broadcast(shape)
                        tt(w["x"], s["th"].unsqueeze(2).to_broadcast(shape), pj, ALU.mult)
                        reduce_angle(w["x"], w["t"])
                        link(clip(w["x"]))
                        nc.vector.tensor_tensor(w["t"], s["ldt"].unsqueeze(2).to_broadcast(shape), pj,
                                                ALU.mult).then_inc(pow_ready, 1)

                    def matrices(u):
                        s, w = s_, w_
                        dve.wait_ge(pow_done, 3 * (u + 1))
                        tt(w["cos"], w["cos"], w["cos"], ALU.mult)
                        ts(w["cos"], w["cos"], -2.0, 1.0, ALU.mult, ALU.add)
                        tt(w["ar"], w["mag"], w["cos"], ALU.mult)
                        tt(w["ai"], w["mag"], w["sin"], ALU.mult)
                        ts(w["sar"], w["ar"], sign[:, 0:1], None, ALU.mult)
                        ts(w["sai"], w["ai"], sign[:, 0:1], None, ALU.mult)
                        ts(w["nai"], w["ai"], -1.0, None, ALU.mult)
                        if u:
                            dve.wait_ge(m8_kept, 16 * u)
                        link(nc.vector.tensor_copy(m8[:, :], pw["mag"][:, :, CH]))
                        ar1, ai1 = pw["ar"][:, :, 1], pw["ai"][:, :, 1]
                        tt(s["den"], ldr, ldr, ALU.mult)
                        tt(s["t0"], lim, lim, ALU.mult)
                        tt(s["den"], s["den"], s["t0"], ALU.add)
                        link(nc.vector.reciprocal(s["den"], s["den"]))
                        ts(s["nr"], ar1, -1.0, None, ALU.add)
                        tt(s["t0"], s["nr"], ldr, ALU.mult)
                        tt(s["t1"], ai1, lim, ALU.mult)
                        tt(s["t0"], s["t0"], s["t1"], ALU.add)
                        tt(s["fr"], s["t0"], s["den"], ALU.mult)
                        tt(s["t0"], ai1, ldr, ALU.mult)
                        tt(s["t1"], s["nr"], lim, ALU.mult)
                        tt(s["t0"], s["t0"], s["t1"], ALU.subtract)
                        tt(s["t0"], s["t0"], s["den"], ALU.mult)
                        ts(s["sfi"], s["t0"], sign[:, 0:1], None, ALU.mult)
                        ts(s["sph"], pw["x"][:, :, CH], sign[:, 0:1], None, ALU.mult)
                        sh = (P, UG, HG)
                        fr, sfi = (s[a].unsqueeze(2).to_broadcast(sh) for a in ("fr", "sfi"))
                        t3 = tmp[:, :, 0, :]
                        link(combine(bb[:, :, :], t3, fr, bc[2], sfi, bc[3], ALU.subtract))
                        link(combine(bbs[:, :, :], t3, fr, bc[3], sfi, bc[2], ALU.add))
                        if u:
                            dve.wait_ge(ca_kept, 32 * u)
                        sh = (P, UG, CH + 1, HG)
                        cv = [a.unsqueeze(2).to_broadcast(sh) for a in bc[0:2]]
                        pf = {a: pw[a][:, :, 0:CH + 1].unsqueeze(3).to_broadcast(sh) for a in ("sar", "nai")}
                        link(combine(cas[:, :, :, :], tmp[:, :, :, :], pf["nai"], cv[0], pf["sar"], cv[1],
                                     ALU.subtract))
                        combine(ca[:, :, :, :], tmp[:, :, :, :], pf["sar"], cv[0], pf["nai"], cv[1],
                                ALU.add).then_inc(ca_ready, 1)

                    def transposable(u):
                        dve.wait_ge(ca_ready, u + 1)
                        if u:
                            dve.wait_ge(bt_mm, 2 * u)
                        sh = (P, UG, CH, HG)
                        bv = [a[:, :, :].unsqueeze(2).to_broadcast(sh) for a in (bb, bbs)]
                        pf = {a: pw[a][:, :, CH + 1:NP].unsqueeze(3).to_broadcast(sh) for a in ("ar", "sai")}
                        tm = tmp[:, :, 0:CH, :]
                        link(combine(ba[:, :, :, :], tm, pf["ar"], bv[0], pf["sai"], bv[1], ALU.subtract))
                        combine(bas[:, :, :, :], tm, pf["ar"], bv[1], pf["sai"], bv[0],
                                ALU.add).then_inc(ba_ready, 1)

                    def angles(u, half):
                        for g in (2 * half, 2 * half + 1):
                            x = tx[:, g % 2, :]
                            if u or half:
                                dve.wait_ge(cs_done, 2 * (UG * u + g - 1))
                            ts(x, steps[:, :], small["sph"][:, g:g + 1], None, ALU.mult)
                            reduce_angle(x, tmp[:, :, :, :].rearrange("p g j h -> p (g j h)")[:, 0:NC])
                            clip(x).then_inc(ang_ready, 1)

                    def cosines(u, half):
                        dve.wait_ge(cs_done, 2 * (UG * u + 2 * half + 2))
                        c = cs[:, :, 0, :]
                        tt(c, c, c, ALU.mult)
                        nc.vector.tensor_scalar(c, c, -2.0, 1.0, ALU.mult, ALU.add).then_inc(cs_ready, 1)

                    def response(u):
                        dve.wait_ge(k_mm, u + 1)
                        if u:
                            dve.wait_ge(k_kept, 16 * CH * u)
                        kp = kpad[:, :, (CH - 1) * HG:]
                        idb = ident[0:HG, 0:HG].unsqueeze(1).to_broadcast((HG, UG, HG))
                        tt(dpar[:, :, :], dpar[:, :, :], idb, ALU.mult)
                        nc.vector.tensor_copy(kp, psum[7][0:HG, :].rearrange("p (g c) -> p g c", g=UG)).then_inc(k_out, 1)
                        dve.wait_ge(k_out, u + 1)
                        nc.vector.tensor_tensor(kp[:, :, 0:HG], kp[:, :, 0:HG], dpar[:, :, :], ALU.add).then_inc(k_ready, 1)

                    def turned_inputs(u):
                        if u:
                            dve.wait_ge(m3_kept, 32 * u)
                        for half in range(2):
                            dve.wait_ge(bt_mm, 2 * u + half + 1)
                            nc.vector.tensor_copy(m3[:, half, :, :].rearrange("p g c -> p (g c)"),
                                                  psum[6 + half][:, :]).then_inc(m3_half, 1)
                        dve.wait_ge(m3_half, 2 * u + 2)

                    def table_window(m, slot):
                        u, part = unit_of(m, -2)
                        if u is not None and (part, slot) == (0, 0):
                            turned_inputs(u)
                            cosines(u, 1)
                        u, part = unit_of(m)
                        if u is None:
                            return
                        if (part, slot) == (0, 0):
                            powers_of(u)
                        elif (part, slot) == (0, 1):
                            matrices(u)
                        elif (part, slot) == (1, 0):
                            response(u)
                            transposable(u)
                            angles(u, 0)
                        else:
                            cosines(u, 0)
                            angles(u, 1)

                    for m in range(N_MAIN):
                        if m == M_TAB:
                            nc.vector.memset(kpad[:, :, :], 0.0).then_inc(tab, 1)
                            steps_done[0] += 1
                            dve.wait_ge(tab, steps_done[0])
                            dve.wait_ge(const_loaded, 16 * 9)
                        for s in range(2):
                            if m + 1 < N_MAIN:
                                done = products(m, 1 if kind_of[m] == "value" else s, NQ - 1)
                                split_pair(dve, NKV + m + 1, lambda s: (mm_done, done), slots=(s,))
                            table_window(m, s)

                @block.tensor
                def _(pe):
                    pe.wait_ge(consts, 2)

                    def sum_squares(j):
                        w = jobs[j][0]
                        if j >= 2:
                            pe.wait_ge(root_done, j - 1)
                        for k in range(KD):
                            pe.wait_ge(sq_ready, 8 * j + k + 1)
                            mm = nc.tensor.matmul(psum[2 + j % 2][:, 0:w], ones[:, :], sq[:, k % 4, 0:w],
                                                  start=(k == 0), stop=(k == KD - 1)).then_inc(sq_used, 1)

                    def memory_kv(n):
                        for s in range(2):
                            pe.wait_ge(w_split[s], n + 1)
                        mcol = L - CW
                        for s in range(2):
                            if n < 2:
                                pairs = [(wt(s, k), (h_hi[:, k, mcol:mcol + ML], h_lo[:, k, mcol:mcol + ML]))
                                         for k in range(KD)]
                                out = psum[4 + n][:, ML * s:ML * (s + 1)]
                            else:
                                tok = slice(mcol + P * s, mcol + P * (s + 1))
                                pairs = [((h_hi[:, k, tok], h_lo[:, k, tok]), (w_hi[:, :, k, :], w_lo[:, :, k, :]))
                                         for k in range(KD)]
                                out = psum[4 + n][:, ML * s:ML * (s + 1)].rearrange("p (a b) -> p a b", a=2)
                            three_pass(out, pairs).then_inc(kv_mm, 1)

                    def table_window(m, s):
                        if s == 0:
                            return
                        u, part = unit_of(m)
                        if u is not None and part == 1:
                            pe.wait_ge(ca_ready, u + 1)
                            pe.wait_ge(bank_free, 8 * m)
                            for g in range(UG):
                                mm = nc.tensor.matmul(psum[7][0:HG, P * g:P * (g + 1)], bb[:, g, :],
                                                      ca[:, g, 0:CH, :], start=True, stop=True)
                            mm.then_inc(k_mm, 1)
                        u, part = unit_of(m, -2)
                        if u is not None and part == 0:
                            pe.wait_ge(ba_ready, u + 1)
                            pe.wait_ge(bank_free, 8 * m)
                            for half, b in ((0, ba), (1, bas)):
                                for g in range(UG):
                                    mm = nc.tensor.transpose(psum[6 + half][:, P * g:P * (g + 1)],
                                                             b[:, g, :, :].rearrange("p s h -> p (s h)"), ident[:, :])
                                mm.then_inc(bt_mm, 1)

                    def table_banks_free(m):
                        u, part = unit_of(m)
                        if u is not None and part == 1:
                            pe.wait_ge(k_out, u + 1)
                        u, part = unit_of(m, -2)
                        if u is not None and part == 0:
                            pe.wait_ge(m3_half, 2 * u + 2)

                    def first_pair(s, c):
                        assert segments[0][0] == "copy"
                        pe.wait_ge(w_split[s], NKV + 1)
                        pe.wait_ge(h_ready, 2 * (c + 2))
                        if s == 0 and c >= 2:
                            pe.wait_ge(root_done, len(jobs))
                        if s == 1:
                            pe.wait_ge(kv_out, 2 * (c + 1))
                        cols = slice(CW * c, CW * (c + 1))
                        three_pass(psum[4 * s + c][:, :], [(wt(s, k), (h_hi[:, k, cols], h_lo[:, k, cols]))
                                                           for k in range(KD)]).then_inc(mm_done, 1)

                    sum_squares(0)
                    sum_squares(1)
                    pe.wait_ge(h_ready, 2)
                    memory_kv(0)
                    memory_kv(1)
                    sum_squares(2)
                    memory_kv(2)
                    memory_kv(3)
                    sum_squares(3)
                    first_pair(0, 0)
                    sum_squares(4)
                    first_pair(1, 0)
                    for c in range(1, NQ):
                        for s in range(2):
                            first_pair(s, c)
                    for kind, m0, n, tiles, r in segments:
                        for i in range(n):
                            m = m0 + i
                            if m == 0:
                                continue
                            for s in range(2):
                                table_window(m, s)
                                pe.wait_ge(w_split[s], NKV + m + 1)
                                if kind == "value":
                                    pe.wait_ge(w_split[1], NKV + m + 1)
                                for c in range(NQ):
                                    pe.wait_ge(bank_free, 8 * (m - 1) + 4 * s + c + 1)
                                    if s == 1 and c == 2:
                                        table_banks_free(m)
                                    bank = psum[4 * s + c]
                                    if kind != "value":
                                        cols = slice(CW * c, CW * (c + 1))
                                        mm = three_pass(bank[:, :], [(wt(s, k), (h_hi[:, k, cols], h_lo[:, k, cols]))
                                                                     for k in range(KD)])
                                        mm.then_inc(mm_done, 1)
                                        continue
                                    for half in range(2):
                                        b = 2 * (4 * s + c) + half
                                        res, blk = divmod(b, NBLK // r)
                                        first = res + r * P * blk
                                        tok = slice(first, first + r * (P - 1) + 1, r)
                                        out = bank[:, 256 * half:256 * (half + 1)].rearrange(
                                            "p (a b) -> p a b", a=2)
                                        mm = three_pass(out, [((h_hi[:, k, tok], h_lo[:, k, tok]),
                                                               (w_hi[:, :, k, :], w_lo[:, :, k, :]))
                                                              for k in range(KD)])
                                    mm.then_inc(mm_done, 1)

        mats_loaded = [sem(f"mats_loaded{i}") for i in range(4)]
        ub_loaded = [sem(f"ub_loaded{i}") for i in range(3)]
        bias_in, bias_rows, bias_neg, bias_kept, bias_loaded, bias_turned, bias_copied, first_mask = (sem(a) for a in (
            "bias_in", "bias_rows", "bias_neg", "bias_kept", "bias_loaded", "bias_turned", "bias_copied",
            "first_mask"))
        v_mm, turned, w_sum, scanned, state_done, y_mm, y_out_done = (sem(a) for a in (
            "v_mm", "turned", "w_sum", "scanned", "state_done", "y_mm", "y_out_done"))
        ys_stored = [sem(f"ys_stored{i}") for i in range(2)]
        PLOADS = 3
        space = sb(ctx, "space", [P, 6144])
        bias = space[:, :].rearrange("p (h a k) -> p h a k", h=NH, a=2)
        mirrored = bias[:, :, 0, :]
        with ExitStack() as ph:
            bk = sb(ph, "bk", [NBUCKET + 1, 3, 384])
            rel = sb(ph, "rel", [NBUCKET + 1, NH])
            brow = sb(ph, "brow", [NH, 3, 384])
            anti = sb(ph, "anti", [P, P])
            mats = sb(ph, "mats", [P, 2, GB, 5, P])
            csb = sb(ph, "csb", [P, 2, GB, 2, NC])
            m8b = sb(ph, "m8b", [P, 2, GB])
            ub = sb(ph, "ub", [P, 3, GB, NC])
            yb = sb(ph, "yb", [P, 2, GB, NC])
            tv = sb(ph, "tv", [P, 4, 2, NC])
            wv = sb(ph, "wv", [P, 4, NC])
            zv = sb(ph, "zv", [P, 4, NC])
            xz = sb(ph, "xz", [P, 4, 2, NC])
            R = 4

            with nc.Block() as block:
                @block.sync
                def _(sp):
                    sp.dma_start(bk[:, :, :], buckets).then_inc(bias_in, 16)
                    sp.dma_start(rel[0:NBUCKET, :], rel_bias).then_inc(bias_in, 16)
                    sp.dma_start(anti[:, :], anti_c).then_inc(bias_in, 16)
                    for b in range(NB):
                        if b >= 3:
                            sp.wait_ge(y_mm, GB * (b - 2))
                        src = proj_d[T_U + b].rearrange("(g h) (s c) -> s h g c", g=GB, s=CH)
                        for t in range(CH):
                            sp.dma_start(ub[HG * t:HG * (t + 1), b % 3, :, :], src[t]).then_inc(ub_loaded[b % 3], 16)
                        for part in range(2):
                            i, gs = b % 2, slice(UG * part, UG * (part + 1))
                            if b >= 2:
                                sp.wait_ge(y_mm, GB * (b - 2) + UG * (part + 1))
                            loaded = mats_loaded[2 * i + part]
                            sp.dma_start(mats[:, i, gs, :, :], mats_d[2 * b + part]).then_inc(loaded, 16)
                            sp.dma_start(csb[:, i, gs, :, :], cs_d[2 * b + part]).then_inc(loaded, 16)
                            sp.dma_start(m8b[:, i, gs], m8_d[2 * b + part]).then_inc(loaded, 16)
                    sp.wait_ge(bias_neg, 3)
                    for g in range(3):
                        sp.dma_start(bias_d[g], brow[:, g, :]).then_inc(bias_kept, 16)
                    sp.wait_ge(bias_kept, 48)
                    for h in range(NH):
                        row = bias_d[h // HPG, h]
                        src = bass.AP(row.tensor, row.offset, [[1, P], [1, 256]])
                        sp.dma_start(mirrored[:, h, :], src).then_inc(bias_loaded, 16)

                @block.gpsimd
                def _(pool):
                    nc.gpsimd.memset(rel[NBUCKET:NBUCKET + 1, :], 1.0).then_inc(first_mask, 1)
                    for q in range(G):
                        pool.wait_ge(turned, q + 1)
                        if q >= R:
                            pool.wait_ge(scanned, q - R + 1)
                        nc.gpsimd.tensor_tensor(wv[:, q % R, :], tv[:, q % R, 0, :], tv[:, q % R, 1, :],
                                                ALU.add).then_inc(w_sum, 1)
                    pool.wait_ge(bias_turned, NH // 2)
                    nc.gpsimd.memset(bias[:, :, 0, 0:P], BIG).then_inc(first_mask, 1)

                @block.vector
                def _(dve):
                    def half_loaded(q):
                        b, part = q // GB, q // UG % 2
                        dve.wait_ge(mats_loaded[2 * (b % 2) + part], 16 * PLOADS * (b // 2 + 1))

                    for g in range(3):
                        dve.wait_ge(bias_rows, g + 1)
                        nc.vector.tensor_scalar(brow[:, g, :], psum[g][0:NH, 0:384], -1.0, None,
                                                ALU.mult).then_inc(bias_neg, 1)
                    for q in range(G + 2):
                        if q < G:
                            if q % UG == 0:
                                half_loaded(q)
                            dve.wait_ge(v_mm, q + 1)
                            if q >= R:
                                dve.wait_ge(w_sum, q - R + 1)
                            nc.vector.tensor_tensor(tv[:, q % R, :, :],
                                                    psum[q % 4][:, :].rearrange("p (a c) -> p a c", a=2),
                                                    csb[:, q // GB % 2, q % GB, :, :], ALU.mult).then_inc(turned, 1)
                        if q >= 2:
                            g = q - 2
                            dve.wait_ge(w_sum, g + 1)
                            if g >= R:
                                dve.wait_ge(state_done, g - R + 1)
                            m = m8b[:, g // GB % 2, g % GB:g % GB + 1].to_broadcast((P, NC))
                            nc.vector.tensor_tensor_scan(zv[:, g % R, :], m, wv[:, g % R, :], 0.0,
                                                         ALU.mult, ALU.add).then_inc(scanned, 1)
                            dve.wait_ge(scanned, g + 1)
                            if g >= R:
                                dve.wait_ge(y_mm, g - R + 1)
                            z = zv[:, g % R, :].unsqueeze(1).to_broadcast((P, 2, NC))
                            nc.vector.tensor_tensor(xz[:, g % R, :, :], csb[:, g // GB % 2, g % GB, :, :], z,
                                                    ALU.mult).then_inc(state_done, 1)
                    for n in range(NH // 2):
                        dve.wait_ge(bias_turned, n + 1)
                        src = psum[n % 4][:, :].rearrange("p (a k) -> p a k", a=2)
                        nc.vector.tensor_copy(bias[:, 2 * n:2 * n + 2, 1, :], src).then_inc(bias_copied, 1)
                    dve.wait_ge(bias_copied, NH // 2)
                    nc.vector.tensor_copy(bias[:, :, 0, P:2 * P], bias[:, :, 1, P:2 * P]).then_inc(bias_copied, 1)

                @block.tensor
                def _(pe):
                    pe.wait_ge(bias_in, 48)
                    pe.wait_ge(first_mask, 1)
                    for g in range(3):
                        nc.tensor.matmul(psum[g][0:NH, 0:384], rel[:, :], bk[:, g, :], start=True,
                                         stop=True).then_inc(bias_rows, 1)
                    LAG = 3
                    for q in range(G + LAG):
                        if q < G:
                            b, g = divmod(q, GB)
                            if g == 0:
                                pe.wait_ge(ub_loaded[b % 3], 16 * CH * (b // 3 + 1))
                            if g % UG == 0:
                                pe.wait_ge(mats_loaded[2 * (b % 2) + g // UG], 16 * PLOADS * (b // 2 + 1))
                            if q < 3:
                                pe.wait_ge(bias_neg, q + 1)
                            if q >= R:
                                pe.wait_ge(turned, q - R + 1)
                            for half in range(2):
                                mm = nc.tensor.matmul(psum[q % 4][:, NC * half:NC * (half + 1)],
                                                      mats[:, b % 2, g, half, :], ub[:, b % 3, g, :],
                                                      start=True, stop=True)
                            mm.then_inc(v_mm, 1)
                        if q >= LAG:
                            q2 = q - LAG
                            b, g = divmod(q2, GB)
                            if q2 >= R:
                                pe.wait_ge(y_out_done, q2 - R + 1)
                            y = psum[4 + q2 % 4]
                            nc.tensor.matmul(y[:, 0:NC], mats[:, b % 2, g, 4, :], ub[:, b % 3, g, :],
                                             start=True, stop=False)
                            pe.wait_ge(state_done, q2 + 1)
                            for part in range(2):
                                mm = nc.tensor.matmul(y[:, 1:NC], mats[:, b % 2, g, 2 + part, :],
                                                      xz[:, q2 % R, part, 0:NC - 1], start=False, stop=(part == 1))
                            mm.then_inc(y_mm, 1)
                    pe.wait_ge(bias_loaded, 16 * NH)
                    pe.wait_ge(turned, G)
                    for n in range(NH // 2):
                        if n >= 4:
                            pe.wait_ge(bias_copied, n - 3)
                        nc.tensor.matmul(psum[n % 4][:, :].rearrange("p (a k) -> p a k", a=2), anti[:, :],
                                         mirrored[:, 2 * n:2 * n + 2, :], start=True, stop=True).then_inc(
                                             bias_turned, 1)

                @block.scalar
                def _(act):
                    for b in range(NB):
                        for g in range(GB):
                            q = GB * b + g
                            act.wait_ge(y_mm, q + 1)
                            if g == 0 and b >= 2:
                                act.wait_ge(ys_stored[b % 2], 16 * CH * (b // 2))
                            nc.scalar.activation(yb[:, b % 2, g, :], psum[4 + q % 4][:, 0:NC],
                                                 ACT.Gelu_apprx_tanh).then_inc(y_out_done, 1)
                        act.wait_ge(y_out_done, GB * (b + 1))
                        dst = ys_d[b].rearrange("(g h) (s c) -> s h g c", g=GB, s=CH)
                        for t in range(CH):
                            act.dma_start(dst[t], yb[HG * t:HG * (t + 1), b % 2, :, :]).then_inc(ys_stored[b % 2], 16)
                    for i in range(2):
                        act.wait_ge(ys_stored[i], 16 * CH * (NB // 2))

        SCALE = HD ** -0.5
        batches = []
        for h in range(NH):
            g = h // HPG
            per = 4 if g == 2 else 2
            for b in range(0, NBLK, per):
                batches.append((h, g, list(range(b, b + per)), 512 // per))
        NT_B = len(batches)
        qk_loaded = [sem(f"qk_loaded{i}") for i in range(2)]
        vg_loaded = [sem(f"vg_loaded{i}") for i in range(2)]
        s_mm, s_biased, s_min, e_done, t_mm, t_out, o_mm, o_out = (sem(a) for a in (
            "s_mm", "s_biased", "s_min", "e_done", "t_mm", "t_out", "o_mm", "o_out"))
        st_mm, st_out, st_kept = sem("st_mm"), sem("st_out"), sem("st_kept")

        with ExitStack() as ph:
            oT = sb(ph, "oT", [P, NH // 2, L])
            with ExitStack() as pa:
                qk = sb(pa, "qk", [P, 2, 2, L])
                vg = sb(pa, "vg", [P, 2, NBLK, HPG * HD])
                tsc = sb(pa, "tsc", [P, 3, 512])
                esc = sb(pa, "esc", [P, 3, 512])
                ptr = sb(pa, "ptr", [P, 3, 512])
                stat = sb(pa, "stat", [P, 2, NH * NBLK])
                strow = sb(pa, "strow", [P, 4, P])

                def has_prev(g, b):
                    return b % (NBLK // DIL[g]) != 0

                with nc.Block() as block:
                    @block.sync
                    def _(sp):
                        for pair in range(2):
                            for a, t in enumerate((T_Q, T_K)):
                                sp.dma_start(qk[:, pair, a, :], proj_d[t + pair]).then_inc(qk_loaded[pair], 16)
                        sp.dma_start(vg[:, 0, :, :].rearrange("p b c -> p (b c)"), v_d[0]).then_inc(vg_loaded[0], 16)
                        sp.dma_start(vg[:, 1, :, :].rearrange("p b c -> p (b c)"), v_d[1]).then_inc(vg_loaded[1], 16)
                        for pair in range(2, NH // 2):
                            n = sum(1 for b in batches if b[0] < 2 * (pair - 1))
                            sp.wait_ge(s_mm, n)
                            for a, t in enumerate((T_Q, T_K)):
                                sp.dma_start(qk[:, pair % 2, a, :], proj_d[t + pair]).then_inc(
                                    qk_loaded[pair % 2], 16)
                            if pair == 4:
                                sp.wait_ge(o_mm, HPG * NBLK // 2)
                                sp.dma_start(vg[:, 0, :, :].rearrange("p b c -> p (b c)"), v_d[2]).then_inc(
                                    vg_loaded[0], 16)
                        sp.wait_ge(st_out, 1)
                        for w in range(2):
                            sp.dma_start(st_d[w, 0:P, :], strow[:, 2 * w, :]).then_inc(st_kept, 16)
                            sp.dma_start(st_d[w, P:NH * NBLK, :], strow[0:NH * NBLK - P, 2 * w + 1, :]).then_inc(
                                st_kept, 16)
                        sp.wait_ge(st_kept, 64)

                    @block.tensor
                    def _(pe):
                        def scores(t):
                            h, g, blocks, nk = batches[t]
                            pair, half = divmod(h, 2)
                            rows = slice(64 * half, 64 * half + 64)
                            pe.wait_ge(qk_loaded[pair % 2], 32 * (pair // 2 + 1))
                            if t >= 2:
                                pe.wait_ge(s_biased, t - 1)
                            q, k = qk[rows, pair % 2, 0, :], qk[rows, pair % 2, 1, :]
                            for i, b in enumerate(blocks):
                                lhs = q[:, P * b:P * (b + 1)]
                                out = psum[t % 2][:, nk * i:nk * (i + 1)]
                                if nk == 128 or has_prev(g, b):
                                    mm = nc.tensor.matmul(out, lhs, k[:, P * (b + 1) - nk:P * (b + 1)],
                                                          start=True, stop=True)
                                else:
                                    for part in range(2):
                                        mm = nc.tensor.matmul(out[:, P * part:P * (part + 1)], lhs,
                                                              k[:, P * b:P * (b + 1)], start=True, stop=True)
                            mm.then_inc(s_mm, 1)

                        def turn(t):
                            pe.wait_ge(e_done, sum(len(b[2]) for b in batches[:t + 1]))
                            if t >= 2:
                                pe.wait_ge(t_out, t - 1)
                            for i in range(4):
                                mm = nc.tensor.transpose(psum[2 + t % 2][:, P * i:P * (i + 1)],
                                                         esc[:, t % 3, P * i:P * (i + 1)], ident[:, :])
                            mm.then_inc(t_mm, 1)

                        def output(t):
                            h, g, blocks, nk = batches[t]
                            rows = slice(64 * (h % 2), 64 * (h % 2) + 64)
                            pe.wait_ge(vg_loaded[g % 2], 16 * (g // 2 + 1))
                            pe.wait_ge(t_out, t + 1)
                            bank = (h * NBLK + blocks[0]) // 4
                            if blocks[0] % 4 == 0 and bank >= 4:
                                pe.wait_ge(o_out, bank - 3)
                            for i, b in enumerate(blocks):
                                out = psum[4 + bank % 4][rows, P * (b % 4):P * (b % 4 + 1)]
                                parts = [1] if nk == 256 else [0]
                                if nk == 256 and has_prev(g, b):
                                    parts = [0, 1]
                                for part in parts:
                                    kb = b - 1 + part if nk == 256 else b
                                    e = ptr[:, t % 3, nk * i + P * part:nk * i + P * (part + 1)]
                                    mm = nc.tensor.matmul(out, vg[:, g % 2, kb, HD * (h % HPG):HD * (h % HPG + 1)], e,
                                                          start=(part == parts[0]), stop=(part == parts[-1]))
                            mm.then_inc(o_mm, 1)

                        for t in range(NT_B + 4):
                            if t < NT_B:
                                scores(t)
                            if 0 <= t - 2 < NT_B:
                                turn(t - 2)
                            if 0 <= t - 3 < NT_B:
                                output(t - 3)
                        pe.wait_ge(o_out, NH * NBLK // 4)
                        for w in range(2):
                            nc.tensor.transpose(psum[0][:, 2 * w * P:(2 * w + 1) * P], stat[:, w, 0:P], ident[:, :])
                            mm = nc.tensor.transpose(psum[0][0:NH * NBLK - P, (2 * w + 1) * P:(2 * w + 2) * P],
                                                     stat[:, w, P:NH * NBLK], ident[:, :])
                        mm.then_inc(st_mm, 1)

                    @block.vector
                    def _(dve):
                        def negate_and_min(t):
                            h, g, blocks, nk = batches[t]
                            n = len(blocks)
                            dve.wait_ge(s_mm, t + 1)
                            if t >= 3:
                                dve.wait_ge(e_done, sum(len(b[2]) for b in batches[:t - 2]))
                            out = tsc[:, t % 3, :].rearrange("p (n k) -> p n k", n=n)
                            sc = psum[t % 2][:, :].rearrange("p (n k) -> p n k", n=n)
                            if nk == 128:
                                bi = bias[:, h, 1, 128:256].unsqueeze(1).to_broadcast((P, n, nk))
                            elif has_prev(g, blocks[0]):
                                bi = bias[:, h, 1, :].unsqueeze(1).to_broadcast((P, n, nk))
                            else:
                                bi = bias[:, h, :, :]
                            nc.vector.scalar_tensor_tensor(out, sc, -SCALE, bi, ALU.mult,
                                                           ALU.add).then_inc(s_biased, 1)
                            dve.wait_ge(s_biased, t + 1)
                            at = h * NBLK + blocks[0]
                            nc.vector.tensor_reduce(stat[:, 0, at:at + n], out, AX.X, ALU.min).then_inc(s_min, 1)

                        def keep_turned(t):
                            dve.wait_ge(t_mm, t + 1)
                            if t >= 3:
                                dve.wait_ge(o_mm, t - 2)
                            nc.vector.tensor_copy(ptr[:, t % 3, :], psum[2 + t % 2][:, :]).then_inc(t_out, 1)

                        for t in range(NT_B + 2):
                            if t < NT_B:
                                negate_and_min(t)
                            if t >= 2:
                                keep_turned(t - 2)
                        dve.wait_ge(st_mm, 1)
                        nc.vector.tensor_copy(strow[:, :, :].rearrange("p a b -> p (a b)"),
                                              psum[0][:, :]).then_inc(st_out, 1)

                    @block.scalar
                    def _(act):
                        def exponentials(t):
                            h, g, blocks, nk = batches[t]
                            act.wait_ge(s_min, t + 1)
                            if t >= 3:
                                act.wait_ge(t_mm, t - 2)
                            for i, b in enumerate(blocks):
                                at = h * NBLK + b
                                nc.scalar.activation(esc[:, t % 3, nk * i:nk * (i + 1)],
                                                     tsc[:, t % 3, nk * i:nk * (i + 1)], ACT.Exp,
                                                     bias=stat[:, 0, at:at + 1], scale=-1.0,
                                                     accum_out=stat[:, 1, at:at + 1]).then_inc(e_done, 1)

                        def keep_output(bank, batch):
                            h, b4 = divmod(bank, NBLK // 4)
                            g, r = h // HPG, DIL[h // HPG]
                            rows = slice(64 * (h % 2), 64 * (h % 2) + 64)
                            act.wait_ge(o_mm, batch + 1)
                            src = psum[4 + bank % 4][rows, :]
                            dst = oT[rows, h // 2, :]
                            if r == 1:
                                dst = dst[:, CW * b4:CW * (b4 + 1)]
                            elif r == 4:
                                dst = dst.rearrange("p (m r) -> p r m", r=r)[:, b4, :]
                            else:
                                dst = dst.rearrange("p (m r) -> p r m", r=r)[:, 4 * b4:4 * b4 + 4, :]
                                src = src.rearrange("p (r m) -> p r m", r=4)
                            nc.scalar.activation(dst, src, ACT.Copy).then_inc(o_out, 1)

                        kept = 0
                        for t in range(NT_B + 4):
                            if t < NT_B:
                                exponentials(t)
                            if t >= 4:
                                h, g, blocks, nk = batches[t - 4]
                                if blocks[-1] % 4 == 3:
                                    keep_output(kept, t - 4)
                                    kept += 1

            yr_loaded = [sem(f"yr_loaded{c}") for c in range(NQ)]
            N_GLU = NKV + N_MAIN
            y_ahead = space[:, :].rearrange("p (c k t) -> p c k t", c=2, k=KS)

            def load_y(sp, c, dst):
                src = ys_d[:, :, CW * c:CW * (c + 1)].rearrange("k p t -> p k t")
                sp.dma_start(dst, src).then_inc(yr_loaded[c], 16)

            cmb_loaded, cmb, cmb_exp, f_kept = sem("cmb_loaded"), sem("cmb"), sem("cmb_exp"), sem("f_kept")
            fz_loaded = [sem(f"fz_loaded{i}") for i in range(2)]
            weighted, gated, oa_kept = sem("weighted"), sem("gated"), sem("oa_kept")
            MSCALE = MD ** -0.5
            T_CMB = 3
            MB = L // (2 * P)
            qm_loaded = [sem(f"qm_loaded{i}") for i in range(2)]
            zm_loaded = [sem(f"zm_loaded{i}") for i in range(2)]
            om_kept = [sem(f"om_kept{i}") for i in range(2)]
            ms_mm, m_max, m_bias, m_exp, m_rec, m_norm, mt_mm, mt_out, mo_mm, mo_out = (sem(a) for a in (
                "ms_mm", "m_max", "m_bias", "m_exp", "m_rec", "m_norm", "mt_mm", "mt_out", "mo_mm", "mo_out"))
            with ExitStack() as pb:
                R64 = HPG * NBLK
                sraw = sb(pb, "sraw", [R64, 3, 2, P])
                sm = sb(pb, "sm", [R64, 3, 2, P])
                mn = sb(pb, "mn", [R64, P])
                fe = sb(pb, "fe", [R64, 3, P])
                el = sb(pb, "el", [R64, 3, P])
                fb = sb(pb, "fb", [P, 2, L])
                zb = sb(pb, "zb", [P, 2, L])
                qm = sb(pb, "qm", [P, 2, L])
                zm = sb(pb, "zm", [P, 2, L])
                mx = sb(pb, "mx", [P, 4, 2])
                nb = sb(pb, "nb", [P, 4, 2])
                ls = sb(pb, "ls", [P, 4, 2])
                rl = sb(pb, "rl", [P, 4, 2])
                em = sb(pb, "em", [P, 4, 2, ML])
                pt = sb(pb, "pt", [P, 3, 2, 2 * P])
                NT_M = MH * MB
                with nc.Block() as block:
                    @block.sync
                    def _(sp):
                        st_rows = st_d.rearrange("w (h b) c -> w h (b c)", b=NBLK)
                        for g, r in enumerate(DIL):
                            for w in range(2):
                                for j in range(HPG):
                                    src = st_rows[w, HPG * g + j].rearrange("(r a m) -> a r m", r=r, a=NBLK)
                                    dst = sraw[NBLK * j:NBLK * (j + 1), g, w, :].rearrange("p (r m) -> p r m", r=r)
                                    sp.dma_start(dst, src).then_inc(cmb_loaded, 16)
                        for pair in range(2):
                            sp.dma_start(zb[:, pair, :], proj_d[T_ZA + pair]).then_inc(fz_loaded[pair], 16)
                        sp.wait_ge(cmb, 11)
                        for g in range(3):
                            sp.dma_start(f_d[g].rearrange("j a c -> (j a) c"), fe[:, g, :]).then_inc(f_kept, 16)
                        sp.wait_ge(f_kept, 48)
                        load_pair(sp, N_GLU, w_glu[0], w_glu[1], KS)
                        for c in range(2):
                            load_y(sp, c, y_ahead[:, c, :, :])
                        for pair in range(NH // 2 + 1):
                            if pair < NH // 2:
                                i = pair % 2
                                if pair >= 2:
                                    sp.dma_start(zb[:, i, :], proj_d[T_ZA + pair]).then_inc(fz_loaded[i], 16)
                                for half in range(2):
                                    g, j = divmod(2 * pair + half, HPG)
                                    src = f_d[g, j].rearrange("a c -> (a c)").partition_broadcast(64)
                                    sp.dma_start(fb[64 * half:64 * half + 64, i, :], src).then_inc(fz_loaded[i], 16)
                            if pair:
                                sp.wait_ge(gated, 2 * pair)
                                sp.dma_start(o_d[6 + pair - 1], oT[:, pair - 1, :]).then_inc(oa_kept, 16)
                        sp.wait_ge(oa_kept, 16 * (NH // 2))

                    @block.gpsimd
                    def _(pool):
                        for h in range(2):
                            pool.dma_start(qm[:, h, :], proj_d[T_QM + h]).then_inc(qm_loaded[h], 16)
                        for h in range(2):
                            pool.dma_start(zm[:, h, :], proj_d[T_ZM + h]).then_inc(zm_loaded[h], 16)
                        for h in range(MH):
                            i = h % 2
                            if h + 2 < MH:
                                pool.wait_ge(ms_mm, MB * (h + 1))
                                pool.dma_start(qm[:, i, :], proj_d[T_QM + h + 2]).then_inc(qm_loaded[i], 16)
                            for half in range(2):
                                cols = slice(half * L // 2, (half + 1) * L // 2)
                                pool.wait_ge(mo_out, MB * h + MB // 2 * (half + 1))
                                pool.dma_start(o_d[12 + h, :, cols], zm[:, i, cols]).then_inc(om_kept[i], 16)
                            if h + 2 < MH:
                                pool.wait_ge(om_kept[i], 32 * (h // 2 + 1))
                                pool.dma_start(zm[:, i, :], proj_d[T_ZM + h + 2]).then_inc(zm_loaded[i], 16)
                        for i in range(2):
                            pool.wait_ge(om_kept[i], 64)

                    @block.tensor
                    def _(pe):
                        def scores(t):
                            h, b = divmod(t, MB)
                            pe.wait_ge(qm_loaded[h % 2], 16 * (h // 2 + 1))
                            if t >= 2:
                                pe.wait_ge(m_exp, 2 * (t - 1))
                            for i in range(2):
                                q = qm[:, h % 2, P * (2 * b + i):P * (2 * b + i + 1)]
                                mm = nc.tensor.matmul(psum[t % 2][:, ML * i:ML * (i + 1)], q, k_mem[:, h, :],
                                                      start=True, stop=True)
                            mm.then_inc(ms_mm, 1)

                        def turn(t):
                            pe.wait_ge(m_norm, 2 * (t + 1))
                            if t >= 2:
                                pe.wait_ge(mt_out, t - 1)
                            for kb in range(2):
                                for i in range(2):
                                    mm = nc.tensor.transpose(psum[2 + t % 2][:, P * (2 * kb + i):P * (2 * kb + i + 1)],
                                                             em[:, t % 4, i, P * kb:P * (kb + 1)], ident[:, :])
                            mm.then_inc(mt_mm, 1)

                        def output(t):
                            h = t // MB
                            pe.wait_ge(mt_out, t + 1)
                            if t >= 2:
                                pe.wait_ge(mo_out, t - 1)
                            for kb in range(2):
                                mm = nc.tensor.matmul(psum[4 + t % 2][:, 0:2 * P], v_mem[:, kb, MD * h:MD * (h + 1)],
                                                      pt[:, t % 3, kb, :], start=(kb == 0), stop=(kb == 1))
                            mm.then_inc(mo_mm, 1)

                        for t in range(NT_M + 3):
                            if t < NT_M:
                                scores(t)
                            if 0 <= t - 2 < NT_M:
                                turn(t - 2)
                            if 0 <= t - 3 < NT_M:
                                output(t - 3)

                    @block.vector
                    def _(dve):
                        def maximum(t):
                            dve.wait_ge(ms_mm, t + 1)
                            nc.vector.tensor_reduce(mx[:, t % 4, :], psum[t % 2][:, :].rearrange("p (n k) -> p n k", n=2),
                                                    AX.X, ALU.max).then_inc(m_max, 1)
                            dve.wait_ge(m_max, t + 1)
                            if t >= 4:
                                dve.wait_ge(m_exp, 2 * (t - 3))
                            nc.vector.tensor_scalar(nb[:, t % 4, :], mx[:, t % 4, :], -MSCALE, None,
                                                    ALU.mult).then_inc(m_bias, 1)

                        def normalise(t):
                            dve.wait_ge(m_exp, 2 * (t + 1))
                            nc.vector.reciprocal(rl[:, t % 4, :], ls[:, t % 4, :]).then_inc(m_rec, 1)
                            dve.wait_ge(m_rec, t + 1)
                            for i in range(2):
                                nc.vector.tensor_scalar(em[:, t % 4, i, :], em[:, t % 4, i, :], rl[:, t % 4, i:i + 1],
                                                        None, ALU.mult).then_inc(m_norm, 1)

                        def gate(t):
                            h, b = divmod(t, MB)
                            dve.wait_ge(mo_mm, t + 1)
                            dve.wait_ge(zm_loaded[h % 2], 16 * (h // 2 + 1))
                            z = zm[:, h % 2, 2 * P * b:2 * P * (b + 1)]
                            nc.vector.tensor_tensor(z, psum[4 + t % 2][:, 0:2 * P], z, ALU.mult).then_inc(mo_out, 1)

                        def step(n, instruction):
                            instruction.then_inc(cmb, 1)
                            dve.wait_ge(cmb, n)

                        def exponents():
                            dve.wait_ge(cmb_loaded, 16 * 6 * HPG)
                            for g, r in enumerate(DIL):
                                step(g + 1, nc.vector.tensor_copy(
                                    sm[:, g, :, :].rearrange("p w (m r) -> p w r m", r=r),
                                    sraw[:, g, :, :].rearrange("p w (r m) -> p w r m", r=r)))
                            step(4, nc.vector.tensor_tensor(mn[:, :], sm[:, 0, 0, :], sm[:, 1, 0, :], ALU.min))
                            step(5, nc.vector.tensor_tensor(mn[:, :], mn[:, :], sm[:, 2, 0, :], ALU.min))
                            step(6, nc.vector.tensor_tensor(fe[:, :, :], mn[:, :].unsqueeze(1).to_broadcast((R64, 3, P)),
                                                            sm[:, :, 0, :], ALU.subtract))

                        def weights():
                            dve.wait_ge(cmb_exp, 1)
                            step(7, nc.vector.tensor_tensor(el[:, :, :], fe[:, :, :], sm[:, :, 1, :], ALU.mult))
                            step(8, nc.vector.tensor_tensor(mn[:, :], el[:, 0, :], el[:, 1, :], ALU.add))
                            step(9, nc.vector.tensor_tensor(mn[:, :], mn[:, :], el[:, 2, :], ALU.add))
                            step(10, nc.vector.reciprocal(mn[:, :], mn[:, :]))
                            step(11, nc.vector.tensor_tensor(fe[:, :, :], fe[:, :, :],
                                                             mn[:, :].unsqueeze(1).to_broadcast((R64, 3, P)), ALU.mult))

                        def weigh(pair, half):
                            i, cols = pair % 2, slice(half * L // 2, (half + 1) * L // 2)
                            if half == 0:
                                dve.wait_ge(fz_loaded[i], 48 * (pair // 2 + 1))
                            nc.vector.tensor_tensor(oT[:, pair, cols], oT[:, pair, cols], fb[:, i, cols],
                                                    ALU.mult).then_inc(weighted, 1)

                        def gate_pair(pair, half):
                            i, cols = pair % 2, slice(half * L // 2, (half + 1) * L // 2)
                            dve.wait_ge(weighted, 2 * pair + half + 1)
                            nc.vector.tensor_tensor(oT[:, pair, cols], oT[:, pair, cols], zb[:, i, cols],
                                                    ALU.mult).then_inc(gated, 1)

                        for t in range(NT_M + 4):
                            if t < NT_M:
                                maximum(t)
                            if 0 <= t - 1 < NT_M:
                                normalise(t - 1)
                            if 0 <= t - 4 < NT_M:
                                gate(t - 4)
                            if t in (6, 7):
                                split_pair(dve, N_GLU, lambda s: (mm_done, 8 * N_MAIN), KS, (t - 6,))
                            if t == T_CMB:
                                exponents()
                            if t == T_CMB + 1:
                                weights()
                            if t >= T_CMB + 9:
                                pair, part = divmod(t - T_CMB - 9, 4)
                                if pair < NH // 2:
                                    (weigh, gate_pair)[part // 2](pair, part % 2)

                    @block.scalar
                    def _(act):
                        def exponentials(t):
                            act.wait_ge(m_bias, t + 1)
                            if t >= 4:
                                act.wait_ge(mt_mm, t - 3)
                            for i in range(2):
                                nc.scalar.activation(em[:, t % 4, i, :], psum[t % 2][:, ML * i:ML * (i + 1)], ACT.Exp,
                                                     bias=nb[:, t % 4, i:i + 1], scale=MSCALE,
                                                     accum_out=ls[:, t % 4, i:i + 1]).then_inc(m_exp, 1)

                        def keep_turned(t):
                            act.wait_ge(mt_mm, t + 1)
                            if t >= 3:
                                act.wait_ge(mo_mm, t - 2)
                            nc.scalar.activation(pt[:, t % 3, :, :].rearrange("p a b -> p (a b)"), psum[2 + t % 2][:, :],
                                                 ACT.Copy).then_inc(mt_out, 1)

                        for t in range(NT_M + 2):
                            if t < NT_M:
                                exponentials(t)
                            if t == T_CMB:
                                act.wait_ge(cmb, 6)
                                nc.scalar.activation(fe[:, :, :], fe[:, :, :], ACT.Exp).then_inc(cmb_exp, 1)
                            if t >= 2:
                                keep_turned(t - 2)

        ys_hi_done, ys_split = sem("ys_hi_done"), sem("ys_split")
        g_mm, g_sig, g_y, g_z = sem("g_mm"), sem("g_sig"), sem("g_y"), sem("g_z")
        zs_loaded = [sem(f"zs_loaded{i}") for i in range(2)]
        os_kept = [sem(f"os_kept{i}") for i in range(2)]
        with ExitStack() as ph:
            ys_hi = sb(ph, "ys_hi", [P, KS, L], F32R)
            ys_lo = sb(ph, "ys_lo", [P, KS, L], F32R)
            yr = sb(ph, "yr", [P, 2, KS, CW])
            sg = sb(ph, "sg", [P, 2, CW])
            zs = sb(ph, "zs", [P, 2, L])

            def y_chunk(c):
                return y_ahead[:, c, :, :] if c < 2 else yr[:, c - 2, :, :]

            with nc.Block() as block:
                @block.sync
                def _(sp):
                    for c in (2, 3):
                        load_y(sp, c, yr[:, c - 2, :, :])
                    for pair in (1, 2):
                        load_pair(sp, N_GLU + pair, w_glu[2 * pair], w_glu[2 * pair + 1], KS)
                    load_pair(sp, N_GLU + 3, w_br[0, 0], w_br[0, 1])

                @block.gpsimd
                def _(pool):
                    for n in range(2):
                        pool.dma_start(zs[:, n, :], proj_d[T_ZS + n]).then_inc(zs_loaded[n], 16)
                    for n in range(KS):
                        i = n % 2
                        pool.wait_ge(g_z, NQ * (n + 1))
                        pool.dma_start(o_d[n], zs[:, i, :]).then_inc(os_kept[i], 16)
                        if n + 2 < KS:
                            pool.wait_ge(os_kept[i], 16 * (n // 2 + 1))
                            pool.dma_start(zs[:, i, :], proj_d[T_ZS + n + 2]).then_inc(zs_loaded[i], 16)
                    for i in range(2):
                        pool.wait_ge(os_kept[i], 16 * KS // 2)

                @block.scalar
                def _(act):
                    for c in range(NQ):
                        act.wait_ge(yr_loaded[c], 16)
                        cols = slice(CW * c, CW * (c + 1))
                        for ks in (slice(0, KS // 2), slice(KS // 2, KS)):
                            nc.scalar.activation(ys_hi[:, ks, cols], y_chunk(c)[:, ks, :], ACT.Copy).then_inc(
                                ys_hi_done, 1)
                    for n in range(KS):
                        for c in range(NQ):
                            u = NQ * n + c
                            act.wait_ge(g_mm, u + 1)
                            if u >= 2:
                                act.wait_ge(g_y, u - 1)
                            nc.scalar.activation(sg[:, u % 2, :], psum[4 * (n % 2) + c][:, :], ACT.Sigmoid,
                                                 bias=bglu[:, n:n + 1]).then_inc(g_sig, 1)

                @block.vector
                def _(dve):
                    for c in range(NQ):
                        cols = slice(CW * c, CW * (c + 1))
                        for half in range(2):
                            ks = slice(KS // 2 * half, KS // 2 * (half + 1))
                            dve.wait_ge(ys_hi_done, 2 * c + half + 1)
                            nc.vector.tensor_tensor(ys_lo[:, ks, cols], y_chunk(c)[:, ks, :],
                                                    ys_hi[:, ks, cols].bitcast(F32), ALU.subtract).then_inc(ys_split, 1)
                    for pair in range(3):
                        for n in (2 * pair, 2 * pair + 1):
                            dve.wait_ge(zs_loaded[n % 2], 16 * (n // 2 + 1))
                            for c in range(NQ):
                                u = NQ * n + c
                                dve.wait_ge(g_sig, u + 1)
                                y = y_chunk(c)[:, n, :]
                                nc.vector.tensor_tensor(y, sg[:, u % 2, :], y, ALU.mult).then_inc(g_y, 1)
                                dve.wait_ge(g_y, u + 1)
                                z = zs[:, n % 2, :].rearrange("p (c s) -> p s c", s=CH)[
                                    :, CW // NC * c:CW // NC * (c + 1), :]
                                nc.vector.tensor_tensor(z, y.rearrange("p (s c) -> p s c", c=NC), z,
                                                        ALU.mult).then_inc(g_z, 1)
                            if pair < 2:
                                split_pair(dve, N_GLU + pair + 1, lambda s: (g_mm, 8 * pair + 4 * s + 4), KS,
                                           (n % 2,))

                @block.tensor
                def _(pe):
                    for n in range(KS):
                        s = n % 2
                        pe.wait_ge(w_split[s], N_GLU + n // 2 + 1)
                        for c in range(NQ):
                            if n >= 2:
                                pe.wait_ge(g_sig, NQ * (n - 2) + c + 1)
                            cols = slice(CW * c, CW * (c + 1))
                            out = psum[4 * s + c][:, :]
                            parts = [(wt(s, k), (ys_hi[:, k, cols], ys_lo[:, k, cols])) for k in range(KS)]
                            if n == 0:
                                pe.wait_ge(ys_split, 2 * c + 1)
                            three_pass(out, parts[:KS // 2], stop=False)
                            if n == 0:
                                pe.wait_ge(ys_split, 2 * c + 2)
                            three_pass(out, parts[KS // 2:], start=False).then_inc(g_mm, 1)

        NBR, NOUT = D // P, D // (2 * P)
        N_MRG = N_GLU + 3
        o_loaded = [sem(f"o_loaded{i}") for i in range(4)]
        o_hi_done, o_split = sem("o_hi_done"), sem("o_split")
        gt_loaded = [sem(f"gt_loaded{i}") for i in range(2)]
        xq_loaded, y_kept = sem("xq_loaded"), sem("y_kept")
        b_half = sem("b_half")
        wx_loaded = [sem(f"wx_loaded{s}") for s in range(2)]
        b_mm, b_gated, b_sum, m_hi_done, m_split = (sem(a) for a in (
            "b_mm", "b_gated", "b_sum", "m_hi_done", "m_split"))
        p_mm, y_sum, y_sq, y_acc, f_mm, f_root, f_rstd, y_out_ready = (sem(a) for a in (
            "p_mm", "y_sum", "y_sq", "y_acc", "f_mm", "f_root", "f_rstd", "y_out_ready"))
        with ExitStack() as ph:
            KO = 16
            orw = space[:, 0:KO // 2 * CW].rearrange("p (k c) -> p k c", c=CW)
            wx_raw = space[:, KO // 2 * CW:].rearrange("p (s k c) -> p s k c", s=2, c=P)
            wx_hi = sb(ph, "wx_hi", [P, 2, KD, P], F32R)
            wx_lo = sb(ph, "wx_lo", [P, 2, KD, P], F32R)
            o_hi = sb(ph, "o_hi", [P, KO, CW], F32R)
            o_lo = sb(ph, "o_lo", [P, KO, CW], F32R)
            gt = sb(ph, "gt", [P, 2, 3, CW])
            m_hi = sb(ph, "m_hi", [P, KD, CW], F32R)
            m_lo = sb(ph, "m_lo", [P, KD, CW], F32R)
            xq = sb(ph, "xq", [P, KD, CW])
            tb = sb(ph, "tb", [P, CW])
            sqb = sb(ph, "sqb", [P, CW])
            acc = sb(ph, "acc", [P, CW])
            rs = sb(ph, "rs", [P, CW])
            BR = ((0, 6), (6, 12), (12, 16))

            def o_piece(q, piece):
                raw = xq if q == 0 and piece >= 2 else orw
                return raw[:, 4 * (piece % 2):4 * (piece % 2) + 4, :]

            def wq(i, s, k):
                hi, lo = (w_hi, w_lo) if i % 2 == 0 else (wx_hi, wx_lo)
                return hi[:, s, k, :], lo[:, s, k, :]

            def chunk_cols(q):
                return slice(CW * q, CW * (q + 1))

            with nc.Block() as block:
                @block.sync
                def _(sp):
                    def load_o(q, half):
                        for piece in (2 * half, 2 * half + 1):
                            if q:
                                sp.wait_ge(o_split, 4 * q + piece - 1)
                            src = o_d[4 * piece:4 * piece + 4, :, chunk_cols(q)]
                            sp.dma_start(o_piece(q, piece), src.rearrange("k p c -> p k c")).then_inc(
                                o_loaded[piece], 16)

                    def load_next(i, src0, src1):
                        raw, loaded = ((w_raw, w_loaded), (wx_raw, wx_loaded))[i % 2]
                        for s, src in enumerate((src0, src1)):
                            if i != 1:
                                sp.wait_ge(w_split[s], N_MRG + max(i - 1, 0))
                            sp.dma_start(raw[:, s, :, :], src).then_inc(loaded[s], 16)

                    for q in range(NQ):
                        if q == 0:
                            load_o(0, 0)
                        for i in range(NBR):
                            if q or i:
                                load_next(12 * q + i, w_br[i, 0], w_br[i, 1])
                            if i == 0:
                                load_o(q, 1)
                            if i == 5:
                                if q:
                                    sp.wait_ge(y_kept, 16 * q)
                                else:
                                    sp.wait_ge(o_split, 4)
                                sp.dma_start(xq[:, :, :], x_t[:, :, chunk_cols(q)]).then_inc(xq_loaded, 16)
                            if i == 4 and q + 1 < NQ:
                                load_o(q + 1, 0)
                        for i in range(NOUT):
                            load_next(12 * q + NBR + i, w_out[2 * i], w_out[2 * i + 1])

                @block.gpsimd
                def _(pool):
                    for q in range(NQ):
                        for n in range(NBR):
                            u = NBR * q + n
                            if u >= 2:
                                pool.wait_ge(b_sum, u - 1)
                            src = proj_d[T_G:NT].rearrange("(b n) p c -> n p b c", b=3)
                            pool.dma_start(gt[:, u % 2, :, :], src[n][:, :, chunk_cols(q)]).then_inc(
                                gt_loaded[u % 2], 16)
                            if n == 2 and q:
                                pool.wait_ge(y_out_ready, KD * q)
                                pool.dma_start(y_out[:, :, chunk_cols(q - 1)], xq[:, :, :]).then_inc(y_kept, 16)
                    for n in range(0, KD, 2):
                        pool.wait_ge(y_out_ready, KD * (NQ - 1) + n + 2)
                        pool.dma_start(y_out[:, n:n + 2, chunk_cols(NQ - 1)], xq[:, n:n + 2, :]).then_inc(y_kept, 16)
                    pool.wait_ge(y_kept, 16 * (NQ - 1 + KD // 2))

                @block.tensor
                def _(pe):
                    def total(q):
                        pe.wait_ge(y_acc, KD * (q + 1))
                        nc.tensor.matmul(psum[7][:, :], ones[:, :], acc[:, :], start=True, stop=True).then_inc(f_mm, 1)

                    for q in range(NQ):
                        for n in range(NBR):
                            u = NBR * q + n
                            for s in range(2):
                                pe.wait_ge(w_split[s], N_MRG + 12 * q + n + 1)
                            if n == 0 and q:
                                pe.wait_ge(o_split, 4 * (q + 1))
                            for b, (k0, k1) in enumerate(BR):
                                if u >= 2:
                                    pe.wait_ge(b_gated, 3 * (u - 2) + b + 1)
                                parts = [(wq(n, k // 8, k % 8), (o_hi[:, k, :], o_lo[:, k, :])) for k in range(k0, k1)]
                                out = psum[3 * (n % 2) + b][:, :]
                                first = n == 0 and q == 0 and b == 0
                                if first:
                                    pe.wait_ge(o_split, 1)
                                    three_pass(out, parts[:4], stop=False)
                                    parts = parts[4:]
                                if n == 0 and q == 0:
                                    pe.wait_ge(o_split, -(-k1 // 4))
                                three_pass(out, parts, start=not first).then_inc(b_mm, 1)
                            if n == 0 and q:
                                total(q - 1)
                        def output(n, ks):
                            return three_pass(psum[6 + n % 2][:, :], [
                                (wq(NBR + n // 2, n % 2, k), (m_hi[:, k, :], m_lo[:, k, :])) for k in ks],
                                start=(0 in ks), stop=(KD - 1 in ks))

                        pe.wait_ge(m_split, KD * (q + 1) - 1)
                        if q:
                            pe.wait_ge(y_sum, KD * q)
                            pe.wait_ge(f_root, q)
                        for n in range(2):
                            pe.wait_ge(w_split[n], N_MRG + 12 * q + NBR + 1)
                            output(n, range(KD - 1))
                        pe.wait_ge(m_split, KD * (q + 1))
                        for n in range(2):
                            output(n, [KD - 1]).then_inc(p_mm, 1)
                        for n in range(2, KD):
                            pe.wait_ge(w_split[n % 2], N_MRG + 12 * q + NBR + n // 2 + 1)
                            pe.wait_ge(y_sum, KD * q + n - 1)
                            output(n, range(KD)).then_inc(p_mm, 1)
                    total(NQ - 1)

                @block.scalar
                def _(act):
                    def split_hi(q, piece):
                        act.wait_ge(o_loaded[piece], 16 * (q + 1))
                        if q:
                            act.wait_ge(b_mm, 3 * NBR * q)
                        ks = slice(4 * piece, 4 * piece + 4)
                        nc.scalar.activation(o_hi[:, ks, :], o_piece(q, piece), ACT.Copy).then_inc(o_hi_done, 1)

                    def root(q):
                        act.wait_ge(f_mm, q + 1)
                        nc.scalar.activation(rs[:, :], psum[7][:, :], ACT.Sqrt, bias=eps[:, 0:1],
                                             scale=1.0 / D).then_inc(f_root, 1)

                    for piece in range(4):
                        split_hi(0, piece)
                    for q in range(NQ):
                        for n in range(NBR):
                            u = NBR * q + n
                            act.wait_ge(b_sum, u + 1)
                            if n == 0 and q:
                                act.wait_ge(p_mm, KD * q)
                            nc.scalar.activation(m_hi[:, n, :], tb[:, :], ACT.Copy).then_inc(m_hi_done, 1)
                            if n == 0 and q:
                                root(q - 1)
                        if q + 1 < NQ:
                            split_hi(q + 1, 0)
                        for n in range(KD):
                            u = KD * q + n
                            act.wait_ge(y_sum, u + 1)
                            if u >= 1:
                                act.wait_ge(y_acc, u)
                            nc.scalar.activation(sqb[:, :], xq[:, n, :], ACT.Square).then_inc(y_sq, 1)
                            if n % 2 and n < KD - 1 and q + 1 < NQ:
                                split_hi(q + 1, n // 2 + 1)
                    root(NQ - 1)

                @block.vector
                def _(dve):
                    def split_lo(q, piece):
                        dve.wait_ge(o_hi_done, 4 * q + piece + 1)
                        ks = slice(4 * piece, 4 * piece + 4)
                        nc.vector.tensor_tensor(o_lo[:, ks, :], o_piece(q, piece), o_hi[:, ks, :].bitcast(F32),
                                                ALU.subtract).then_inc(o_split, 1)

                    def normalise(q, half):
                        if half == 0:
                            dve.wait_ge(f_root, q + 1)
                            nc.vector.reciprocal(rs[:, :], rs[:, :]).then_inc(f_rstd, 1)
                            dve.wait_ge(f_rstd, q + 1)
                        for n in range(KD // 2 * half, KD // 2 * (half + 1)):
                            nc.vector.scalar_tensor_tensor(xq[:, n, :], xq[:, n, :], g_in[:, 2, n:n + 1], rs[:, :],
                                                           ALU.mult, ALU.mult).then_inc(y_out_ready, 1)

                    def split_next(i):
                        if i >= 12 * NQ:
                            return
                        q, n = divmod(i - 2, 12)
                        if i < 2:
                            used = (lambda s: (g_mm, 4 * KS)) if i == 0 else None
                        elif n < NBR:
                            used = lambda s: (b_mm, 3 * (NBR * q + n) + 2 + s)
                        else:
                            used = lambda s: (p_mm, KD * q + 2 * (n - NBR) + 1 + s)
                        if i % 2 == 0:
                            split_pair(dve, N_MRG + i, used, loads=N_MRG + i // 2 + 1)
                        else:
                            split_pair(dve, N_MRG + i, used, into=(wx_hi, wx_lo), raw=wx_raw, loaded=wx_loaded,
                                       loads=i // 2 + 1)

                    split_next(0)
                    for piece in range(4):
                        split_lo(0, piece)
                    split_next(1)
                    for q in range(NQ):
                        for n in range(NBR):
                            u = NBR * q + n
                            dve.wait_ge(gt_loaded[u % 2], 16 * (u // 2 + 1))
                            gates = gt[:, u % 2, :, :]
                            for b in range(3):
                                dve.wait_ge(b_mm, 3 * u + b + 1)
                                nc.vector.tensor_tensor(gates[:, b, :], psum[3 * (n % 2) + b][:, :], gates[:, b, :],
                                                        ALU.mult).then_inc(b_gated, 1)
                            split_next(12 * q + n + 2)
                            dve.wait_ge(b_gated, 3 * (u + 1))
                            nc.vector.tensor_tensor(gates[:, 0, :], gates[:, 0, :], gates[:, 1, :],
                                                    ALU.add).then_inc(b_half, 1)
                            dve.wait_ge(b_half, u + 1)
                            if u:
                                dve.wait_ge(m_split, u)
                            nc.vector.tensor_tensor(tb[:, :], gates[:, 0, :], gates[:, 2, :],
                                                    ALU.add).then_inc(b_sum, 1)
                            dve.wait_ge(m_hi_done, u + 1)
                            nc.vector.tensor_tensor(m_lo[:, n, :], tb[:, :], m_hi[:, n, :].bitcast(F32),
                                                    ALU.subtract).then_inc(m_split, 1)
                            if n < 2 and q:
                                normalise(q - 1, n)
                        dve.wait_ge(xq_loaded, 16 * (q + 1))
                        for n in range(KD):
                            u = KD * q + n
                            dve.wait_ge(p_mm, u + 1)
                            nc.vector.tensor_tensor(xq[:, n, :], psum[6 + n % 2][:, :], xq[:, n, :],
                                                    ALU.add).then_inc(y_sum, 1)
                            if n % 2:
                                split_next(12 * q + NBR + n // 2 + 2)
                            dve.wait_ge(y_sq, u + 1)
                            if n == 0:
                                if q:
                                    dve.wait_ge(f_mm, q)
                                nc.vector.tensor_copy(acc[:, :], sqb[:, :]).then_inc(y_acc, 1)
                            else:
                                dve.wait_ge(y_acc, u)
                                nc.vector.tensor_tensor(acc[:, :], acc[:, :], sqb[:, :], ALU.add).then_inc(y_acc, 1)
                            if n % 2 == 0 and q + 1 < NQ:
                                split_lo(q + 1, n // 2)
                    for half in range(2):
                        normalise(NQ - 1, half)


def _dram_inputs(nc, arrays):
    return {n: nc.dram_tensor(n, a.shape, mybir.dt.from_np(a.dtype), kind="ExternalInput").ap()
            for n, a in arrays.items()}


def rel_buckets():
    out = np.zeros((NBUCKET + 1, 3, 384), np.float32)
    for g, r in enumerate(DIL):
        for x in range(384):
            delta = 255 - x
            if not 0 <= delta <= P:
                out[NBUCKET, g, x] = -BIG
                continue
            n = delta * r
            if n < NBUCKET // 2:
                b = n
            else:
                b = NBUCKET // 2 + int(np.float32(
                    np.log(np.float32(n) / np.float32(NBUCKET // 2)) / np.float32(math.log(MAXD / (NBUCKET // 2)))
                    * np.float32(NBUCKET - NBUCKET // 2)))
                b = min(b, NBUCKET - 1)
            out[b, g, x] = 1.0
    return out


def layouts(i):
    def f(a):
        return np.ascontiguousarray(a, np.float32)

    def tiles(w):
        k, n = w.shape
        return f(w.reshape(k // P, P, n // P, P).transpose(2, 1, 0, 3))

    def by_channel(v):
        return f(v.reshape(-1, P).T)

    def transposed(x):
        return f(x.T.reshape(-1, P, x.shape[0]).transpose(1, 0, 2))

    def stack(re, im):
        return np.concatenate([re, im], 1)

    i = {k: np.asarray(v) for k, v in i.items()}
    lam = [i[n][0].T for n in ("ssm_lambda_re", "ssm_lambda_im")]
    dt = np.broadcast_to(i["ssm_log_dt"][0], (NS, G))
    b = [i[n][0].transpose(1, 0, 2) for n in ("ssm_b_re", "ssm_b_im")]
    c = [i[n][0].transpose(2, 0, 1) for n in ("ssm_c_re", "ssm_c_im")]

    def unit(parts, u):
        gs = slice(UG * u, UG * (u + 1))
        return np.concatenate([np.concatenate([p[:, gs].reshape(NS, -1) for p in half], 1) for half in parts], 0)

    halves = ([lam[0], lam[1], dt, c[0], c[1], b[0], b[1]], [lam[0], lam[1], dt, c[1], c[0], b[1], b[0]])
    ssm_par = np.stack([unit(halves, u) for u in range(NU)])
    d = i["ssm_d"][0].reshape(NU, 1, UG, HG)
    br = np.concatenate([i["w_br_ssm"][0], i["w_br_attn"][0], i["w_br_mem"][0]], 0)
    w_br = tiles(br).reshape(D // P, P, 2, 8, P).transpose(0, 2, 1, 3, 4)
    return {
        "x_t": transposed(i["x"][0]), "mem_t": transposed(i["mem"][0]),
        "norm_g": by_channel(i["norm_g"][0]), "mem_norm_g": by_channel(i["mem_norm_g"][0]),
        "final_g": by_channel(i["final_norm_g"]),
        "w_in": tiles(i["w_in"][0]), "w_kv": tiles(i["w_mem_kv"][0]), "b_gate": by_channel(i["b_gate"][0]),
        "ssm_par": f(ssm_par), "ssm_d": f(np.broadcast_to(d, (NU, HG, UG, HG))),
        "w_glu": tiles(i["w_glu"][0]), "b_glu": by_channel(i["b_glu"][0]),
        "w_br": f(w_br), "w_out": tiles(i["w_out"][0]), "rel_bias": f(i["rel_bias"]),
        "buckets": rel_buckets(), "ident_c": np.eye(P, dtype=np.float32),
        "anti_c": np.eye(P, dtype=np.float32)[::-1].copy(),
        "sign_c": np.repeat(np.array([1.0, -1.0], np.float32), NS)[:, None].copy(),
        "steps_c": np.tile(np.arange(1, NC + 1, dtype=np.float32), (P, 1)),
        "powers_c": np.tile(np.r_[np.arange(CH + 1), np.arange(CH)[::-1]].astype(np.float32), (P, 1)),
    }


def kernel(**inputs):
    import concourse.bacc as _bacc
    from concourse.bass_utils import run_bass_kernel_spmd as _run

    nc = _bacc.Bacc("TRN2", target_bir_lowering=False, num_devices=1)
    arrays = layouts(inputs)
    aps = _dram_inputs(nc, arrays)
    y_out = nc.dram_tensor("y_out", (P, KD, L), F32, kind="ExternalOutput").ap()
    build_program(nc, y_out=y_out, **aps)
    r = _run(nc, [arrays], core_ids=[0])
    y = r.results[0]["y_out"]
    return np.ascontiguousarray(y.transpose(2, 1, 0).reshape(1, L, D))
```
